# Optimizing a Trainium2 kernel written in Bass

```python
import math
import jax, jax.numpy as jnp
from jax import lax
import numpy as np

D_MODEL = 1024
BATCH = 1
SEQ = 512
DEPTH = 2
DEC_BATCH = 8
DEC_SEQ = 8
PAST_LEN = 4096
PAGE_SIZE = 128

D_FF = 2752
DN_ALPHA = (2 * DEPTH) ** 0.25
DN_BETA = (8 * DEPTH) ** -0.25
LN_EPS = 1e-5
POOL_WIDTH = D_MODEL // 2
POOL_GROUPS = 4
POOL_GW = POOL_WIDTH // POOL_GROUPS
POOL_WINDOWS = (2, 4, 8, 16)
POOL_STATE = max(POOL_WINDOWS) - 1
GMLP_WIDTH = D_MODEL // 2
GMLP_HEADS = 4
GMLP_HD = GMLP_WIDTH // GMLP_HEADS
GMLP_CHUNK = 128
NSA_HEADS = 16
NSA_KV = 4
NSA_HPG = NSA_HEADS // NSA_KV
NSA_HD = 64
CMP_LEN = 32
CMP_STRIDE = 16
CMP_HIDDEN = 128
SEL_BLOCK = 64
N_SEL = 16
WINDOW = 512
SEL_QBLK = 16
WIN_QBLK = 128

kernel_name = "pool_gmlp_nsa_macaron_deepnorm_step"

def layer_norm(x, g, b):
    xf = x.astype(jnp.float32)
    mu = jnp.mean(xf, -1, keepdims=True)
    var = jnp.mean(jnp.square(xf - mu), -1, keepdims=True)
    return ((xf - mu) * lax.rsqrt(var + LN_EPS) * g + b).astype(x.dtype)

def swiglu(x, w_in, w_out):
    gate, up = jnp.split(x @ w_in, 2, axis=-1)
    return (jax.nn.silu(gate) * up) @ w_out

def alibi_slopes(n_heads):
    return 2.0 ** (-8.0 * (jnp.arange(n_heads, dtype=jnp.float32) + 1.0) / n_heads)

def masked_softmax(s, mask):
    s = jnp.where(mask, s.astype(jnp.float32), -1e30)
    m = jnp.max(s, -1, keepdims=True)
    e = jnp.where(mask, jnp.exp(s - m), 0.0)
    return e / jnp.maximum(jnp.sum(e, -1, keepdims=True), 1e-30)

def pool_gmlp_mixer(h, pos0, pool_past, w_in, pool_w, pool_scale, gm_ln_g, gm_ln_b, gm_ws, gm_b, w_out):
    B, T, _ = h.shape
    z = h @ w_in
    p = z[..., :POOL_WIDTH]
    u = z[..., POOL_WIDTH:POOL_WIDTH + GMLP_WIDTH]
    v = layer_norm(z[..., POOL_WIDTH + GMLP_WIDTH:], gm_ln_g, gm_ln_b)
    ext = jnp.concatenate([pool_past.astype(p.dtype), p], axis=1)
    ext32 = ext.astype(jnp.float32)
    csum = jnp.pad(jnp.cumsum(ext32, axis=1), ((0, 0), (1, 0), (0, 0)))
    hi = csum[:, POOL_STATE + 1:]
    tpos = pos0 + jnp.arange(T)
    means = []
    for g, w in enumerate(POOL_WINDOWS):
        ch = slice(g * POOL_GW, (g + 1) * POOL_GW)
        lo = csum[:, POOL_STATE + 1 - w:POOL_STATE + 1 - w + T, ch]
        cnt = jnp.minimum(w, tpos + 1).astype(jnp.float32)[None, :, None]
        means.append((hi[..., ch] - lo) / cnt)
    d = (jnp.concatenate(means, -1) - ext32[:, POOL_STATE:]).astype(h.dtype)
    a = jnp.einsum('btgc,gcd->btgd', d.reshape(B, T, POOL_GROUPS, POOL_GW), pool_w).reshape(B, T, POOL_WIDTH) * pool_scale
    C = min(T, GMLP_CHUNK)
    nc = T // C
    causal = jnp.tril(jnp.ones((C, C), dtype=bool))
    ws = jnp.where(causal, gm_ws[:, :C, :C], 0)
    mix = jnp.einsum('hts,bcshd->bcthd', ws, v.reshape(B, nc, C, GMLP_HEADS, GMLP_HD)) + gm_b[:, :C].T[None, None, :, :, None]
    gb = u * mix.reshape(B, T, GMLP_WIDTH)
    y = jnp.concatenate([a, gb], axis=-1) @ w_out
    return y, ext[:, -POOL_STATE:], v

def compress_blocks(x, pe, w1, b1, w2):
    B, L = x.shape[:2]
    rc = CMP_LEN // CMP_STRIDE
    nch = -(-L // CMP_STRIDE)
    xc = jnp.pad(x, ((0, 0), (0, nch * CMP_STRIDE - L), (0, 0), (0, 0))).reshape(B, nch, CMP_STRIDE, NSA_KV, NSA_HD)
    pe = pe.reshape(rc, CMP_STRIDE, NSA_HD)
    w1 = w1.reshape(rc, CMP_STRIDE, NSA_HD, CMP_HIDDEN)
    nb = nch - rc + 1
    hid = b1
    for r in range(rc):
        hid = hid + jnp.einsum('bcpgd,pdf->bcgf', xc[:, r:r + nb] + pe[r][:, None, :], w1[r])
    return jax.nn.gelu(hid) @ w2

def selection_importance(pc, nsb):
    rs = SEL_BLOCK // CMP_STRIDE
    rc = CMP_LEN // CMP_STRIDE
    nb = pc.shape[-1]
    pp = jnp.pad(pc, [(0, 0)] * (pc.ndim - 1) + [(rc - 1, rs * nsb - nb)])
    imp = None
    for n in range(rc):
        seg = pp[..., rc - 1 - n:rc - 1 - n + rs * nsb]
        part = seg.reshape(seg.shape[:-1] + (nsb, rs)).sum(-1)
        imp = part if imp is None else imp + part
    return imp

def nsa_mixer(h, pos0, cmp_past, slc_past, win_past, w_in, cmp_pe, cmp_w1, cmp_b1, cmp_w2, w_out):
    B, T, _ = h.shape
    qw = NSA_HEADS * NSA_HD
    kvw = 3 * 2 * NSA_KV * NSA_HD
    z = h @ w_in
    q = z[..., :qw].reshape(B, T, NSA_KV, NSA_HPG, NSA_HD)
    kv = z[..., qw:qw + kvw].reshape(B, T, 3, 2, NSA_KV, NSA_HD)
    gates = jax.nn.sigmoid(z[..., qw + kvw:].astype(jnp.float32)).reshape(B, T, 3, NSA_KV, NSA_HPG)
    kv_cmp, kv_slc, kv_win = kv[:, :, 0], kv[:, :, 1], kv[:, :, 2]
    tpos = pos0 + jnp.arange(T)
    slopes = alibi_slopes(NSA_HEADS).reshape(NSA_KV, NSA_HPG)
    scale = NSA_HD ** -0.5

    full_cmp = kv_cmp if cmp_past is None else jnp.concatenate([cmp_past, kv_cmp], axis=1)
    L = full_cmp.shape[1]
    kc = compress_blocks(full_cmp[:, :, 0], cmp_pe[0], cmp_w1[0], cmp_b1[0], cmp_w2[0])
    vc = compress_blocks(full_cmp[:, :, 1], cmp_pe[1], cmp_w1[1], cmp_b1[1], cmp_w2[1])
    nb = kc.shape[1]
    cend = jnp.arange(nb) * CMP_STRIDE + CMP_LEN - 1
    dist_c = tpos[:, None] - cend[None, :]
    s_c = jnp.einsum('btghd,bngd->bghtn', q, kc).astype(jnp.float32) * scale - slopes[:, :, None, None] * dist_c
    p_cmp = masked_softmax(s_c, dist_c >= 0)
    o_cmp = jnp.einsum('bghtn,bngd->btghd', p_cmp.astype(vc.dtype), vc)

    full_slc = kv_slc if slc_past is None else jnp.concatenate([slc_past, kv_slc], axis=1)
    nsb = -(-L // SEL_BLOCK)
    imp = selection_importance(jnp.sum(p_cmp, axis=2), nsb)
    jblk = jnp.arange(nsb)[None, :]
    jt = (tpos // SEL_BLOCK)[:, None]
    forced = (jblk == 0) | (jblk == jt) | (jblk == jt - 1)
    score = jnp.where(forced, jnp.inf, jnp.where(jblk <= jt, imp, -jnp.inf))
    n_sel = min(N_SEL, nsb)
    _, idx = lax.top_k(score, n_sel)
    idx = idx.transpose(0, 2, 1, 3)
    kvb = jnp.pad(full_slc, ((0, 0), (0, nsb * SEL_BLOCK - L), (0, 0), (0, 0), (0, 0)))
    kvb = kvb.reshape(B, nsb, SEL_BLOCK, 2, NSA_KV, NSA_HD).transpose(0, 4, 1, 2, 3, 5)
    bi = jnp.arange(B)[:, None, None, None]
    gi = jnp.arange(NSA_KV)[None, None, :, None]
    qb = SEL_QBLK if T % SEL_QBLK == 0 else T
    nq = T // qb

    def sel_block(args):
        q_b, i_b, t_b = args
        g = kvb[bi, gi, i_b].reshape(B, qb, NSA_KV, n_sel * SEL_BLOCK, 2, NSA_HD)
        kpos = (i_b[..., None] * SEL_BLOCK + jnp.arange(SEL_BLOCK)).reshape(B, qb, NSA_KV, n_sel * SEL_BLOCK)
        dd = t_b[None, :, None, None] - kpos
        s = jnp.einsum('bqghd,bqgkd->bqghk', q_b, g[..., 0, :]).astype(jnp.float32) * scale - slopes[None, None, :, :, None] * dd[:, :, :, None, :]
        pr = masked_softmax(s, (dd >= 0)[:, :, :, None, :])
        return jnp.einsum('bqghk,bqgkd->bqghd', pr.astype(g.dtype), g[..., 1, :])

    def to_blocks(a, blk, n):
        return a.reshape((B, n, blk) + a.shape[2:]).swapaxes(0, 1)

    o_slc = lax.map(sel_block, (to_blocks(q, qb, nq), to_blocks(idx, qb, nq), tpos.reshape(nq, qb)))
    o_slc = o_slc.swapaxes(0, 1).reshape(B, T, NSA_KV, NSA_HPG, NSA_HD)

    if win_past is None:
        ext = jnp.pad(kv_win, ((0, 0), (WINDOW, 0), (0, 0), (0, 0), (0, 0)))
        new_win = kv_win[:, -min(WINDOW, T):]
    else:
        wb = win_past.shape[1]
        buf = jnp.concatenate([win_past, kv_win], axis=1)
        new_win = buf[:, -wb:]
        ext = jnp.pad(buf, ((0, 0), (WINDOW - wb, 0), (0, 0), (0, 0), (0, 0)))
    wq = WIN_QBLK if T % WIN_QBLK == 0 else T
    nw = T // wq

    def win_block(args):
        q_b, c = args
        kvs = lax.dynamic_slice_in_dim(ext, c * wq, WINDOW + wq, axis=1)
        kpos = pos0 - WINDOW + c * wq + jnp.arange(WINDOW + wq)
        tq = pos0 + c * wq + jnp.arange(wq)
        dd = tq[:, None] - kpos[None, :]
        mask = (dd >= 0) & (dd < WINDOW) & (kpos[None, :] >= 0)
        s = jnp.einsum('bqghd,bkgd->bghqk', q_b, kvs[:, :, 0]).astype(jnp.float32) * scale - slopes[:, :, None, None] * dd
        pr = masked_softmax(s, mask)
        return jnp.einsum('bghqk,bkgd->bqghd', pr.astype(kvs.dtype), kvs[:, :, 1])

    o_win = lax.map(win_block, (to_blocks(q, wq, nw), jnp.arange(nw)))
    o_win = o_win.swapaxes(0, 1).reshape(B, T, NSA_KV, NSA_HPG, NSA_HD)

    o = (gates[:, :, 0, :, :, None] * o_cmp + gates[:, :, 1, :, :, None] * o_slc + gates[:, :, 2, :, :, None] * o_win)
    y = o.reshape(B, T, NSA_HEADS * NSA_HD).astype(h.dtype) @ w_out
    return y, kv_cmp, kv_slc, new_win

def trunk(x, pos0, pool_past, cmp_past, slc_past, win_past, w_ffn_in, w_ffn_out, ln_g, ln_b,
          w_in_even, pool_w, pool_scale, gm_ln_g, gm_ln_b, gm_ws, gm_b, w_out_even,
          w_in_odd, cmp_pe, cmp_w1, cmp_b1, cmp_w2, w_out_odd):
    for layer in range(DEPTH):
        x = layer_norm(DN_ALPHA * x + 0.5 * swiglu(x, w_ffn_in[layer, 0], w_ffn_out[layer, 0]), ln_g[layer, 0], ln_b[layer, 0])
        if layer % 2 == 0:
            y, pool_state, gm_v = pool_gmlp_mixer(x, pos0, pool_past, w_in_even, pool_w, pool_scale,
                                                  gm_ln_g, gm_ln_b, gm_ws, gm_b, w_out_even)
        else:
            y, cmp_rows, slc_rows, win_buf = nsa_mixer(x, pos0, cmp_past, slc_past, win_past, w_in_odd,
                                                       cmp_pe, cmp_w1, cmp_b1, cmp_w2, w_out_odd)
        x = layer_norm(DN_ALPHA * x + y, ln_g[layer, 1], ln_b[layer, 1])
        x = layer_norm(DN_ALPHA * x + 0.5 * swiglu(x, w_ffn_in[layer, 1], w_ffn_out[layer, 1]), ln_g[layer, 2], ln_b[layer, 2])
    return x, pool_state, gm_v, cmp_rows, slc_rows, win_buf

def setup_inputs(seed: int = 0) -> dict:
    key = jax.random.key(seed)
    ks = jax.random.split(key, 24)
    n_pages = PAST_LEN // PAGE_SIZE
    n_used = DEC_BATCH * n_pages
    n_phys = n_used + n_used // 4
    wb = min(WINDOW, PAST_LEN)

    def nrm(k, shape, s):
        return jax.random.normal(k, shape, jnp.float32) * s

    kv_scale = jnp.array([1.0, DN_BETA], jnp.float32)
    x_prompt = nrm(ks[0], (BATCH, SEQ, D_MODEL), 1.0)
    x_sample = nrm(ks[1], (DEC_BATCH, DEC_SEQ, D_MODEL), 1.0)
    state_l0_pool = nrm(ks[2], (DEC_BATCH, POOL_STATE, POOL_WIDTH), 1.0)
    cache_l1_cmp_kv = nrm(ks[3], (n_phys, PAGE_SIZE, 2, NSA_KV, NSA_HD), 1.0) * kv_scale[:, None, None]
    cache_l1_slc_kv = nrm(ks[4], (n_phys, PAGE_SIZE, 2, NSA_KV, NSA_HD), 1.0) * kv_scale[:, None, None]
    cache_l1_win_kv = nrm(ks[5], (DEC_BATCH, wb, 2, NSA_KV, NSA_HD), 1.0) * kv_scale[:, None, None]
    page_table = jax.random.permutation(ks[6], n_phys)[:n_used].reshape(DEC_BATCH, n_pages).astype(jnp.int32)
    w_ffn_in = nrm(ks[7], (DEPTH, 2, D_MODEL, 2 * D_FF), D_MODEL ** -0.5)
    w_ffn_out = nrm(ks[8], (DEPTH, 2, D_FF, D_MODEL), D_FF ** -0.5 * DN_BETA)
    ln_g = 1.0 + nrm(ks[9], (DEPTH, 3, D_MODEL), 0.02)
    ln_b = nrm(ks[10], (DEPTH, 3, D_MODEL), 0.02)
    w_in_even = nrm(ks[11], (D_MODEL, POOL_WIDTH + 2 * GMLP_WIDTH), D_MODEL ** -0.5)
    pool_w = nrm(ks[12], (POOL_GROUPS, POOL_GW, POOL_GW), POOL_GW ** -0.5)
    pool_scale = 1.0 + nrm(ks[13], (POOL_WIDTH,), 0.1)
    gm_ln_g = 1.0 + nrm(ks[14], (GMLP_WIDTH,), 0.02)
    gm_ln_b = nrm(ks[15], (GMLP_WIDTH,), 0.02)
    gm_ws = nrm(ks[16], (GMLP_HEADS, GMLP_CHUNK, GMLP_CHUNK), GMLP_CHUNK ** -0.5)
    gm_b = 1.0 + nrm(ks[17], (GMLP_HEADS, GMLP_CHUNK), 0.1)
    w_out_even = nrm(ks[18], (POOL_WIDTH + GMLP_WIDTH, D_MODEL), (POOL_WIDTH + GMLP_WIDTH) ** -0.5 * DN_BETA)
    kq, kkv, kg = jax.random.split(ks[19], 3)
    wq = nrm(kq, (D_MODEL, NSA_HEADS * NSA_HD), D_MODEL ** -0.5)
    wkv = nrm(kkv, (D_MODEL, 3, 2, NSA_KV * NSA_HD), D_MODEL ** -0.5) * kv_scale[:, None]
    wg = nrm(kg, (D_MODEL, 3 * NSA_HEADS), D_MODEL ** -0.5)
    w_in_odd = jnp.concatenate([wq, wkv.reshape(D_MODEL, -1), wg], axis=1)
    cmp_pe = nrm(ks[20], (2, CMP_LEN, NSA_HD), 0.1)
    k1, k2 = jax.random.split(ks[21])
    cmp_w1 = nrm(k1, (2, CMP_LEN * NSA_HD, CMP_HIDDEN), (CMP_LEN * NSA_HD) ** -0.5)
    cmp_b1 = nrm(k2, (2, CMP_HIDDEN), 0.02)
    cmp_w2 = nrm(ks[22], (2, CMP_HIDDEN, NSA_HD), CMP_HIDDEN ** -0.5)
    w_out_odd = nrm(ks[23], (NSA_HEADS * NSA_HD, D_MODEL), (NSA_HEADS * NSA_HD) ** -0.5 * DN_BETA)
    return {"x_prompt": x_prompt, "x_sample": x_sample, "state_l0_pool": state_l0_pool,
            "cache_l1_cmp_kv": cache_l1_cmp_kv, "cache_l1_slc_kv": cache_l1_slc_kv,
            "cache_l1_win_kv": cache_l1_win_kv, "page_table": page_table,
            "w_ffn_in": w_ffn_in, "w_ffn_out": w_ffn_out, "ln_g": ln_g, "ln_b": ln_b,
            "w_in_even": w_in_even, "pool_w": pool_w, "pool_scale": pool_scale,
            "gm_ln_g": gm_ln_g, "gm_ln_b": gm_ln_b, "gm_ws": gm_ws, "gm_b": gm_b, "w_out_even": w_out_even,
            "w_in_odd": w_in_odd, "cmp_pe": cmp_pe, "cmp_w1": cmp_w1, "cmp_b1": cmp_b1, "cmp_w2": cmp_w2,
            "w_out_odd": w_out_odd}

def reference(x_prompt, x_sample, state_l0_pool, cache_l1_cmp_kv, cache_l1_slc_kv, cache_l1_win_kv, page_table,
              w_ffn_in, w_ffn_out, ln_g, ln_b, w_in_even, pool_w, pool_scale, gm_ln_g, gm_ln_b, gm_ws, gm_b,
              w_out_even, w_in_odd, cmp_pe, cmp_w1, cmp_b1, cmp_w2, w_out_odd):
    pool0 = jnp.zeros((x_prompt.shape[0], POOL_STATE, POOL_WIDTH), x_prompt.dtype)
    y_prompt, pool_p, _, cmp_p, slc_p, win_p = trunk(
        x_prompt, 0, pool0, None, None, None, w_ffn_in, w_ffn_out, ln_g, ln_b,
        w_in_even, pool_w, pool_scale, gm_ln_g, gm_ln_b, gm_ws, gm_b, w_out_even,
        w_in_odd, cmp_pe, cmp_w1, cmp_b1, cmp_w2, w_out_odd)
    db, n_pages = page_table.shape
    cmp_past = cache_l1_cmp_kv[page_table].reshape((db, n_pages * PAGE_SIZE) + cache_l1_cmp_kv.shape[2:])
    slc_past = cache_l1_slc_kv[page_table].reshape((db, n_pages * PAGE_SIZE) + cache_l1_slc_kv.shape[2:])
    y_sample, pool_s, gmv_s, cmp_s, slc_s, win_s = trunk(
        x_sample, n_pages * PAGE_SIZE, state_l0_pool, cmp_past, slc_past, cache_l1_win_kv,
        w_ffn_in, w_ffn_out, ln_g, ln_b,
        w_in_even, pool_w, pool_scale, gm_ln_g, gm_ln_b, gm_ws, gm_b, w_out_even,
        w_in_odd, cmp_pe, cmp_w1, cmp_b1, cmp_w2, w_out_odd)
    return (y_prompt, y_sample, pool_p, pool_s, gmv_s, cmp_p, slc_p, win_p, cmp_s, slc_s, win_s)


_drawn_inputs = setup_inputs


def setup_inputs(seed=0):
    import zlib

    import numpy as np

    out = dict(_drawn_inputs(seed))
    spreads = {}
    factors = {'pool_scale': 2.733,
     'gm_ln_g': 28.047,
     'gm_ln_b': 26.285,
     'cmp_pe': 6.198,
     'cmp_b1': 25.94,
     'gm_b': 3.058,
     'cache_l1_slc_kv': 2.679}
    for name, (base, spread) in spreads.items():
        noise = np.random.default_rng([zlib.crc32(name.encode()), seed]).standard_normal(out[name].shape)
        drawn = base * np.exp(spread * noise) if base else spread * noise
        out[name] = __import__('jax').numpy.asarray(drawn.astype(out[name].dtype))
    for name, factor in factors.items():
        out[name] = (out[name] * factor).astype(out[name].dtype)
    return out
```

```python
from contextlib import ExitStack

import numpy as np

import concourse.bass as bass
from concourse import mybir

F32 = mybir.dt.float32
F32R = mybir.dt.float32r
I32 = mybir.dt.int32
ACT = mybir.ActivationFunctionType
ALU = mybir.AluOpType
AX = mybir.AxisListType

P = 128
DM = 1024
DK = DM // P
TP, DB, DT = 512, 8, 8
TS = DB * DT
T = TP + TS
TT = TP // P
TH = T // 2
TILES = [(i * P, P) for i in range(TT)] + [(TP, TS)]
FF = 2752
FT = -(-FF // P)
FL = FF - (FT - 1) * P
FH = FT // 2
FB = FH + DK
FW = FH * P
ALPHA = 4 ** 0.25
EPS = 1e-5
PW, NG = 512, 4
PAST = 15
EXT = PAST + TP + DB * (PAST + DT)
NH, KV, HPG, HD = 16, 4, 4, 64
HID = 128
PL = 4096
PAGE = 128
NPG = PL // PAGE
CS = 16
NCH = PL // CS
NB = NCH - 1
NBP = TP // CS - 1
NSB = PL // 64 + 1
WIN = 512
NEG = -1e30
STEPS = 52
RING = 4
RB = 2048
ROW = 2 * KV * HD
NLN = 6
LN_OF = [0, 2, 3, 5]
MIX = [1, 4]
Y_BASE = [0, 16, 24, 40, 56, 64]
X_BASE = {1: 8, 2: 16, 4: 24}


def slope(head):
    return 2.0 ** (-8.0 * (head + 1) / NH)


def constants():
    parts = {}
    p = np.arange(P)[:, None]
    parts["ident"] = np.eye(P)
    parts["mean"] = np.full((P, P), 1.0 / DM)
    parts["tri"] = (p <= np.arange(P)[None, :]) * 1.0
    rep = np.zeros((P, TS))
    rep[:DT] = np.tile(np.eye(DT), (1, DB))
    parts["rep"] = rep
    bd = np.zeros((P, TS))
    bd[:TS] = np.kron(np.eye(DB), np.ones((DT, DT)))
    parts["bdiag"] = bd
    parts["rcnt"] = np.tile(np.concatenate([1.0 / np.minimum(w, np.arange(16) + 1) for w in (2, 4, 8, 16)])[None], (P, 1))
    g, t = np.arange(P) // 32, np.arange(P) % 8
    parts["hsum"] = ((g[:, None] == g[None]) & (t[:, None] == t[None])) * 1.0
    d = p + (TP - P) - np.arange(TP)[None]
    parts["negd"] = np.where(d >= 0, -d, NEG)
    n = np.arange(32)[None]
    cmp = []
    for i in range(TT):
        d = p + i * P - (n * CS + 2 * CS - 1)
        cmp.append(np.where((d >= 0) & (n < NBP), -d, NEG))
    parts["negdc"] = np.concatenate(cmp, 1)
    tp = PL + t[:, None]
    n = np.arange(NB + 1)[None]
    d = tp - (n * CS + 2 * CS - 1)
    parts["snegc"] = np.where(d >= 0, -d, NEG)
    q = np.arange(512)[None]
    parts["spos"] = (q % P) * CS + q // P + 0.0 * p
    parts["srow"] = np.stack([-(tp[:, 0]) + h * 2048 + 4 * k for h in range(2) for k in range(4)], 1)
    j, i = q // P, q % P
    kp = PL - WIN + 4 * i + j
    d = tp - kp
    parts["snegw"] = np.where((d >= 0) & (d < WIN), -d, NEG)
    d = t[:, None] - np.arange(DT)[None]
    parts["snegn"] = np.where(d >= 0, -d, NEG)
    sl = slope(np.arange(P) // 8)
    parts["sslope"] = np.stack([sl, -sl], 1)
    gp, h = np.arange(8)[None] // 4, np.arange(8)[None] % 4
    parts["qscale"] = HD ** -0.5 / slope((2 * gp + p // 64) * 4 + h)
    u = np.arange(NH)
    parts["uslope"] = np.tile(slope((u // 8 * 2 + u % 2) * 4 + u // 2 % 4)[None], (P, 1))
    parts["rowpg"] = (p % 8) * 4.0 + np.arange(4)[None]
    at, where, cols = 0, {}, []
    for k, v in parts.items():
        v = np.broadcast_to(v, (P, v.shape[1])).astype(np.float32)
        where[k] = (at, v.shape[1])
        cols.append(v)
        at += v.shape[1]
    return where, np.ascontiguousarray(np.concatenate(cols, 1))


class Chain:

    def __init__(self, eng, sem):
        self.eng, self.sem, self.n, self.off = eng, sem, 0, 0

    def __call__(self, ins):
        self.n += 1
        ins.then_inc(self.sem, 1)
        self.eng.wait_ge(self.sem, self.n + self.off)


def bass_hybrid_trunk_step(nc, a, consts, cdram, outs):
    (x_prompt, x_sample, state_pool, cache_cmp, cache_slc, cache_win, page_table, w_ffn_in, w_ffn_out, ln_g, ln_b,
     w_in_even, pool_w, pool_scale, gm_ln_g, gm_ln_b, gm_ws, gm_b, w_out_even,
     w_in_odd, cmp_pe, cmp_w1, cmp_b1, cmp_w2, w_out_odd) = a
    (y_p, y_s, pool_p, pool_s, gmv_s, cmp_p, slc_p, win_p, cmp_s, slc_s, win_s) = outs
    ctx = ExitStack()
    ctx.enter_context(nc.allow_non_contiguous_dma(reason="small transposed vectors"))
    with ctx:
        at = [-(-nc.sbuf_base // 32) * 32]
        first_byte = {}

        def sb(name, shape, dt=F32, over=None, skip=0):
            size = 4 * int(np.prod(shape[1:]))
            if over is None:
                first_byte[name] = at[0]
                at[0] += -(-size // 32) * 32
            else:
                first_byte[name] = first_byte[over] + 4 * skip
            return nc.alloc_sbuf_tensor_at(name, shape, dt, offset=first_byte[name])

        def sem(name):
            return ctx.enter_context(nc.semaphore(name))

        CN = cdram.shape[1]
        cst = sb("cst", [P, CN])

        def C(name):
            o, w = consts[name]
            return cst[:, o:o + w]

        yT = sb("yT", [P, DK, T])
        x_room = sb("x_room", [P, 2 * DK * T])
        x_hi = sb("x_hi", [P, DK, T], F32R, over="x_room")
        x_lo = sb("x_lo", [P, DK, T], F32R, over="x_room", skip=DK * T)
        big = sb("big", [P, 2 * FH * T])
        h_hi = sb("h_hi", [P, FH, T], F32R, over="big")
        h_lo = sb("h_lo", [P, FH, T], F32R, over="big", skip=FH * T)
        ring = sb("ring", [P, RING, RB])
        w_room = sb("w_room", [P, 4 * RB])
        w_sp = sb("w_sp", [P, 2, 2, RB], F32R, over="w_room")
        act_tmp = sb("act_tmp", [P, 3, T])
        stat = sb("stat", [P, 3, T])
        lng = sb("lng", [P, NLN, DK])
        lnb = sb("lnb", [P, NLN, DK])
        psum = ctx.enter_context(nc.psum_tensor("psum", [P, 4096], F32))
        ident = C("ident")

        def pair(z):
            return psum[:, z * 1024:z * 1024 + T]

        def halves(z):
            return psum[:, z * 1024:(z + 1) * 1024].rearrange("p (c n) -> p c n", c=2)[:, :, 0:TH]

        def hv(x):
            if len(x.shape) == 3:
                return x.rearrange("p o (c n) -> p (o c) n", c=2)
            return x.rearrange("p (c n) -> p c n", c=2)

        def bank(z, n=512):
            return psum[:, z * 512:z * 512 + n]

        consts_in = sem("consts_in")
        x_in = sem("x_in")
        ring_full = [sem(f"ring_full{s}") for s in range(RING)]
        blk_done = sem("blk_done")
        hi_ready = sem("hi_ready")
        lo_ready = sem("lo_ready")
        xt_psum = sem("xt_psum")
        xt_sb = sem("xt_sb")
        xt_first = sem("xt_first")
        silu_ready = sem("silu_ready")
        gu_free = sem("gu_free")
        h_ready = sem("h_ready")
        y_ready = sem("y_ready")
        y_sum = sem("y_sum")
        sq_ready = sem("sq_ready")
        sq_used = sem("sq_used")
        sums_ready = sem("sums_ready")
        stats_done = sem("stats_done")
        mean_ready = sem("mean_ready")
        var_ready = sem("var_ready")
        std_ready = sem("std_ready")
        norm_ready = sem("norm_ready")
        x_full = sem("x_full")
        x_ready = sem("x_ready")
        dve_chain = sem("dve_chain")
        out_done = sem("out_done")
        gmv_out = sem("gmv_out")

        loc_in = sem("loc_in")
        z_ready = sem("z_ready")
        z_freeA = sem("z_freeA")
        z_freeD = sem("z_freeD")
        e_dif = sem("e_dif")
        v_var = sem("v_var")
        v_std = sem("v_std")

        blk_pos = {}
        nblk = 0
        for name, n in [("f0", 2 * FB), ("even", 10), ("f1", 2 * FB), ("f2", 2 * FB), ("odd", 15), ("f3", 2 * FB)]:
            blk_pos[name] = nblk
            nblk += n

        passed = sem("passed")

        def apart(eng):
            eng.sem_inc(passed, 1)

        def full_at(n):
            return 64 * (n // RING + 1)

        ext = big[:, 0:NG * EXT].rearrange("p (g n) -> p g n", g=NG)
        exs = ext[:, :, PAST + TP:].rearrange("p g (b s) -> p g b s", b=DB)
        o = NG * EXT
        uT = big[:, o:o + NG * T].rearrange("p (g n) -> p g n", g=NG)
        o += NG * T
        vtok = big[:, o:o + 5 * PW].rearrange("p (i n) -> p i n", i=5)
        o += 5 * PW
        cat = big[:, o:o + DK * T].rearrange("p (k n) -> p k n", k=DK)
        assert o + DK * T <= FT * T
        loc = x_room
        lo = [0]

        def carve(n):
            lo[0] += n
            assert lo[0] <= 2 * DK * T, lo
            return loc[:, lo[0] - n:lo[0]]
        gms = carve(NG * P).rearrange("p (h s) -> p h s", h=NG)
        wsT = carve(NG * P).rearrange("p (h t) -> p h t", h=NG)
        wsB = carve(NG * TS).rearrange("p (h t) -> p h t", h=NG)
        gmb = carve(NG * P).rearrange("p (h t) -> p h t", h=NG)
        plw = carve(NG * P).rearrange("p (g d) -> p g d", g=NG)
        psc = carve(NG)
        pnew = carve(NG * TS).rearrange("p (g n) -> p g n", g=NG)
        lgg = carve(PW)
        lgb = carve(PW)
        past = carve(PW)
        bns = carve(5 * 6).rearrange("p (i n) -> p i n", i=5)
        mv = carve(5 * 4).rearrange("p (i n) -> p i n", i=5)
        prow_p = carve(PW)
        prow_s = carve(PW)
        sums = carve(2 * EXT).rearrange("p (i n) -> p i n", i=2)
        dif = carve(NG * T).rearrange("p (g n) -> p g n", g=NG)
        xl = big[:, 0:5 * DM].rearrange("p (i n) -> p i n", i=5)

        def cut(region, sizes):
            at, out = 0, {}
            for k, n in sizes:
                out[k] = region[:, at:at + n]
                at += n
            assert at <= region.shape[1], (at, region.shape)
            return out
        b_ = cut(big, [("qT", 8 * T), ("kT", 4 * T), ("vtk", 2 * TT * 256), ("gates", 5 * 48), ("vnew", 512),
                       ("kTc", 2048), ("qb", 256), ("gr", 3 * DB), ("gcur", 4), ("seg", 16)])
        qT = b_["qT"].rearrange("p (i n) -> p i n", i=8)
        kT = b_["kT"].rearrange("p (r g n) -> p r g n", r=2, g=2)
        vtk = b_["vtk"].rearrange("p (r i n) -> p r i n", r=2, i=TT)
        gates = b_["gates"].rearrange("p (i n) -> p i n", i=5)
        vnew = b_["vnew"].rearrange("p (r n) -> p r n", r=2)
        kTc = b_["kTc"].rearrange("p (u g n) -> p u g n", u=2, g=2)
        qb = b_["qb"].rearrange("p (g n) -> p g n", g=2)
        gr = b_["gr"].rearrange("p (b r) -> p b r", b=DB)
        gcur = b_["gcur"]
        y_ = cut(x_room[:, 0:4608], [("oG", 2048), ("sp", 1536), ("free", 512), ("vc", 512)])
        xTc = x_room[:, 0:4096].rearrange("p (u v g n) -> p u v g n", u=2, v=2, g=KV)
        gel = y_["oG"].rearrange("p (v g n) -> p v g n", v=2, g=KV)
        otok = y_["oG"].rearrange("p (i n) -> p i n", i=2)
        sp3 = y_["sp"].rearrange("p (u n) -> p u n", u=3)
        vc = y_["vc"].rearrange("p (i n) -> p i n", i=2)
        w_ = cut(w_room, [("g2", 4096), ("pt", 1024), ("kc", 510), ("gap", 2), ("oc", 12 * HD), ("w2k", 256), ("w2v", HD)])
        gre = w_["g2"].rearrange("p (u v g x) -> p u v g x", u=2, v=2, g=KV)
        kst = w_["g2"][:, 0:2560].rearrange("p (u i n) -> p u i n", u=2, i=5)
        pts = w_["pt"].rearrange("p (u n) -> p u n", u=2)
        kc = w_["kc"].rearrange("p (g n) -> p g n", g=2)
        l_ = cut(x_room[:, 4608:], [("w1c", 4096)])
        w1c = l_["w1c"].rearrange("p (v r k f) -> p v r k f", v=2, r=2, k=8)
        oc = w_["oc"].rearrange("p (a d) -> p a d", a=12)
        w2k = w_["w2k"].rearrange("p (g n) -> p g n", g=2)
        w2v = w_["w2v"]
        a_ = cut(act_tmp[:, :, :].rearrange("p s n -> p (s n)"),
                 [("pp", 264), ("ia", 65), ("ib", 65), ("madd", 65), ("m8", 16), ("kcb", P), ("peT", 32), ("b1", 2),
                  ("hb", 2), ("lp", 64), ("cm", 16), ("cl", 16), ("wts", 12), ("coef", 12), ("mx", 12), ("nb", 12),
                  ("ls", 12), ("tmp", 12), ("od", P)])
        kcb = a_["kcb"].rearrange("p (g n) -> p g n", g=2)
        s_ = cut(stat[:, :, :].rearrange("p i n -> p (i n)"), [("vcb", 512), ("ocs", 12 * HD), ("pst", 4 * 16)])
        vcb = s_["vcb"].rearrange("p (g n) -> p g n", g=2)
        ocs = s_["ocs"].rearrange("p (a d) -> p a d", a=12)
        ps_mx, ps_nb, ps_l, ps_cf = [s_["pst"][:, i * 16:(i + 1) * 16] for i in range(4)]
        extra = sb("extra", [P, RB])
        cmp_slots = [ring[:, 0, :], extra[:, :]]
        idx = sb("idx", [P, 4, 2 * DB], I32)
        idx_cur = sb("idx_cur", [P, 4, 2], I32)[:, :, :]
        idx_set = sem("idx_set")
        y_out = [sem("y_out0"), sem("y_out1")]
        y_tok = sem("y_tok")
        yt_psum = sem("yt_psum")
        ytok = big[:, 0:2 * DM].rearrange("p (i n) -> p i n", i=2)
        ptb = sb("ptb", [P, 2 * DB], I32)
        gscr = nc.dram_tensor("gate_rows", [DB, 48, DT], F32, kind="Internal").ap()

        n_in = sem("n_in")
        pt_in = sem("pt_in")
        idx_ready = sem("idx_ready")
        q_ready = sem("q_ready")
        q_free = sem("q_free")
        kv_ready = sem("kv_ready")
        kv_sb = sem("kv_sb")
        kv_out = [sem("kv_out0"), sem("kv_out1")]
        g_scr = sem("g_scr")
        gr_in = sem("gr_in")
        zeroed = sem("zeroed")
        win_out = sem("win_out")
        cmp_full = [sem("cmp_full0"), sem("cmp_full1")]
        pc_full = [sem("pc_full0"), sem("pc_full1")]
        win_full = sem("win_full")
        cmp_free = sem("cmp_free")
        gre_free = sem("gre_free")
        slc_full = [sem(f"slc_full{s}") for s in range(3)]
        slc_free = sem("slc_free")
        t_ready = sem("t_ready")
        t_act = sem("t_act")
        t_dve = sem("t_dve")
        hid_step = sem("hid_step")
        gel_ready = sem("gel_ready")
        cv_ready = sem("cv_ready")
        cv_sb = sem("cv_sb")
        vn_full = sem("vn_full")
        sc_ready = sem("sc_ready")
        soft = sem("soft")
        p_ready = sem("p_ready")
        p_norm = sem("p_norm")
        ptp_ready = sem("ptp_ready")
        pt_sb = sem("pt_sb")
        o_ready = sem("o_ready")
        o_done = sem("o_done")
        otok_done = sem("otok_done")
        imp_ready = sem("imp_ready")
        imp_done = sem("imp_done")
        q_set = sem("q_set")
        w_ready = sem("w_ready")
        w_exp = sem("w_exp")
        od_ready = sem("od_ready")
        ot_ready = sem("ot_ready")
        ot_done = sem("ot_done")
        hb_ready = sem("hb_ready")
        hb_sb = sem("hb_sb")

        def units():
            out = []
            for i in range(TT):
                out.append(("cmp", i, 0, 0, 0, 0))
                out += [("full", i, r, gp, h, g2) for r in range(2) for gp in range(2) for h in range(HPG) for g2 in range(2)]
            return out
        UNITS = units()
        NU = len(UNITS)
        SU = 12
        CHUNK = {1 + k: k for k in range(8)}
        CHUNK[10] = 8
        R0 = 16 + 2 * TT
        SR = 32 + 18
        assert NU % 6 == 0 and R0 % 2 == 0
        cmp_rows = cache_cmp.rearrange("n (c p) k g d -> (n c) (p k g d)", p=4)
        slc_rows = cache_slc.rearrange("n (c p) k g d -> (n c) (p k g d)", p=4)

        block = ctx.enter_context(nc.Block())

        @block.sync
        def _(sp):
            def load_block(n, pieces):
                if n - RING >= blk_pos["even"] + 10 and n - RING < blk_pos["odd"]:
                    sp.wait_ge(lo_ready, n - blk_pos["f1"] + 2 * FB - (RING - 1))
                elif n - RING < blk_pos["even"]:
                    sp.wait_ge(lo_ready, n - (RING - 1))
                else:
                    sp.wait_ge(blk_done, n - (RING - 1))
                for dst, src in pieces:
                    sp.dma_start(dst, src).then_inc(ring_full[n % RING], 64 // len(pieces))

            def kblock(w, c0, n, slot):
                return ring[:, slot, 0:DK * n].rearrange("p (k n) -> p k n", k=DK), \
                    w.rearrange("(k p) n -> p k n", p=P)[:, :, c0:c0 + n]

            def ffn_loads(l, i, f):
                w1 = w_ffn_in[l, i].rearrange("(k p) n -> p k n", p=P)
                w2 = w_ffn_out[l, i]

                def slot_free(F, n):
                    if isinstance(n, int) and n < RING:
                        return
                    if isinstance(n, int) and f in (1, 3) and n < blk_pos[f"f{f}"] + RING:
                        sp.wait_ge(blk_done, n - (RING - 1))
                    else:
                        sp.wait_ge(lo_ready, F - (RING - 1))

                for h in range(2):
                    F0 = f * 2 * FB + h * FB
                    n0 = blk_pos[f"f{f}"] + h * FB

                    def w1_in(j, u, n=P):
                        s = (n0 + u) % RING
                        slot_free(j + F0, j + n0)
                        v = ring[:, s, 0:2 * DK * n].rearrange("p (k c n) -> p k c n", k=DK, c=2)
                        for c in range(2):
                            d = c if n == P else 1 - c
                            sp.dma_start(v[:, :, d, :], w1[:, :, bass.ds(j * P + (h * FH * P + c * FF), n)])\
                                .then_inc(ring_full[s], 32)

                    def w2_in(m, u):
                        s = (n0 + FH + u) % RING
                        slot_free(m + (F0 + FH), m + (n0 + FH))
                        v = ring[:, s, 0:FW].rearrange("p (k n) -> p k n", n=P)
                        r0, full = h * FW, FH if h == 0 else FH - 1
                        half = FH // 2 if h == 0 else full
                        sp.dma_start(v[:, 0:half], w2[r0:r0 + half * P, bass.ds(m * P, P)]
                                     .rearrange("(k p) n -> p k n", p=P)).then_inc(ring_full[s], 32)
                        if h == 0:
                            sp.dma_start(v[:, half:], w2[half * P:FW, bass.ds(m * P, P)]
                                         .rearrange("(k p) n -> p k n", p=P)).then_inc(ring_full[s], 32)
                        else:
                            sp.dma_start(v[0:FL, full], w2[r0 + full * P:FF, bass.ds(m * P, P)]).then_inc(ring_full[s], 32)

                    for u in range(RING):
                        w1_in(u, u)
                    for j in range(RING, FH):
                        w1_in(j, j, P if h == 0 or j < FH - 1 else FL)
                    with sp.Fori(0, DK // RING) as i:
                        for u in range(RING):
                            w2_in(i * RING + u, u)

            ffn_loads(0, 0, 0)
            n0 = blk_pos["even"]
            for i in range(6):
                load_block(n0 + i, [kblock(w_in_even, i * 256, 256, (n0 + i) % RING)])
            for i in range(4):
                load_block(n0 + 6 + i, [kblock(w_out_even, i * 256, 256, (n0 + 6 + i) % RING)])
            ffn_loads(0, 1, 1)
            ffn_loads(1, 0, 2)
            n0 = blk_pos["odd"]
            wv = w_in_odd.rearrange("(k p) n -> p k n", p=P)
            for gp in range(2):
                for hp in range(2):
                    n = n0 + gp * 2 + hp
                    v = ring[:, n % RING, :].rearrange("p (k h g d) -> p k h g d", k=DK, h=2, g=2)
                    load_block(n, [(v[:, :, h, g2, :], wv[:, :, ((2 * gp + g2) * HPG + 2 * hp + h) * HD:][:, :, 0:HD])
                                   for h in range(2) for g2 in range(2)])
            for c in range(6):
                load_block(n0 + 4 + c, [kblock(w_in_odd, NH * HD + c * 256, 256, (n0 + 4 + c) % RING)])
            load_block(n0 + 10, [kblock(w_in_odd, NH * HD + 6 * 256, 48, (n0 + 10) % RING)])
            sp.wait_ge(blk_done, n0 + 11)
            sp.wait_ge(kv_out[0], 2 * 16)
            sp.wait_ge(kv_out[1], 2 * 16)
            for q in range(4):
                sp.wait_ge(cmp_free, q + 1)
                sp.dma_start(cmp_slots[q % 2][0:TP // CS, :].rearrange("c (p n) -> c p n", p=4),
                             cmp_p[0].rearrange("(c q p) k g d -> q c p (k g d)", q=4, p=4)[q])\
                    .then_inc(pc_full[q % 2], 16)
            sp.dma_start(win_s[:, 0:WIN - DT], cache_win[:, DT:WIN]).then_inc(win_out, 16)
            for c in range(2):
                sp.wait_ge(kv_out[c], 6 * 16)
            with sp.Fori(0, DB) as b:
                sp.wait_ge(o_done, b * SU + NU)
                sp.dma_start(vnew[0:DT, 0, :], slc_s[bass.ds(b, 1), :, 1].rearrange("o t g d -> (o t) (g d)")).then_inc(vn_full, 16)
                sp.dma_start(vnew[0:DT, 1, :], win_s[bass.ds(b, 1), WIN - DT:WIN, 1].rearrange("o t g d -> (o t) (g d)"))\
                    .then_inc(vn_full, 16)
                sp.wait_ge(slc_free, b * 9 + 9)
                apart(sp)
                sp.dma_start(ring[:, 3, :], cache_win[bass.ds(b, 1)].rearrange("o (p j) k g d -> (o p) (j k g d)", j=4))\
                    .then_inc(win_full, 16)
            sp.wait_ge(slc_free, DB * 9 + 3)
            sp.wait_ge(cmp_free, 4 + DB * 8 + 2)
            wo = w_out_odd.rearrange("(a g h d) n -> a g d h n", a=2, g=2, h=HPG)
            for i in range(4):
                n = n0 + 11 + i
                v = ring[:, n % RING, :].rearrange("p (a h n) -> p a h n", a=2, h=HPG)
                load_block(n, [(v[g2 * HD:(g2 + 1) * HD, gp], wo[gp, g2, :, :, i * 256:(i + 1) * 256])
                               for gp in range(2) for g2 in range(2)])
            ffn_loads(1, 1, 3)
            sp.wait_ge(out_done, 3 * 16)
            for c in range(2):
                sp.wait_ge(kv_out[c], 6 * 16)
            sp.wait_ge(win_out, 16)
            sp.wait_ge(y_out[0], 16 * 3)
            sp.wait_ge(y_out[1], 16 * 2)

        @block.gpsimd
        def _(pool):
            def ffn(f):
                def low(F, u, slot, w):
                    pool.wait_ge(hi_ready, F + 1)
                    pool.tensor_tensor(w_sp[:, u % 2, 1, 0:w], ring[:, slot, 0:w], w_sp[:, u % 2, 0, 0:w].bitcast(F32),
                                       ALU.subtract).then_inc(lo_ready, 1)
                for h in range(2):
                    F0 = f * 2 * FB + h * FB
                    n0 = blk_pos[f"f{f}"] + h * FB
                    u0 = h * FB
                    with pool.Fori(0, 2) as i:
                        for u in range(RING):
                            low(i * RING + (F0 + u), u0 + u, (n0 + u) % RING, RB)
                    for j in range(2 * RING, FH):
                        low(F0 + j, u0 + j, (n0 + j) % RING, RB if h == 0 or j < FH - 1 else 2 * DK * FL)
                    with pool.Fori(0, DK // RING) as i:
                        for u in range(RING):
                            low(i * RING + (F0 + FH + u), u0 + FH + u, (n0 + FH + u) % RING, FW)

            ffn(0)
            pool.wait_ge(blk_done, 2 * FB - DK)
            pool.dma_start(gms, gm_ws.rearrange("h t s -> t h s")).then_inc(loc_in, 16)
            pool.dma_start(gmb, gm_b.rearrange("(o h) t -> o h t", o=1).broadcast_to([P, NG, P])).then_inc(loc_in, 16)
            pool.dma_start(plw, pool_w.rearrange("g c d -> c g d")).then_inc(loc_in, 16)
            pool.dma_start(psc, pool_scale.rearrange("(g p) -> p g", p=P)).then_inc(loc_in, 16)
            pool.dma_start(lgg, gm_ln_g.rearrange("(o n) -> o n", o=1).broadcast_to([P, PW])).then_inc(loc_in, 16)
            pool.dma_start(lgb, gm_ln_b.rearrange("(o n) -> o n", o=1).broadcast_to([P, PW])).then_inc(loc_in, 16)
            pool.dma_start(past[0:DB * PAST, :], state_pool.rearrange("b s n -> (b s) n")).then_inc(loc_in, 16)
            pool.dma_start(pool_s[:, 0:PAST - DT, :], state_pool[:, DT:PAST, :]).then_inc(out_done, 16)
            pool.wait_ge(z_freeD, 8)
            pool.dma_start(pool_p.rearrange("o s n -> (o s) n"), prow_p[0:PAST, :]).then_inc(out_done, 16)
            pool.dma_start(pool_s[:, PAST - DT:PAST, :], prow_s[0:TS, :]).then_inc(out_done, 16)
            pool.wait_ge(z_freeD, 13)
            pool.dma_start(gmv_s.rearrange("b t n -> (b t) n"), vtok[0:TS, 4, :]).then_inc(gmv_out, 16)
            pool.wait_ge(gmv_out, 16)
            ffn(1)
            ffn(2)
            pool.wait_ge(x_ready, 4 * DK)
            for g in range(16):
                pool.dma_start(ptb[g * 8:(g + 1) * 8, :], page_table.rearrange("(o b) (h g) -> g o (b h)", o=1, g=16)[g]
                               .broadcast_to([8, 2 * DB])).then_inc(pt_in, 16)
            pool.dma_start(l_["w1c"].rearrange("p (k f) -> p k f", f=HID),
                           cmp_w1.rearrange("v (k p) f -> p (v k) f", p=P)).then_inc(n_in, 16)
            for g2 in range(2):
                pool.dma_start(w2k[:, g2, g2 * HD:(g2 + 1) * HD], cmp_w2[0]).then_inc(n_in, 16)
            pool.dma_start(w2v, cmp_w2[1]).then_inc(n_in, 16)
            pool.memset(w2k[:, 0, HD:P], 0.0).then_inc(zeroed, 1)
            pool.memset(w2k[:, 1, 0:HD], 0.0).then_inc(zeroed, 1)
            for g2 in range(2):
                for k in range(2):
                    pe_ = cmp_pe[k].rearrange("(k p) d -> p d k", p=2)[g2]
                    pool.dma_start(a_["peT"][g2 * HD:(g2 + 1) * HD, k * 16:(k + 1) * 16], pe_).then_inc(n_in, 16)
            pool.dma_start(a_["b1"], cmp_b1.rearrange("v f -> f v")).then_inc(n_in, 16)
            pool.memset(a_["pp"], 0.0).then_inc(zeroed, 1)
            pool.memset(a_["kcb"], 0.0).then_inc(zeroed, 1)
            pool.memset(s_["vcb"], 0.0).then_inc(zeroed, 1)
            pool.memset(b_["qb"], 0.0).then_inc(zeroed, 1)
            kv_dst = [(cmp_p, cmp_s), (slc_p, slc_s), (win_p, win_s[:, WIN - DT:WIN])]
            for c in range(6):
                r, v = c // 2, c % 2
                pool.wait_ge(kv_sb, c + 1)
                pool.dma_start(kv_dst[r][0][0].rearrange("(i p) k g d -> p i k (g d)", p=P)[:, :, v],
                               vtk[:, r - 1] if v and r else kst[:, c % 2, 0:TT]).then_inc(kv_out[c % 2], 16)
                pool.dma_start(kv_dst[r][1].rearrange("b t k g d -> b t k (g d)")[:, :, v],
                               kst[0:TS, c % 2, TT, :]).then_inc(kv_out[c % 2], 16)
            pool.wait_ge(q_free, 13)
            for i in range(DB):
                pool.dma_start(gscr[i].rearrange("c t -> t c"), gates[i * DT:(i + 1) * DT, TT, :]).then_inc(g_scr, 16)
            pool.wait_ge(g_scr, 16 * DB)
            for r in range(3):
                pool.dma_start(gr[:, :, r], gscr.rearrange("b (r u) t -> r (u t) b", r=3)[r]).then_inc(gr_in, 16)
            pool.wait_ge(idx_ready, 4)
            pool.wait_ge(blk_done, blk_pos["odd"] + 11)

            def gather(dst, rows, q, bh, full):
                pool.indirect_dma_start(out=dst, out_offset=None, in_=rows,
                                        in_offset=bass.IndirectOffsetOnAxis(ap=idx_cur[:, q, bh:bh + 1], axis=0)).then_inc(full, 16)
            with pool.Fori(0, DB) as b:
                pool.tensor_copy(idx_cur, idx[:, :, bass.ds(b * 2, 2)]).then_inc(idx_set, 1)
                pool.wait_ge(idx_set, b + 1)
                for i in range(8):
                    pool.wait_ge(cmp_free, b * 8 + (4 + i + 1))
                    apart(pool)
                    gather(cmp_slots[i % 2], cmp_rows, i // 2, i % 2, cmp_full[i % 2])
                for k in range(8):
                    pool.wait_ge(slc_free, b * 9 + (k + 1))
                    apart(pool)
                    gather(ring[:, 1 + k % 3, :], slc_rows, k % 4, k // 4, slc_full[k % 3])
                for s in range(2):
                    pool.wait_ge(cmp_full[s], b * 64 + 64)
                for s in range(3):
                    pool.wait_ge(slc_full[s], (b + 1) * (48 if s < 2 else 32))
            ffn(3)

        @block.scalar
        def _(act):
            act.dma_start(cst[:, :], cdram).then_inc(consts_in, 16)
            for i, (t0, n) in enumerate(TILES):
                src = x_prompt[0, t0:t0 + n, :] if i < TT else x_sample.rearrange("b t n -> (b t) n")
                act.dma_start(xl[0:n, i, :], src).then_inc(x_in, 16)
            act.dma_start(lng[:, :, :], ln_g.rearrange("l i (k p) -> p (l i) k", p=P)).then_inc(consts_in, 16)
            act.dma_start(lnb[:, :, :], ln_b.rearrange("l i (k p) -> p (l i) k", p=P)).then_inc(consts_in, 16)
            act.wait_ge(consts_in, 48)

            def high(f, U, full, done, slot, w=RB):
                act.wait_ge(ring_full[slot], full)
                if done is not None:
                    act.wait_ge(blk_done, done)
                act.activation(w_sp[:, U % 2, 0, 0:w], ring[:, slot, 0:w], ACT.Copy).then_inc(hi_ready, 1)

            def width(U):
                u = U % FB
                return FW if u >= FH else 2 * DK * FL if U == FB + FH - 1 else RB

            def high_at(f, U):
                n = blk_pos[f"f{f}"] + U
                high(f, U, full_at(n), n - 1 if U >= 2 else None, n % RING, width(U))

            def high_in(f, i, U):
                n = blk_pos[f"f{f}"] + U
                high(f, U, i * 64 + full_at(n), i * RING + (n - 1), n % RING, width(U))
            for U in range(2):
                high_at(0, U)
            for k in range(DK):
                act.wait_ge(xt_sb, k + 1)
                act.activation(x_hi[:, k, :], yT[:, k, :], ACT.Copy).then_inc(x_full, 1)

            def ffn(f):
                for h in range(2):
                    n0 = blk_pos[f"f{f}"] + h * FB

                    def silu(j, s, n=P):
                        act.wait_ge(blk_done, j + (n0 + 1))
                        act.activation(act_tmp[0:n, s, :].rearrange("p (c n) -> p c n", c=2), halves(2 * s)[P - n:P],
                                       ACT.Silu).then_inc(silu_ready, 1)
                    silu(0, 0)
                    high_at(f, h * FB + 2)
                    with act.Fori(0, 2) as i:
                        for u in range(1, 1 + RING):
                            silu(i * RING + u, u % 2)
                            high_in(f, i, h * FB + u + 2)
                    for j in range(1 + 2 * RING, FH):
                        silu(j, j % 2, P if h == 0 or j < FH - 1 else FL)
                        high_at(f, h * FB + j + 2)
                    if h == 0:
                        for m in range(DK):
                            high_at(f, FH + m + 2)

            def norm(ln, before=None, after=None):
                b = ln * DK
                y0 = Y_BASE[ln] + 2 + (DK if ln not in MIX else 0)
                for m in range(DK):
                    if before is not None and m + 2 < DK:
                        high_at(before, FB + FH + m + 2)
                    act.wait_ge(y_sum, y0 + m + 1)
                    if m >= 3:
                        act.wait_ge(sq_used, ln * (DK - 1) + max(1, m - 3))
                    act.activation(act_tmp[:, m % 3, :], yT[:, m, :], ACT.Square).then_inc(sq_ready, 1)
                if after is not None:
                    high_at(after, 0)
                act.wait_ge(stats_done, ln + 1)
                act.activation(hv(stat[:, 0, :]), halves(0), ACT.Copy).then_inc(mean_ready, 1)
                act.wait_ge(var_ready, ln + 1)
                act.activation(stat[:, 2, :], stat[:, 1, :], ACT.Sqrt).then_inc(std_ready, 1)
                if ln == 1:
                    act.wait_ge(out_done, 3 * 16)
                for m in range(DK):
                    act.wait_ge(norm_ready, b + m + 1)
                    g, c = lng[:, ln, m:m + 1], lnb[:, ln, m:m + 1]
                    if after is not None:
                        act.activation(x_hi[:, m, :], yT[:, m, :], ACT.Identity, bias=c, scale=g)
                    act.activation(yT[:, m, :], yT[:, m, :], ACT.Identity, bias=c, scale=g)\
                        .then_inc(x_ready if after is None else x_full, 1)
                if after is not None:
                    high_at(after, 1)

            ffn(0)
            norm(0, before=0)
            act.wait_ge(loc_in, 7 * 16)
            for h in range(NG):
                act.wait_ge(z_ready, 4 + h + 1)
                act.activation(hv(uT[:, h, :]), halves(h), ACT.Copy).then_inc(z_freeA, 1)
            for i, (t0, n) in enumerate(TILES):
                act.wait_ge(v_var, i + 1)
                act.activation(mv[0:n, i, 3:4], mv[0:n, i, 2:3], ACT.Sqrt).then_inc(v_std, 1)
            for g in range(NG):
                act.wait_ge(z_ready, 22 + g)
                act.activation(hv(cat[:, g, :]), halves((g + 1) % 4), ACT.Copy, scale=psc[:, g:g + 1]).then_inc(z_freeA, 1)
            norm(1, after=1)
            ffn(1)
            norm(2, before=1, after=2)
            ffn(2)
            norm(3, before=2)

            for z in range(8):
                act.wait_ge(q_ready, z + 1)
                act.activation(hv(qT[:, z, :]), halves(z % 4), ACT.Copy, scale=C("qscale")[:, z:z + 1]).then_inc(q_free, 1)
            for r in range(2):
                for gp in range(2):
                    z = 8 + 2 * r + gp
                    act.wait_ge(q_ready, z + 1)
                    act.activation(hv(kT[:, r, gp, :]), halves(3), ACT.Copy).then_inc(q_free, 1)
            act.wait_ge(q_ready, 13)
            act.activation(gates[:, 0:TT, :], bank(0, TT * 48).rearrange("p (i n) -> p i n", i=TT), ACT.Sigmoid)
            act.activation(gates[0:TS, TT, :], bank(0)[0:TS, TT * 48:(TT + 1) * 48], ACT.Sigmoid).then_inc(q_free, 1)

            def t_round(n, dst, src):
                act.wait_ge(t_ready, n + 1)
                act.activation(dst, src, ACT.Copy).then_inc(t_act, 1)

            def xtc_round(base, kt, v, half, width):
                t_round(base, xTc[:, kt, v, :, half * P:half * P + width],
                        bank(0, KV * width).rearrange("p (g c) -> p g c", g=KV))

            def exps(n, s, w, scale, bias, accum):
                act.wait_ge(soft, n + 1)
                if accum is None:
                    act.activation(sp3[:, s, 0:w], sp3[:, s, 0:w], ACT.Exp).then_inc(p_ready, 1)
                else:
                    act.activation(sp3[:, s, 0:w], sp3[:, s, 0:w], ACT.Exp, scale=scale, bias=bias,
                                   accum_out=accum).then_inc(p_ready, 1)

            def pt_copy(n, u, rows, w):
                act.wait_ge(ptp_ready, n + 1)
                if not isinstance(rows, int):
                    act.activation(pts[0:rows[0], u, 0:P], bank(4 + u)[0:rows[0], 0:P], ACT.Copy)
                    act.activation(pts[0:rows[1], u, P:2 * P], bank(4 + u)[0:rows[1], P:2 * P], ACT.Copy).then_inc(pt_sb, 1)
                else:
                    act.activation(pts[0:rows, u, 0:w], bank(4 + u)[0:rows, 0:w], ACT.Copy).then_inc(pt_sb, 1)

            act.wait_ge(n_in, 9 * 16)
            act.wait_ge(hb_ready, 1)
            for k in range(2):
                ins = act.activation(a_["hb"][:, k:k + 1], bank(7)[:, k:k + 1], ACT.Identity, bias=a_["b1"][:, k:k + 1])
            ins.then_inc(hb_sb, 1)
            act.wait_ge(hb_sb, 1)
            for st in range(8):
                xtc_round(2 * st, st % 2, 0, 0, 32)
            act.wait_ge(hid_step, 8)
            for v in range(2):
                act.activation(gel[:, v, :, 0:NBP], bank(2 + v, KV * NBP).rearrange("p (g n) -> p g n", g=KV),
                               ACT.Gelu_apprx_tanh, bias=a_["hb"][:, v:v + 1]).then_inc(gel_ready, 1)
            def prompt_exp(n):
                kind, i, r, gp, h, g2 = UNITS[n]
                sl = slope((2 * gp + g2) * HPG + h)
                if kind == "cmp":
                    exps(n, n % 3, 512, None, None, None)
                else:
                    exps(n, n % 3, (i + 1) * P, sl, ps_nb[:, n % 16:n % 16 + 1], ps_l[:, n % 16:n % 16 + 1])

            prompt_exp(0)
            for n, (kind, i, r, gp, h, g2) in enumerate(UNITS):
                pt_copy(n, n % 2, P, 512 if kind == "cmp" else (i + 1) * P)
                if n + 1 < NU:
                    prompt_exp(n + 1)
                if n + 1 == NU or UNITS[n + 1][0] == "cmp":
                    t_round(16 + 2 * i, qT[:, 0:4, i * P:(i + 1) * P], bank(0).rearrange("p (h t) -> p h t", h=HPG))
            with act.Fori(0, DB) as b:
                rb = b * SR
                for st in range(8):
                    for v in range(2):
                        xtc_round(rb + (R0 + 4 * st + 2 * v), st % 2, v, 0, P)
                act.wait_ge(hid_step, b * 8 + 16)
                for v in range(2):
                    for gp in range(2):
                        act.activation(gel[:, v, 2 * gp:2 * gp + 2, 0:NB],
                                       bank(2 + 2 * v + gp, 2 * NB).rearrange("p (g n) -> p g n", g=2),
                                       ACT.Gelu_apprx_tanh, bias=a_["hb"][:, v:v + 1]).then_inc(gel_ready, 1)
                ub = b * SU
                sl, nsl = C("sslope")[:, 0:1], C("sslope")[:, 1:2]

                def unit_width(a):
                    return NB if a == 0 else DT if a in (9, 11) else 512

                for a in range(SU + 1):
                    if a < SU and a in CHUNK:
                        t_round(rb + (R0 + 32 + 2 * CHUNK[a]), kTc[:, a % 2, 0, :], bank(0))
                    if a > 0:
                        p = a - 1
                        if p == 0:
                            pt_copy(ub + (NU + p), p % 2, (P, NB - P), None)
                        else:
                            pt_copy(ub + (NU + p), p % 2, P if unit_width(p) == 512 else DT, 512 if unit_width(p) == 512 else P)
                    if a < SU:
                        exps(ub + (NU + a), a % 3, unit_width(a), sl, a_["nb"][:, a:a + 1], a_["ls"][:, a:a + 1])
                act.wait_ge(w_ready, b + 1)
                act.activation(a_["wts"][:, 1:10], a_["mx"][:, 1:10], ACT.Exp, scale=sl, bias=b_["seg"][:, 2:3])
                act.activation(a_["wts"][:, 10:12], a_["mx"][:, 10:12], ACT.Exp, scale=sl, bias=b_["seg"][:, 3:4])\
                    .then_inc(w_exp, 1)
            norm(4, after=3)
            ffn(3)
            norm(5, before=3)
            for i, (t0, n) in enumerate(TILES):
                act.wait_ge(y_tok, i + 1)
                dst = y_p[0, t0:t0 + n, :] if i < TT else y_s.rearrange("b t n -> (b t) n")
                act.dma_start(dst, ytok[0:n, i % 2, :]).then_inc(y_out[i % 2], 16)

        @block.vector
        def _(dve):
            step = Chain(dve, dve_chain)
            dve.sem_inc(gu_free, 2)
            dve.sem_inc(y_sum, 2)
            dve.sem_inc(h_ready, 1)
            dve.sem_inc(ot_done, 1)
            for k in range(DK):
                dve.wait_ge(xt_psum, k + 1)
                dve.tensor_copy(yT[:, k, :], pair(k % 4)).then_inc(xt_sb, 1)
            dve.wait_ge(xt_sb, DK)
            for k in range(DK):
                dve.wait_ge(x_full, k + 1)
                dve.tensor_tensor(x_lo[:, k, :], yT[:, k, :], x_hi[:, k, :].bitcast(F32), ALU.subtract).then_inc(xt_first, 1)

            def add(scale, m, sem_, count):
                dve.wait_ge(sem_, count)
                y = hv(yT[:, m, :]) if isinstance(m, int) else hv(yT[:, bass.ds(m[0], 1), :])
                slot = m % 2 if isinstance(m, int) else m[1] % 2
                dve.scalar_tensor_tensor(y, y, scale, halves(2 + slot), ALU.mult, ALU.add).then_inc(y_sum, 1)

            def last_sums(ln, scale, sem_, count):
                y0 = Y_BASE[ln] + 2 + (DK if ln not in MIX else 0)

                def squares(m):
                    dve.wait_ge(sq_ready, ln * DK + m + 1)
                    first = act_tmp[:, 0, :] if m == 1 else stat[:, 1, :]
                    if m > 1:
                        dve.wait_ge(sq_used, ln * (DK - 1) + m - 1)
                    dve.tensor_tensor(stat[:, 1, :], first, act_tmp[:, m % 3, :], ALU.add).then_inc(sq_used, 1)
                for m in range(DK):
                    add(scale, m, sem_, count + m + 1)
                    dve.wait_ge(y_sum, y0 + m + 1)
                    if m > 0:
                        first = yT[:, 0, :] if m == 1 else stat[:, 0, :]
                        step(dve.tensor_tensor(stat[:, 0, :], first, yT[:, m, :], ALU.add))
                    if m > 1:
                        squares(m - 1)
                squares(DK - 1)
                dve.wait_ge(sq_used, (ln + 1) * (DK - 1))
                dve.sem_inc(sums_ready, 1)

            def ffn(f):
                for h in range(2):
                    c = f * FT + h * FH
                    n0 = blk_pos[f"f{f}"] + h * FB

                    def hidden(j, s, n=P):
                        dve.wait_ge(silu_ready, j + (c + 1))
                        gate = act_tmp[0:n, s, :].rearrange("p (c n) -> p c n", c=2)
                        up = halves(2 * s + (1 if n == P else 0))[0:n]
                        hh = hv(h_hi[0:n, bass.ds(j, 1), :])
                        dve.tensor_tensor(hh, gate, up, ALU.mult)
                        dve.wait_ge(h_ready, j + (c + 1))
                        dve.tensor_tensor(act_tmp[0:n, 2, :].rearrange("p (c n) -> p c n", c=2), gate, up, ALU.mult)\
                            .then_inc(gu_free, 1)
                        dve.wait_ge(gu_free, j + (c + 3))
                        dve.tensor_tensor(h_lo[0:n, bass.ds(j, 1), :], act_tmp[0:n, 2:3, :],
                                          h_hi[0:n, bass.ds(j, 1), :].bitcast(F32), ALU.subtract).then_inc(h_ready, 1)
                    with dve.Fori(0, FH // 2) as i:
                        for u in range(2):
                            hidden(i * 2 + u, u)
                    hidden(FH - 1, (FH - 1) % 2, P if h == 0 else FL)
                    if h == 0:
                        with dve.Fori(0, DK // 2) as i:
                            for u in range(2):
                                add(2 * ALPHA, (i * 2 + u, u), blk_done, i * 2 + (n0 + FH + u + 1))
                    else:
                        last_sums(LN_OF[f], 1.0, blk_done, n0 + FH)

            def norm(ln, eps):
                b = ln * DK

                def low(m):
                    dve.wait_ge(x_full, X_BASE[ln] + m + 1)
                    dve.tensor_tensor(x_lo[:, m, :], yT[:, m, :], x_hi[:, m, :].bitcast(F32), ALU.subtract)\
                        .then_inc(x_ready, 1)
                dve.wait_ge(mean_ready, ln + 1)
                step(dve.tensor_tensor(stat[:, 1, :], stat[:, 0, :], stat[:, 0, :], ALU.mult))
                step(dve.tensor_tensor(hv(stat[:, 1, :]), halves(1), hv(stat[:, 1, :]), ALU.subtract))
                dve.tensor_scalar(stat[:, 1, :], stat[:, 1, :], 0.0, eps, ALU.max, ALU.add).then_inc(var_ready, 1)
                dve.wait_ge(std_ready, ln + 1)
                step(dve.reciprocal(stat[:, 2, :], stat[:, 2, :]))
                for m in range(DK):
                    step(dve.tensor_tensor(yT[:, m, :], yT[:, m, :], stat[:, 0, :], ALU.subtract))
                    dve.tensor_tensor(yT[:, m, :], yT[:, m, :], stat[:, 2, :], ALU.mult).then_inc(norm_ready, 1)
                    if ln in X_BASE and m > 0:
                        low(m - 1)
                if ln in X_BASE:
                    low(DK - 1)

            ffn(0)
            norm(0, 4 * EPS)

            dve.wait_ge(loc_in, 7 * 16)
            step(dve.memset(ext[:, :, 0:PAST], 0.0))
            for g in range(NG):
                dve.wait_ge(z_ready, g + 1)
                step(dve.tensor_copy(ext[:, g, PAST:PAST + TP], psum[:, g * 1024:g * 1024 + TP]))
                step(dve.tensor_copy(pnew[:, g, :], psum[:, g * 1024 + TP:g * 1024 + T]))
                dve.tensor_copy(exs[:, g, :, PAST:], psum[:, g * 1024 + TP:g * 1024 + T]
                                .rearrange("p (b t) -> p b t", b=DB)).then_inc(z_freeD, 1)
            dve.wait_ge(z_ready, 9)
            dve.tensor_tensor(wsT, bank(0).rearrange("p (h t) -> p h t", h=NG),
                              C("tri").rearrange("p (o t) -> p o t", o=1).broadcast_to([P, NG, P]),
                              ALU.mult).then_inc(z_freeD, 1)
            dve.wait_ge(z_ready, 10)
            for g in range(NG):
                ins = dve.tensor_copy(exs[:, g, :, 0:PAST], bank(2)[:, g * DB * PAST:(g + 1) * DB * PAST]
                                      .rearrange("p (b s) -> p b s", b=DB))
            ins.then_inc(z_freeD, 1)
            dve.wait_ge(z_ready, 11)
            dve.tensor_tensor(wsB[0:TS], bank(4, NG * TS)[0:TS].rearrange("p (h t) -> p h t", h=NG),
                              C("bdiag")[0:TS].rearrange("p (o t) -> p o t", o=1).broadcast_to([TS, NG, TS]),
                              ALU.mult).then_inc(z_freeD, 1)
            dve.wait_ge(z_ready, 12)
            dve.tensor_copy(prow_p[0:PAST, :], bank(6)[0:PAST])
            dve.tensor_copy(prow_s[0:TS, :], bank(7)[0:TS]).then_inc(z_freeD, 1)
            for i, (t0, n) in enumerate(TILES):
                src = bank(2 * (i % 4))[0:n]
                dve.wait_ge(z_ready, 13 + i)
                step(dve.bn_stats(bns[0:n, i, :], src))
                step(dve.bn_aggr(mv[0:n, i, 0:2], bns[0:n, i, :]))
                dve.tensor_scalar(mv[0:n, i, 2:3], mv[0:n, i, 1:2], EPS, None, ALU.add).then_inc(v_var, 1)
                dve.wait_ge(v_std, i + 1)
                step(dve.reciprocal(mv[0:n, i, 3:4], mv[0:n, i, 3:4]))
                step(dve.tensor_scalar(vtok[0:n, i, :], src, mv[0:n, i, 0:1], mv[0:n, i, 3:4],
                                       ALU.subtract, ALU.mult))
                step(dve.tensor_tensor(vtok[0:n, i, :], vtok[0:n, i, :], lgg[0:n], ALU.mult))
                dve.tensor_tensor(vtok[0:n, i, :], vtok[0:n, i, :], lgb[0:n], ALU.add).then_inc(z_freeD, 1)
            dve.wait_ge(z_freeD, 13)
            for g in range(NG):
                src = ext[:, g, :]
                for r in range(g + 1):
                    w = 1 << r
                    dst = sums[:, r % 2, :]
                    lo_ = 2 * w - 1
                    step(dve.tensor_tensor(dst[:, lo_:], src[:, lo_:], src[:, lo_ - w:EXT - w], ALU.add))
                    src = dst
                d = dif[:, g, :]
                step(dve.scalar_tensor_tensor(d[:, 0:TP], src[:, PAST:PAST + TP], 0.5 ** (g + 1),
                                              ext[:, g, PAST:PAST + TP], ALU.mult, ALU.subtract))
                step(dve.tensor_tensor(d[:, 0:16], src[:, PAST:PAST + 16], C("rcnt")[:, g * 16:g * 16 + 16], ALU.mult))
                step(dve.tensor_tensor(d[:, 0:16], d[:, 0:16], ext[:, g, PAST:PAST + 16], ALU.subtract))
                dve.scalar_tensor_tensor(
                    d[:, TP:T].rearrange("p (b t) -> p b t", b=DB),
                    src[:, PAST + TP:].rearrange("p (b s) -> p b s", b=DB)[:, :, PAST:], 0.5 ** (g + 1),
                    exs[:, g, :, PAST:], ALU.mult, ALU.subtract).then_inc(e_dif, 1)
                dve.wait_ge(e_dif, g + 1)
            dve.wait_ge(z_freeA, NG)
            for h in range(NG):
                s = (h + 1) % 4
                dve.wait_ge(z_ready, 18 + h)
                pp, ps = psum[:, s * 1024:s * 1024 + TP], psum[:, s * 1024 + TP:s * 1024 + T]
                cp, cs = cat[:, NG + h, 0:TP], cat[:, NG + h, TP:T]
                step(dve.tensor_tensor(cp.rearrange("p (c t) -> p c t", c=TT), pp.rearrange("p (c t) -> p c t", c=TT),
                                       gmb[:, h:h + 1, :].broadcast_to([P, TT, P]), ALU.add))
                step(dve.tensor_tensor(cs.rearrange("p (b t) -> p b t", b=DB), ps.rearrange("p (b t) -> p b t", b=DB),
                                       gmb[:, h:h + 1, 0:DT].broadcast_to([P, DB, DT]), ALU.add))
                dve.tensor_tensor(cat[:, NG + h, :], cat[:, NG + h, :], uT[:, h, :], ALU.mult).then_inc(z_freeD, 1)
            last_sums(1, ALPHA, y_ready, 0)
            dve.wait_ge(out_done, 3 * 16)
            norm(1, EPS)
            dve.wait_ge(gmv_out, 16)
            ffn(1)
            norm(2, 4 * EPS)
            ffn(2)
            norm(3, 4 * EPS)

            dve.wait_ge(pt_in, 16 * 16)
            for q in range(4):
                dve.tensor_scalar(idx[:, q, :], ptb[:, :], 32.0, C("rowpg")[:, q:q + 1], ALU.mult, ALU.add)\
                    .then_inc(idx_ready, 1)
            for c in range(6):
                r, v = c // 2, c % 2
                o0 = (c % 2) * 3
                dve.wait_ge(kv_ready, c + 1)
                if c >= 2:
                    dve.wait_ge(kv_out[c % 2], 16 * 2 * (c // 2))
                src = psum[:, o0 * 512:o0 * 512 + 1024].rearrange("p (i n) -> p i n", i=TT)
                dve.tensor_copy(vtk[:, r - 1] if v and r else kst[:, c % 2, 0:TT], src)
                dve.tensor_copy(kst[0:TS, c % 2, TT, :], bank(o0 + 2)[0:TS, 0:256]).then_inc(kv_sb, 1)

            def t_round(n, dst, src):
                dve.wait_ge(t_ready, n + 1)
                return dve.tensor_copy(dst, src).then_inc(t_dve, 1)

            def xtc_round(base, kt, v, half, width):
                t_round(base, xTc[:, kt, v, :, half * P:half * P + width],
                        bank(1, KV * width).rearrange("p (g c) -> p g c", g=KV))

            def regroup(sems, slot, full, free, rows):
                dve.wait_ge(sems[slot], full)
                dve.wait_ge(gre_free, free)
                src = cmp_slots[slot][0:rows].rearrange("c (p v g d) -> c v g p d", p=4, v=2, g=KV)
                dst = gre[0:rows, slot].rearrange("c v g (p d) -> c v g p d", p=4)
                dve.tensor_copy(dst[:, 0], src[:, 0])
                dve.tensor_copy(dst[:, 1], src[:, 1]).then_inc(cmp_free, 1)

            dve.wait_ge(kv_out[0], 6 * 16)
            dve.wait_ge(kv_out[1], 6 * 16)
            for q in range(4):
                regroup(pc_full, q % 2, 16 * (q // 2 + 1), q + 1, TP // CS)
                for kt in range(2):
                    xtc_round(4 * q + 2 * kt + 1, kt, 1, 0, 32)
            dve.wait_ge(zeroed, 6)
            dve.wait_ge(cv_ready, 1)
            for g2 in range(2):
                ins = dve.tensor_copy(kcb[g2 * HD:(g2 + 1) * HD, :, g2 * 32:g2 * 32 + NBP],
                                      bank(6, 2 * NBP)[g2 * HD:(g2 + 1) * HD].rearrange("p (g n) -> p g n", g=2))
            ins.then_inc(cv_sb, 1)
            dve.wait_ge(cv_ready, 2)
            src = bank(7, 256)[0:NBP].rearrange("p (a g d) -> p a g d", a=2, g=2)
            for h2 in range(2):
                for g2 in range(2):
                    o0 = (h2 * 2 + g2)
                    ins = dve.tensor_copy(vcb[o0 * 32:o0 * 32 + NBP, :, o0 * HD:(o0 + 1) * HD], src[:, :, g2, :])
            ins.then_inc(cv_sb, 1)

            def prompt_soft(n):
                kind, i, r, gp, h, g2 = UNITS[n]
                dve.wait_ge(sc_ready, n + 1)
                if n >= 3:
                    dve.wait_ge(ptp_ready, n - 2)
                S = sp3[:, n % 3, :]
                if kind == "cmp":
                    S3 = S.rearrange("p (u n) -> p u n", u=NH)

                    def bc(x):
                        return x.rearrange("p (u o) -> p u o", o=1).broadcast_to([P, NH, 32])
                    step(dve.tensor_tensor(S3, bank(2 + n % 2).rearrange("p (u n) -> p u n", u=NH),
                                           C("negdc")[:, i * 32:(i + 1) * 32].rearrange("p (o n) -> p o n", o=1)
                                           .broadcast_to([P, NH, 32]), ALU.add))
                    step(dve.tensor_reduce(a_["cm"], S3, AX.X, ALU.max))
                    step(dve.tensor_scalar(a_["cm"], a_["cm"], -1e20, None, ALU.max))
                    step(dve.tensor_tensor(S3, S3, bc(a_["cm"]), ALU.subtract))
                    dve.tensor_tensor(S3, S3, bc(C("uslope")), ALU.mult).then_inc(soft, 1)
                    dve.wait_ge(p_ready, n + 1)
                    step(dve.tensor_reduce(a_["cl"], S3, AX.X, ALU.add))
                    step(dve.tensor_scalar(a_["cl"], a_["cl"], 1e-30, None, ALU.max))
                    step(dve.reciprocal(a_["cl"], a_["cl"]))
                    step(dve.tensor_tensor(a_["cl"].rearrange("p (a h g) -> p a h g", a=2, h=HPG),
                                           a_["cl"].rearrange("p (a h g) -> p a h g", a=2, h=HPG),
                                           gates[:, i, 0:NH].rearrange("p (a g h) -> p a h g", a=2, g=2), ALU.mult))
                    dve.tensor_tensor(S3, S3, bc(a_["cl"]), ALU.mult).then_inc(p_norm, 1)
                    return
                c = n % 16
                w = (i + 1) * P
                step(dve.tensor_tensor_reduce(out=S[:, 0:w], in0=bank(2 + n % 2, w), in1=C("negd")[:, TP - w:TP], scale=1.0,
                                              scalar=-3e38, op0=ALU.add, op1=ALU.max, accum_out=ps_mx[:, c:c + 1]))
                dve.tensor_scalar(ps_nb[:, c:c + 1], ps_mx[:, c:c + 1], -slope((2 * gp + g2) * HPG + h), None,
                                  ALU.mult).then_inc(soft, 1)

            def prompt_out(n):
                kind, i, r, gp, h, g2 = UNITS[n]
                O = otok[:, i % 2, :]
                if kind == "cmp":
                    dve.wait_ge(o_ready, n + 1)
                    dve.tensor_copy(O, psum[:, 6 * 512:8 * 512]).then_inc(o_done, 1)
                    return
                c = n % 16
                dve.wait_ge(p_ready, n + 1)
                step(dve.reciprocal(ps_cf[:, c:c + 1], ps_l[:, c:c + 1]))
                gc = (1 + r) * NH + (2 * gp + g2) * HPG + h
                step(dve.tensor_tensor(ps_cf[:, c:c + 1], ps_cf[:, c:c + 1], gates[:, i, gc:gc + 1], ALU.mult))
                dve.wait_ge(o_ready, n + 1)
                dve.wait_ge(o_done, n)
                u = (gp * HPG + h) * 2 + g2
                dve.scalar_tensor_tensor(O[:, u * HD:(u + 1) * HD], bank(6 + n % 2, HD), ps_cf[:, c:c + 1],
                                         O[:, u * HD:(u + 1) * HD], ALU.mult, ALU.add).then_inc(o_done, 1)

            prompt_soft(0)
            for n, (kind, i, r, gp, h, g2) in enumerate(UNITS):
                if n + 1 < NU:
                    if UNITS[n + 1][0] == "cmp":
                        prompt_out(n)
                        dve.wait_ge(o_done, n + 1)
                        prompt_soft(n + 1)
                    else:
                        prompt_soft(n + 1)
                        prompt_out(n)
                else:
                    prompt_out(n)
                if n + 1 == NU or UNITS[n + 1][0] == "cmp":
                    t_round(16 + 2 * i + 1, qT[:, 4:8, i * P:(i + 1) * P], bank(1).rearrange("p (h t) -> p h t", h=HPG))

            dve.wait_ge(gr_in, 16 * 3)
            nsl = C("sslope")[:, 1:2]
            with dve.Fori(0, DB) as b:
                step.off = b * STEPS
                n_before = step.n
                for g2 in range(2):
                    for gp in range(2):
                        g = 2 * gp + g2
                        dve.tensor_copy(qb[g2 * HD:(g2 + 1) * HD, gp, g * 32:(g + 1) * 32].rearrange("p (h t) -> p h t", h=HPG),
                                        qT[g2 * HD:(g2 + 1) * HD, gp * HPG:(gp + 1) * HPG, bass.ds(b * DT + TP, DT)])\
                            .then_inc(q_set, 1)
                step(dve.tensor_copy(gcur[:, 0:3].rearrange("p (o r) -> p o r", o=1), gr[:, bass.ds(b, 1), :]))
                rb = b * SR
                for q in range(4):
                    for half in range(2):
                        regroup(cmp_full, half, b * 64 + 16 * (q + 1), b * 8 + (4 + 2 * q + half + 1), P)
                    for kt in range(2):
                        for v in range(2):
                            xtc_round(rb + (R0 + 4 * (2 * q + kt) + 2 * v + 1), kt, v, 1, P)
                dve.wait_ge(cv_ready, b * 2 + 3)
                dve.tensor_copy(kc, bank(6, 2 * NB).rearrange("p (g n) -> p g n", g=2)).then_inc(cv_sb, 1)
                dve.wait_ge(cv_ready, b * 2 + 4)
                dve.tensor_copy(vc[:, 0, :], bank(7)[:, 0:256])
                dve.tensor_copy(vc[0:NB - P, 1, :], bank(7)[0:NB - P, 256:512]).then_inc(cv_sb, 1)
                ub = b * SU

                def soft_unit(a):
                    dve.wait_ge(sc_ready, ub + (NU + a + 1))
                    S = sp3[:, a % 3, :]
                    src = bank(2 + a % 2)
                    dve.wait_ge(ptp_ready, ub + (NU + a - 2))
                    if a in CHUNK and a < 9:
                        k = a - 1
                        step(dve.scalar_tensor_tensor(S, C("spos"), C("srow")[:, k:k + 1], src, ALU.add, ALU.add))
                        m = a_["madd"][:, (k // 4) * 32:(k // 4) * 32 + 32].rearrange("p (o n u) -> p o n u", o=1, u=1)\
                            .broadcast_to([P, 4, 32, 4])
                        S4 = S.rearrange("p (i n u) -> p i n u", i=4, u=4)
                        step(dve.tensor_tensor(S4, S4, m, ALU.add))
                        step(dve.tensor_reduce(a_["mx"][:, a:a + 1], S, AX.X, ALU.max))
                    else:
                        apart(dve)
                        w, m = {0: (NB, C("snegc")), 9: (DT, C("snegn")), 10: (512, C("snegw")), 11: (DT, C("snegn"))}[a]
                        step(dve.tensor_tensor_reduce(out=S[:, 0:w], in0=src[:, 0:w], in1=m[:, 0:w], scale=1.0,
                                                      scalar=-3e38, op0=ALU.add, op1=ALU.max,
                                                      accum_out=a_["mx"][:, a:a + 1]))
                    dve.tensor_tensor(a_["nb"][:, a:a + 1], a_["mx"][:, a:a + 1], nsl, ALU.mult).then_inc(soft, 1)

                def out_unit(a):
                    dve.wait_ge(o_ready, ub + (NU + a + 1))
                    for g in range(KV):
                        ins = dve.tensor_copy(oc[g * 32:(g + 1) * 32, a, :],
                                              bank(6 + a % 2)[g * 32:(g + 1) * 32, g * HD:(g + 1) * HD])
                    ins.then_inc(o_done, 1)

                def top_k():
                    dve.wait_ge(imp_ready, b + 1)
                    pp, ia, ib, m8 = a_["pp"], a_["ia"], a_["ib"], a_["m8"]
                    dve.tensor_copy(pp[:, 1:1 + NB], bank(7, NB)).then_inc(imp_done, 1)
                    dve.wait_ge(imp_done, b + 1)
                    step(dve.tensor_reduce(ia, pp[:, 1:1 + 4 * NSB].rearrange("p (j r) -> p j r", r=4), AX.X, ALU.add))
                    step(dve.tensor_reduce(ib, pp[:, 0:4 * NSB].rearrange("p (j r) -> p j r", r=4), AX.X, ALU.add))
                    step(dve.tensor_tensor(ia, ia, ib, ALU.add))
                    step(dve.memset(ia[:, 0:1], -NEG))
                    step(dve.memset(ia[:, NSB - 2:NSB], -NEG))
                    apart(dve)
                    step(dve.max(m8[:, 0:8], ia))
                    apart(dve)
                    step(dve.match_replace(ib, m8[:, 0:8], ia, NEG))
                    apart(dve)
                    step(dve.max(m8[:, 8:16], ib))
                    apart(dve)
                    step(dve.match_replace(ia, m8[:, 8:16], ib, NEG))
                    step(dve.tensor_scalar(a_["madd"], ia, NEG, NEG, ALU.not_equal, ALU.mult))

                soft_unit(0)
                dve.wait_ge(p_ready, ub + (NU + 1))
                step(dve.reciprocal(a_["tmp"][:, 0:1], a_["ls"][:, 0:1]))
                dve.tensor_scalar(sp3[:, 0, 0:NB], sp3[:, 0, 0:NB], a_["tmp"][:, 0:1], None, ALU.mult).then_inc(p_norm, 1)
                for a in range(1, SU):
                    if a in CHUNK:
                        t_round(rb + (R0 + 32 + 2 * CHUNK[a] + 1), kTc[:, a % 2, 1, :], bank(1))
                    if a == 1:
                        top_k()
                    soft_unit(a)
                    out_unit(a - 1)
                out_unit(SU - 1)
                dve.wait_ge(o_done, ub + (NU + SU))
                seg, wl, coef, tmp = b_["seg"], a_["tmp"], a_["coef"], a_["tmp"]
                for j, (a0, a1) in enumerate(((1, 10), (10, 12))):
                    step(dve.tensor_reduce(seg[:, j:j + 1], a_["mx"][:, a0:a1], AX.X, ALU.max))
                dve.tensor_tensor(seg[:, 2:4], seg[:, 0:2], nsl.broadcast_to([P, 2]), ALU.mult).then_inc(w_ready, 1)
                dve.wait_ge(w_exp, b + 1)
                step(dve.tensor_tensor(tmp[:, 1:12], a_["wts"][:, 1:12], a_["ls"][:, 1:12], ALU.mult))
                for j, (a0, a1) in enumerate(((1, 10), (10, 12))):
                    step(dve.tensor_reduce(seg[:, 4 + j:5 + j], tmp[:, a0:a1], AX.X, ALU.add))
                step(dve.reciprocal(seg[:, 6:8], seg[:, 4:6]))
                step(dve.tensor_tensor(seg[:, 6:8], seg[:, 6:8], gcur[:, 1:3], ALU.mult))
                step(dve.tensor_copy(coef[:, 0:1], gcur[:, 0:1]))
                for j, (a0, a1) in enumerate(((1, 10), (10, 12))):
                    step(dve.tensor_scalar(coef[:, a0:a1], a_["wts"][:, a0:a1], seg[:, 6 + j:7 + j], None, ALU.mult))
                step(dve.tensor_tensor(ocs, oc, coef.rearrange("p (a o) -> p a o", o=1).broadcast_to([P, SU, HD]), ALU.mult))
                step(dve.tensor_reduce(a_["od"][:, 0:HD], ocs.rearrange("p a d -> p d a"), AX.X, ALU.add))
                dve.tensor_copy(a_["od"][:, HD:P], a_["od"][:, 0:HD]).then_inc(od_ready, 1)
                dve.wait_ge(ot_ready, b + 1)
                apart(dve)
                for g2 in range(2):
                    src = bank(4)[g2 * HD:(g2 + 1) * HD, 0:P].rearrange("p (a g h t) -> p a g h t", a=2, g=2, h=HPG)[:, :, g2]
                    ins = dve.tensor_copy(qT[g2 * HD:(g2 + 1) * HD, :, bass.ds(b * DT + TP, DT)]
                                          .rearrange("p (a h) t -> p a h t", a=2), src)
                ins.then_inc(ot_done, 1)
                assert step.n - n_before == STEPS, step.n - n_before
            step.n += (DB - 1) * STEPS
            step.off = 0
            last_sums(4, ALPHA, y_ready, DK)
            norm(4, EPS)
            ffn(3)
            norm(5, 4 * EPS)
            for i, (t0, n) in enumerate(TILES):
                dve.wait_ge(yt_psum, i + 1)
                if i >= 2:
                    dve.wait_ge(y_out[i % 2], 16 * (i // 2))
                dve.tensor_copy(ytok[0:n, i % 2, :], psum[0:n, (i % 4) * 1024:(i % 4 + 1) * 1024]).then_inc(y_tok, 1)

        @block.tensor
        def _(pe):
            def wide(out, lhsT, rhs, start, stop):
                m = lhsT.shape[-1]
                pe.matmul(out[0:m, 0:TP], lhsT, rhs[:, 0:TP], start=start, stop=stop)
                return pe.matmul(out[0:m, TP:T], lhsT, rhs[:, TP:T], start=start, stop=stop)

            def split(out, lhsT, rhs, start, stop):
                for c in range(2):
                    last = pe.matmul(out[:, c], lhsT, rhs[:, c * TH:(c + 1) * TH], start=start, stop=stop)
                return last

            def split3(out, hi, lo, rhs_hi, rhs_lo, start, stop):
                split(out, hi, rhs_hi, start, False)
                split(out, hi, rhs_lo, False, False)
                return split(out, lo, rhs_hi, False, stop)

            def norm_sums(ln):
                pe.wait_ge(sums_ready, ln + 1)
                split(halves(0), C("mean"), stat[:, 0, :], True, True)
                split(halves(1), C("mean"), stat[:, 1, :], True, True).then_inc(stats_done, 1)

            def ffn(f, ln):
                for h in range(2):
                    F0 = f * 2 * FB + h * FB
                    u0 = h * FB
                    c0 = f * FT + h * FH
                    y0 = Y_BASE[ln] + 2 + h * DK

                    def gate_up(j, u, first=False):
                        pe.wait_ge(lo_ready, j + (F0 + 1))
                        if not isinstance(j, int) or j >= 2 or h + f > 0:
                            pe.wait_ge(gu_free, j + (c0 + 1))
                        if h == 1 and u > 0:
                            pe.wait_ge(y_sum, y0)
                        hi, lo = [w_sp[:, (u0 + u) % 2, d, :].rearrange("p (k c n) -> p k c n", k=DK, c=2)
                                  for d in range(2)]
                        s = u % 2
                        for k, c in [(k, c) for k in range(DK) for c in range(2)] if first else \
                                [(k, c) for c in range(2) for k in range(DK)]:
                            if first and c == 0 and ln > 0:
                                pe.wait_ge(x_ready, DK * (ln - 1) + k + 1)
                            last = split3(halves(2 * s + c), hi[:, k, c, :], lo[:, k, c, :], x_hi[:, k, :], x_lo[:, k, :],
                                          k == 0, k == DK - 1)
                        last.then_inc(blk_done, 1)

                    def gate_up_half():
                        j = FH - 1
                        pe.wait_ge(lo_ready, F0 + j + 1)
                        pe.wait_ge(gu_free, c0 + j + 1)
                        hi, lo = [w_sp[:, (u0 + j) % 2, d, 0:2 * DK * FL].rearrange("p (k n) -> p k n", k=DK)
                                  for d in range(2)]
                        for k in range(DK):
                            last = split3(halves(2 * (j % 2)), hi[:, k, :], lo[:, k, :], x_hi[:, k, :], x_lo[:, k, :],
                                          k == 0, k == DK - 1)
                        last.then_inc(blk_done, 1)

                    def down(m, u):
                        pe.wait_ge(lo_ready, m + (F0 + FH + 1))
                        pe.wait_ge(gu_free, c0 + FH + 1)
                        pe.wait_ge(y_sum, m + (y0 - 1))
                        hi, lo = [w_sp[:, (u0 + FH + u) % 2, d, 0:FW].rearrange("p (k n) -> p k n", n=P) for d in range(2)]
                        for k in range(FH):
                            n = P if h == 0 or k < FH - 1 else FL
                            if k == FH - 1:
                                pe.wait_ge(h_ready, c0 + FH + 1)
                            last = split3(halves(2 + u % 2), hi[0:n, k, :], lo[0:n, k, :], h_hi[0:n, k, :], h_lo[0:n, k, :],
                                          k == 0, k == FH - 1)
                        last.then_inc(blk_done, 1)

                    gate_up(0, 0, first=h == 0)
                    with pe.Fori(0, 2) as i:
                        for u in range(1, 1 + RING):
                            gate_up(i * RING + u, u)
                    for j in range(1 + 2 * RING, FH):
                        if h == 1 and j == FH - 1:
                            gate_up_half()
                        else:
                            gate_up(j, j)
                    pe.wait_ge(h_ready, c0 + FH)
                    with pe.Fori(0, DK // 2) as i:
                        for u in range(2):
                            down(i * 2 + u, u)
                norm_sums(ln)

            def out_projection(ln, n0, src):
                for i in range(4):
                    n = n0 + i
                    v = ring[:, n % RING, :].rearrange("p (k n) -> p k n", k=DK)
                    pe.wait_ge(ring_full[n % RING], full_at(n))
                    for c in range(2):
                        m = 2 * i + c
                        pe.wait_ge(y_sum, Y_BASE[ln] + m + 1)
                        for k in range(DK):
                            last = split(halves(2 + c), v[:, k, c * P:(c + 1) * P], src[:, k, :], k == 0, k == DK - 1)
                        last.then_inc(y_ready, 1)
                    pe.wait_ge(y_ready, MIX.index(ln) * DK + m + 1)
                    pe.sem_inc(blk_done, 1)
                norm_sums(ln)

            pe.wait_ge(consts_in, 48)
            pe.wait_ge(x_in, 16 * len(TILES))
            for k in range(DK):
                if k >= 4:
                    pe.wait_ge(xt_sb, k - 3)
                for i, (t0, n) in enumerate(TILES):
                    last = pe.transpose(psum[:, (k % 4) * 1024 + t0:(k % 4) * 1024 + t0 + n],
                                        xl[0:n, i, k * P:(k + 1) * P], ident[0:n, 0:n])
                last.then_inc(xt_psum, 1)
            pe.wait_ge(xt_first, DK)

            ffn(0, 0)

            n0 = blk_pos["even"]
            pe.wait_ge(x_ready, DK)
            for i in range(4):
                s = (n0 + i) % RING
                v = ring[:, s, :].rearrange("p (k n) -> p k n", k=DK)
                pe.wait_ge(ring_full[s], full_at(n0 + i))
                for c in range(2):
                    z = 2 * i + c
                    if z >= 4:
                        pe.wait_ge(z_freeD, z - 3)
                    for k in range(DK):
                        if z < 4:
                            last = wide(pair(z % 4), v[:, k, c * P:(c + 1) * P], yT[:, k, :], k == 0, k == DK - 1)
                        else:
                            last = split(halves(z % 4), v[:, k, c * P:(c + 1) * P], yT[:, k, :], k == 0, k == DK - 1)
                    last.then_inc(z_ready, 1)
                pe.wait_ge(z_ready, z + 1)
                pe.sem_inc(blk_done, 1)
            pe.wait_ge(loc_in, 7 * 16)
            pe.wait_ge(z_freeA, 1)
            for h in range(NG):
                last = pe.transpose(bank(0)[:, h * P:(h + 1) * P], gms[:, h, :], ident)
            last.then_inc(z_ready, 1)
            pe.wait_ge(z_freeA, 2)
            for g in range(NG):
                last = pe.transpose(bank(2)[:, g * DB * PAST:(g + 1) * DB * PAST], past[0:DB * PAST, g * P:(g + 1) * P],
                                    ident[0:DB * PAST, 0:DB * PAST])
            last.then_inc(z_ready, 1)
            pe.wait_ge(z_freeA, 3)
            pe.wait_ge(z_freeD, 5)
            for h in range(NG):
                last = pe.matmul(bank(4)[0:TS, h * TS:(h + 1) * TS], C("rep")[0:DT, :],
                                 wsT[0:DT, h:h + 1, 0:DT].broadcast_to([DT, DB, DT]), start=True, stop=True)
            last.then_inc(z_ready, 1)
            pe.wait_ge(z_freeA, 4)
            for g in range(NG):
                pe.transpose(bank(6)[0:PAST, g * P:(g + 1) * P], ext[:, g, TP:TP + PAST], ident)
                last = pe.transpose(bank(7)[0:TS, g * P:(g + 1) * P], pnew[:, g, :], ident)
            last.then_inc(z_ready, 1)
            for c in range(2):
                pe.wait_ge(ring_full[(n0 + 4 + c) % RING], full_at(n0 + 4 + c))
            for i, (t0, n) in enumerate(TILES):
                pe.wait_ge(z_freeD, 5 + i)
                for c in range(2):
                    v = ring[:, (n0 + 4 + c) % RING, :].rearrange("p (k n) -> p k n", k=DK)
                    for k in range(DK):
                        last = pe.matmul(bank(2 * (i % 4))[0:n, c * 256:(c + 1) * 256], yT[:, k, t0:t0 + n],
                                         v[:, k, :], start=k == 0, stop=k == DK - 1)
                last.then_inc(z_ready, 1)
            pe.wait_ge(z_ready, 17)
            pe.sem_inc(blk_done, 2)
            for h in range(NG):
                s = (h + 1) % 4
                pe.wait_ge(z_freeD, 13)
                for c in range(TT):
                    pe.matmul(psum[:, s * 1024 + c * P:s * 1024 + (c + 1) * P], vtok[:, c, h * P:(h + 1) * P],
                              wsT[:, h, :], start=True, stop=True)
                pe.matmul(psum[:, s * 1024 + TP:s * 1024 + T], vtok[0:TS, TT, h * P:(h + 1) * P],
                          wsB[0:TS, h, :], start=True, stop=True).then_inc(z_ready, 1)
            for g in range(NG):
                pe.wait_ge(z_freeD, 14 + g)
                pe.wait_ge(e_dif, g + 1)
                split(halves((g + 1) % 4), plw[:, g, :], dif[:, g, :], True, True).then_inc(z_ready, 1)
            pe.wait_ge(z_freeD, 17)
            pe.wait_ge(z_freeA, 8)
            out_projection(1, n0 + 6, cat)

            ffn(1, 2)
            ffn(2, 3)

            n0 = blk_pos["odd"]
            pe.wait_ge(x_ready, 4 * DK)
            for i in range(4):
                n = n0 + i
                v = ring[:, n % RING, :].rearrange("p (k h n) -> p k h n", k=DK, h=2)
                pe.wait_ge(ring_full[n % RING], full_at(n))
                for h in range(2):
                    z = 2 * i + h
                    if z >= 4:
                        pe.wait_ge(q_free, z - 3)
                    for k in range(DK):
                        last = split(halves(z % 4), v[:, k, h, :], yT[:, k, :], k == 0, k == DK - 1)
                    last.then_inc(q_ready, 1)
                pe.wait_ge(q_ready, z + 1)
                pe.sem_inc(blk_done, 1)
            pe.wait_ge(q_free, 8)
            for c in range(6):
                n = n0 + 4 + c
                v = ring[:, n % RING, :].rearrange("p (k n) -> p k n", k=DK)
                pe.wait_ge(ring_full[n % RING], full_at(n))
                o0 = (c % 2) * 3
                if c >= 2:
                    pe.wait_ge(kv_sb, c - 1)
                for i, (t0, m) in enumerate(TILES):
                    for k in range(DK):
                        last = pe.matmul(psum[0:m, o0 * 512 + i * 256:o0 * 512 + (i + 1) * 256], yT[:, k, t0:t0 + m],
                                         v[:, k, :], start=k == 0, stop=k == DK - 1)
                last.then_inc(kv_ready, 1)
                if c in (2, 4):
                    for gp in range(2):
                        z = 8 + (c - 2) + gp
                        pe.wait_ge(q_free, z)
                        for k in range(DK):
                            last = split(halves(3), v[:, k, gp * P:(gp + 1) * P], yT[:, k, :], k == 0, k == DK - 1)
                        last.then_inc(q_ready, 1)
                    pe.wait_ge(q_ready, z + 1)
                pe.wait_ge(kv_ready, c + 1)
                pe.sem_inc(blk_done, 1)
            n = n0 + 10
            v = ring[:, n % RING, 0:DK * 48].rearrange("p (k n) -> p k n", k=DK)
            pe.wait_ge(ring_full[n % RING], full_at(n))
            pe.wait_ge(kv_sb, 5)
            for i, (t0, m) in enumerate(TILES):
                for k in range(DK):
                    last = pe.matmul(bank(0)[0:m, i * 48:(i + 1) * 48], yT[:, k, t0:t0 + m], v[:, k, :],
                                     start=k == 0, stop=k == DK - 1)
            last.then_inc(q_ready, 1)
            pe.wait_ge(q_ready, 13)
            pe.sem_inc(blk_done, 1)
            pe.sem_inc(cmp_free, 2)
            pe.sem_inc(slc_free, 3)
            pe.sem_inc(gre_free, 2)

            pe.wait_ge(n_in, 9 * 16)
            pe.wait_ge(q_free, 12)
            for k in range(2):
                for j in range(16):
                    last = pe.matmul(bank(7)[:, k:k + 1], w1c[:, k, j // 8, j % 8, :], a_["peT"][:, k * 16 + j:k * 16 + j + 1],
                                     start=j == 0, stop=j == 15)
            last.then_inc(hb_ready, 1)

            def t_round(n, even, tiles):
                pe.wait_ge(t_act if even else t_dve, n)
                for out, src in tiles:
                    last = pe.transpose(out, src, ident[0:src.shape[0], 0:src.shape[0]])
                return last.then_inc(t_ready, 1)

            def xtc_round(n, even, slot, v, kt, rows):
                bk = bank(0 if even else 1)
                t_round(n, even, [(bk[:, g * rows:(g + 1) * rows], gre[0:rows, slot, v, g, kt * P:(kt + 1) * P])
                                  for g in range(KV)])

            pe.wait_ge(q_free, 13)
            pe.wait_ge(kv_sb, 6)
            for st in range(9):
                q, kt = st // 2, st % 2
                if st < 8:
                    pe.wait_ge(cmp_free, q + 3)
                    for v in range(2):
                        xtc_round(st, v == 0, q % 2, v, kt, TP // CS)
                    if kt == 1:
                        pe.wait_ge(t_ready, 2 * st + 2)
                        pe.sem_inc(gre_free, 1)
                if st > 0:
                    pe.wait_ge(t_act, st)
                    pe.wait_ge(t_dve, st)
                    for v in range(2):
                        for r in range(2):
                            last = pe.matmul(bank(2 + v, KV * NBP), w1c[:, v, r, st - 1, :],
                                             xTc[:, (st - 1) % 2, v, :, r:r + NBP], start=st == 1 and r == 0,
                                             stop=st == 8 and r == 1)
                    last.then_inc(hid_step, 1)
            pe.wait_ge(gel_ready, 2)
            pe.wait_ge(hb_sb, 1)
            pe.wait_ge(zeroed, 2)
            for gp in range(2):
                for g2 in range(2):
                    last = pe.matmul(bank(6)[:, gp * NBP:(gp + 1) * NBP], w2k[:, g2, :], gel[:, 0, 2 * gp + g2, 0:NBP],
                                     start=g2 == 0, stop=g2 == 1)
            last.then_inc(cv_ready, 1)
            for g in range(KV):
                last = pe.matmul(bank(7)[0:NBP, g * HD:(g + 1) * HD], gel[:, 1, g, 0:NBP], w2v, start=True, stop=True)
            last.then_inc(cv_ready, 1)

            pe.wait_ge(cv_sb, 2)

            def prompt_scores(n):
                kind, i, r, gp, h, g2 = UNITS[n]
                if n >= 2:
                    pe.wait_ge(soft, n - 1)
                if kind == "cmp":
                    for a in range(2):
                        for hh in range(HPG):
                            last = pe.matmul(bank(2 + n % 2)[:, (a * HPG + hh) * 64:(a * HPG + hh + 1) * 64],
                                             qT[:, a * HPG + hh, i * P:(i + 1) * P], kcb[:, a, :], start=True, stop=True)
                else:
                    rows = slice(g2 * HD, (g2 + 1) * HD)
                    last = pe.matmul(bank(2 + n % 2, (i + 1) * P), qT[rows, gp * HPG + h, i * P:(i + 1) * P],
                                     kT[rows, r, gp, 0:(i + 1) * P], start=True, stop=True)
                last.then_inc(sc_ready, 1)

            prompt_scores(0)
            for n, (kind, i, r, gp, h, g2) in enumerate(UNITS):
                pe.wait_ge(p_norm if kind == "cmp" else p_ready, i + 1 if kind == "cmp" else n + 1)
                if n >= 2:
                    pe.wait_ge(pt_sb, n - 1)
                nk = 4 if kind == "cmp" else i + 1
                for j in range(nk):
                    last = pe.transpose(bank(4 + n % 2)[:, j * P:(j + 1) * P], sp3[:, n % 3, j * P:(j + 1) * P], ident)
                last.then_inc(ptp_ready, 1)
                if n + 1 < NU:
                    prompt_scores(n + 1)
                pe.wait_ge(pt_sb, n + 1)
                if n >= 1:
                    pe.wait_ge(o_done, n if kind == "cmp" or UNITS[n - 1][0] == "cmp" else n - 1)
                for j in range(nk):
                    pt = pts[:, n % 2, j * P:(j + 1) * P]
                    if kind == "cmp":
                        last = pe.matmul(bank(6 + j // 2)[:, (j % 2) * 256:(j % 2 + 1) * 256], pt, vcb[:, j // 2, :],
                                         start=True, stop=True)
                    else:
                        g = 2 * gp + g2
                        last = pe.matmul(bank(6 + n % 2, HD), pt, vtk[:, r, j, g * HD:(g + 1) * HD],
                                         start=j == 0, stop=j == nk - 1)
                last.then_inc(o_ready, 1)
                if n + 1 == NU or UNITS[n + 1][0] == "cmp":
                    pe.wait_ge(o_done, n + 1)
                    for a in range(2):
                        t_round(8 + i, a == 0, [(bank(a)[:, hh * P:(hh + 1) * P],
                                                 otok[:, i % 2, (a * HPG + hh) * P:(a * HPG + hh + 1) * P])
                                                for hh in range(HPG)])

            with pe.Fori(0, DB) as b:
                hb_ = b * (SR // 2)
                ub = b * SU

                def products(st, j):
                    v, gp = j // 2, j % 2
                    for r in range(2):
                        last = pe.matmul(bank(2 + j, 2 * NB), w1c[:, v, r, st, :],
                                         xTc[:, st % 2, v, 2 * gp:2 * gp + 2, r:r + NB], start=st == 0 and r == 0,
                                         stop=st == 7 and r == 1)
                    return last

                for st in range(9):
                    q, kt = st // 2, st % 2
                    if st > 0:
                        pe.wait_ge(t_act, hb_ + (R0 // 2 + 2 * st))
                        pe.wait_ge(t_dve, hb_ + (R0 // 2 + 2 * st))
                    if st == 1:
                        pe.wait_ge(pt_sb, ub + NU)
                        pe.wait_ge(ot_done, b + 1)
                    if st < 8 and kt == 0:
                        pe.wait_ge(cmp_free, b * 8 + (4 + 2 * q + 2 + 2))
                    for j in range(4):
                        if st > 0:
                            last = products(st - 1, j)
                        if st < 8:
                            v, half = j // 2, j % 2
                            xtc_round(hb_ + (R0 // 2 + 2 * st + v), half == 0, half, v, kt, P)
                    if st > 0:
                        last.then_inc(hid_step, 1)
                    if st < 8 and kt == 1:
                        pe.wait_ge(t_ready, b * SR + (R0 + 4 * st + 4))
                        pe.sem_inc(gre_free, 2)
                pe.wait_ge(gel_ready, b * 4 + 6)
                pe.wait_ge(o_done, ub + NU)
                for gp in range(2):
                    for g2 in range(2):
                        last = pe.matmul(bank(6)[:, gp * NB:(gp + 1) * NB], w2k[:, g2, :], gel[:, 0, 2 * gp + g2, 0:NB],
                                         start=g2 == 0, stop=g2 == 1)
                last.then_inc(cv_ready, 1)
                for i, m in enumerate((P, NB - P)):
                    for g in range(KV):
                        last = pe.matmul(bank(7)[0:m, i * 256 + g * HD:i * 256 + (g + 1) * HD],
                                         gel[:, 1, g, i * P:i * P + m], w2v, start=True, stop=True)
                last.then_inc(cv_ready, 1)

                def keys(a):
                    k = CHUNK[a]
                    if k == 8:
                        pe.wait_ge(win_full, b * 16 + 16)
                    else:
                        pe.wait_ge(slc_full[k % 3], b * (32 if k % 3 == 2 else 48) + 16 * (k // 3 + 1))
                    for gp in range(2):
                        t_round(hb_ + (R0 // 2 + 16 + k), gp == 0,
                                [(bank(gp)[:, p * P:(p + 1) * P],
                                  ring[:, 1 + k % 3, p * ROW + gp * P:p * ROW + (gp + 1) * P]) for p in range(4)])

                def scores(a):
                    if a > 1:
                        pe.wait_ge(soft, ub + (NU + a - 1))
                    out = bank(2 + a % 2)
                    for gp in range(2):
                        if a == 0:
                            w, rhs = NB, kc[:, gp, :]
                        elif a in CHUNK:
                            w, rhs = 512, kTc[:, a % 2, gp, :]
                            if gp == 0:
                                pe.wait_ge(t_act, hb_ + (R0 // 2 + 16 + CHUNK[a] + 1))
                                pe.wait_ge(t_dve, hb_ + (R0 // 2 + 16 + CHUNK[a] + 1))
                        else:
                            w, rhs = DT, kT[:, 0 if a == 9 else 1, gp, bass.ds(b * DT + TP, DT)]
                        last = pe.matmul(out[:, 0:w], qb[:, gp, :], rhs, start=gp == 0, stop=gp == 1)
                    last.then_inc(sc_ready, 1)

                pe.wait_ge(cv_sb, b * 2 + 4)
                pe.wait_ge(q_set, b * 4 + 4)
                scores(0)
                for a in range(SU):
                    if a + 1 in CHUNK:
                        keys(a + 1)
                    pe.wait_ge(p_norm if a == 0 else p_ready, b + (TT + 1) if a == 0 else ub + (NU + a + 1))
                    if a == 0:
                        pe.matmul(bank(7, NB), C("hsum"), sp3[:, 0, 0:NB], start=True, stop=True).then_inc(imp_ready, 1)
                    pe.wait_ge(pt_sb, ub + (NU + a - 1))
                    S = sp3[:, a % 3, :]
                    if a == 0:
                        parts = [(P, 0, P), (NB - P, P, NB - P)]
                    elif a in CHUNK:
                        parts = [(P, p * P, P) for p in range(4)]
                    else:
                        parts = [(DT, 0, DT)]
                    for j, (m, c0, w) in enumerate(parts):
                        last = pe.transpose(bank(4 + a % 2)[0:m, j * P:(j + 1) * P], S[:, c0:c0 + w], ident)
                    last.then_inc(ptp_ready, 1)
                    if a + 1 < SU:
                        scores(a + 1)
                    pe.wait_ge(pt_sb, ub + (NU + a + 1))
                    pe.wait_ge(o_done, ub + (NU + a - 1))
                    if a == 1:
                        pe.wait_ge(imp_done, b + 1)
                    if a == 9:
                        pe.wait_ge(vn_full, b * 32 + 32)
                    for j, (m, c0, w) in enumerate(parts):
                        if a == 0:
                            rhs = vc[0:m, j, :]
                        elif a in CHUNK:
                            rhs = ring[:, 1 + CHUNK[a] % 3, j * ROW + 256:j * ROW + 512]
                        else:
                            rhs = vnew[0:DT, 0 if a == 9 else 1, :]
                        last = pe.matmul(bank(6 + a % 2, 256), pts[0:m, a % 2, j * P:(j + 1) * P], rhs,
                                         start=j == 0, stop=j == len(parts) - 1)
                    last.then_inc(o_ready, 1)
                    if a in CHUNK:
                        pe.wait_ge(o_ready, ub + (NU + a + 1))
                        pe.sem_inc(slc_free, 1)
                pe.wait_ge(od_ready, b + 1)
                pe.wait_ge(pt_sb, ub + (NU + SU))
                pe.transpose(bank(4, P), a_["od"], ident).then_inc(ot_ready, 1)

            pe.wait_ge(ot_done, DB + 1)
            pe.wait_ge(o_done, NU + DB * SU)
            out_projection(4, n0 + 11, qT)
            ffn(3, 5)
            pe.wait_ge(x_ready, 6 * DK)
            for i, (t0, n) in enumerate(TILES):
                if i >= 4:
                    pe.wait_ge(y_tok, i - 3)
                for k in range(DK):
                    last = pe.transpose(psum[0:n, (i % 4) * 1024 + k * P:(i % 4) * 1024 + (k + 1) * P],
                                        yT[:, k, t0:t0 + n], ident)
                last.then_inc(yt_psum, 1)


_INS = ["x_prompt", "x_sample", "state_l0_pool", "cache_l1_cmp_kv", "cache_l1_slc_kv", "cache_l1_win_kv", "page_table",
        "w_ffn_in", "w_ffn_out", "ln_g", "ln_b", "w_in_even", "pool_w", "pool_scale", "gm_ln_g", "gm_ln_b", "gm_ws",
        "gm_b", "w_out_even", "w_in_odd", "cmp_pe", "cmp_w1", "cmp_b1", "cmp_w2", "w_out_odd"]
_OUTS = [(1, TP, DM), (DB, DT, DM), (1, PAST, PW), (DB, PAST, PW), (DB, DT, PW),
         (1, TP, 2, KV, HD), (1, TP, 2, KV, HD), (1, WIN, 2, KV, HD),
         (DB, DT, 2, KV, HD), (DB, DT, 2, KV, HD), (DB, WIN, 2, KV, HD)]


def kernel(**inputs):
    import concourse.bacc as _bacc
    from concourse.bass_utils import run_bass_kernel_spmd as _run

    nc = _bacc.Bacc("TRN2", target_bir_lowering=False, num_devices=1)
    arrays, args = {}, []
    for name in _INS:
        a = np.ascontiguousarray(inputs[name])
        arrays[f"in_{name}"] = a
        args.append(nc.dram_tensor(f"in_{name}", a.shape, mybir.dt.from_np(a.dtype), kind="ExternalInput").ap())
    where, table = constants()
    arrays["shape_tables"] = table
    tables = nc.dram_tensor("shape_tables", table.shape, F32, kind="ExternalInput").ap()
    outs = [nc.dram_tensor(f"out_{i}", shape, F32, kind="ExternalOutput").ap() for i, shape in enumerate(_OUTS)]
    bass_hybrid_trunk_step(nc, args, where, tables, outs)
    r = _run(nc, [arrays], core_ids=[0])
    return tuple(r.results[0][f"out_{i}"] for i in range(len(_OUTS)))
```

```python
from contextlib import ExitStack

import numpy as np

import concourse.bass as bass
from concourse import mybir

F32 = mybir.dt.float32
F32R = mybir.dt.float32r
I32 = mybir.dt.int32
ACT = mybir.ActivationFunctionType
ALU = mybir.AluOpType
AX = mybir.AxisListType

P = 128
DM = 1024
DK = DM // P
TP, DB, DT = 512, 8, 8
TS = DB * DT
T = TP + TS
TT = TP // P
TH = T // 2
TILES = [(i * P, P) for i in range(TT)] + [(TP, TS)]
FF = 2752
FT = -(-FF // P)
FL = FF - (FT - 1) * P
FH = FT // 2
FB = FH + DK
FW = FH * P
ALPHA = 4 ** 0.25
EPS = 1e-5
PW, NG = 512, 4
PAST = 15
EXT = PAST + TP + DB * (PAST + DT)
NH, KV, HPG, HD = 16, 4, 4, 64
HID = 128
PL = 4096
PAGE = 128
CS = 16
NCH = PL // CS
NB = NCH - 1
NBP = TP // CS - 1
NSB = PL // 64 + 1
WIN = 512
NEG = -1e30
STEPS = 41
RING = 4
RB = 2048
ROW = 2 * KV * HD
NLN = 6
ODD_SPLIT = 10
SP_BASE = [0, 2 * FB, 4 * FB, 6 * FB + ODD_SPLIT]
LN_OF = [0, 2, 3, 5]
MIX = [1, 4]
Y_BASE = [0, 16, 24, 40, 56, 64]
X_BASE = {1: 8, 2: 16, 3: 24, 4: 32}


def slope(head):
    return 2.0 ** (-8.0 * (head + 1) / NH)


def constants():
    parts = {}
    p = np.arange(P)[:, None]
    parts["ident"] = np.eye(P)
    parts["mean"] = np.full((P, P), 1.0 / DM)
    parts["tri"] = (p <= np.arange(P)[None, :]) * 1.0
    rep = np.zeros((P, TS))
    rep[:DT] = np.tile(np.eye(DT), (1, DB))
    parts["rep"] = rep
    bd = np.zeros((P, TS))
    bd[:TS] = np.kron(np.eye(DB), np.ones((DT, DT)))
    parts["bdiag"] = bd
    parts["rcnt"] = np.tile(np.concatenate([1.0 / np.minimum(w, np.arange(16) + 1) for w in (2, 4, 8, 16)])[None], (P, 1))
    g, t = np.arange(P) // 32, np.arange(P) % 8
    parts["hsum"] = ((g[:, None] == g[None]) & (t[:, None] == t[None])) * 1.0
    d = p + (TP - P) - np.arange(TP)[None]
    parts["negd"] = np.where(d >= 0, -d, NEG)
    n = np.arange(32)[None]
    cmp = []
    for i in range(TT):
        d = p + i * P - (n * CS + 2 * CS - 1)
        cmp.append(np.where((d >= 0) & (n < NBP), -d, NEG))
    parts["negdc"] = np.concatenate(cmp, 1)
    tp = PL + t[:, None]
    n = np.arange(NB + 1)[None]
    d = tp - (n * CS + 2 * CS - 1)
    parts["snegc"] = np.where(d >= 0, -d, NEG)
    q = np.arange(512)[None]
    parts["spos"] = (q % P) * CS + q // P + 0.0 * p
    parts["srow"] = np.stack([-(tp[:, 0]) + h * 2048 for h in range(2)], 1)
    parts["spiece"] = np.tile(4.0 * np.arange(4)[None], (P, 2))
    j, i = q // P, q % P
    kp = PL - WIN + 4 * i + j
    d = tp - kp
    parts["snegw"] = np.where((d >= 0) & (d < WIN), -d, NEG)
    d = t[:, None] - np.arange(DT)[None]
    parts["snegn"] = np.where(d >= 0, -d, NEG)
    sl = slope(np.arange(P) // 8)
    parts["sslope"] = np.stack([sl, -sl], 1)
    gp, h = np.arange(8)[None] // 4, np.arange(8)[None] % 4
    parts["qscale"] = HD ** -0.5 / slope((2 * gp + p // 64) * 4 + h)
    u = np.arange(NH)
    parts["uslope"] = np.tile(slope((u // 8 * 2 + u % 2) * 4 + u // 2 % 4)[None], (P, 1))
    parts["rowpg"] = (p % 8) * 4.0 + np.arange(4)[None]
    at, where, cols = 0, {}, []
    for k, v in parts.items():
        v = np.broadcast_to(v, (P, v.shape[1])).astype(np.float32)
        where[k] = (at, v.shape[1])
        cols.append(v)
        at += v.shape[1]
    return where, np.ascontiguousarray(np.concatenate(cols, 1))


class Chain:

    def __init__(self, eng, sem):
        self.eng, self.sem, self.n, self.off = eng, sem, 0, 0

    def __call__(self, ins):
        self.n += 1
        ins.then_inc(self.sem, 1)
        self.eng.wait_ge(self.sem, self.n + self.off)


def bass_hybrid_trunk_step(nc, a, consts, cdram, outs):
    (x_prompt, x_sample, state_pool, cache_cmp, cache_slc, cache_win, page_table, w_ffn_in, w_ffn_out, ln_g, ln_b,
     w_in_even, pool_w, pool_scale, gm_ln_g, gm_ln_b, gm_ws, gm_b, w_out_even,
     w_in_odd, cmp_pe, cmp_w1, cmp_b1, cmp_w2, w_out_odd) = a
    (y_p, y_s, pool_p, pool_s, gmv_s, cmp_p, slc_p, win_p, cmp_s, slc_s, win_s) = outs
    ctx = ExitStack()
    ctx.enter_context(nc.allow_non_contiguous_dma(reason="small transposed vectors"))
    with ctx:
        at = [-(-nc.sbuf_base // 32) * 32]
        first_byte = {}

        def sb(name, shape, dt=F32, over=None, skip=0):
            size = 4 * int(np.prod(shape[1:]))
            if over is None:
                first_byte[name] = at[0]
                at[0] += -(-size // 32) * 32
            else:
                first_byte[name] = first_byte[over] + 4 * skip
            return nc.alloc_sbuf_tensor_at(name, shape, dt, offset=first_byte[name])

        def sem(name):
            return ctx.enter_context(nc.semaphore(name))

        CN = cdram.shape[1]
        cst = sb("cst", [P, CN])

        def C(name):
            o, w = consts[name]
            return cst[:, o:o + w]

        yT = sb("yT", [P, DK, T])
        x_room = sb("x_room", [P, 2 * DK * T])
        x_hi = sb("x_hi", [P, DK, T], F32R, over="x_room")
        x_lo = sb("x_lo", [P, DK, T], F32R, over="x_room", skip=DK * T)
        big = sb("big", [P, 2 * FH * T])
        h_hi = sb("h_hi", [P, FH, T], F32R, over="big")
        h_lo = sb("h_lo", [P, FH, T], F32R, over="big", skip=FH * T)
        ring = sb("ring", [P, RING, RB])
        w_room = sb("w_room", [P, 4 * RB])
        w_sp = sb("w_sp", [P, 2, 2, RB], F32R, over="w_room")
        act_tmp = sb("act_tmp", [P, 2, T])
        stat = sb("stat", [P, 3, T])
        tmp3 = [act_tmp[:, 0, :], act_tmp[:, 1, :], stat[:, 2, :]]
        lng = sb("lng", [P, NLN, DK])
        lnb = sb("lnb", [P, NLN, DK])
        psum = ctx.enter_context(nc.psum_tensor("psum", [P, 4096], F32))
        ident = C("ident")

        def pair(z):
            return psum[:, z * 1024:z * 1024 + T]

        def halves(z):
            return psum[:, z * 1024:(z + 1) * 1024].rearrange("p (c n) -> p c n", c=2)[:, :, 0:TH]

        def hv(x):
            if len(x.shape) == 3:
                return x.rearrange("p o (c n) -> p (o c) n", c=2)
            return x.rearrange("p (c n) -> p c n", c=2)

        def bank(z, n=512):
            return psum[:, z * 512:z * 512 + n]

        ident_in = sem("ident_in")
        consts_in = sem("consts_in")
        ln_in = sem("ln_in")
        x_in = sem("x_in")
        ring_full = [sem(f"ring_full{s}") for s in range(RING)]
        blk_done = sem("blk_done")
        hi_ready = sem("hi_ready")
        lo_ready = sem("lo_ready")
        xt_psum = sem("xt_psum")
        xt_sb = sem("xt_sb")
        xt_first = sem("xt_first")
        silu_ready = sem("silu_ready")
        gu_free = sem("gu_free")
        h_ready = sem("h_ready")
        y_ready = sem("y_ready")
        y_sum = sem("y_sum")
        sq_ready = sem("sq_ready")
        sq_used = sem("sq_used")
        sums_ready = sem("sums_ready")
        stats_done = sem("stats_done")
        centred = sem("centred")
        mean_ready = sem("mean_ready")
        var_ready = sem("var_ready")
        std_ready = sem("std_ready")
        norm_ready = sem("norm_ready")
        x_full = sem("x_full")
        x_ready = sem("x_ready")
        dve_chain = sem("dve_chain")
        out_done = sem("out_done")
        gmv_out = sem("gmv_out")

        loc_in = sem("loc_in")
        z_ready = sem("z_ready")
        z_freeA = sem("z_freeA")
        z_freeD = sem("z_freeD")
        e_dif = sem("e_dif")
        v_var = sem("v_var")
        v_std = sem("v_std")

        blk_pos = {}
        nblk = 0
        for name, n in [("f0", 2 * FB), ("even", 10), ("f1", 2 * FB), ("f2", 2 * FB), ("odd", 15), ("f3", 2 * FB)]:
            blk_pos[name] = nblk
            nblk += n

        passed = sem("passed")

        def apart(eng):
            eng.sem_inc(passed, 1)

        def full_at(n):
            return 64 * (n // RING + 1)

        ext = big[:, 0:NG * EXT].rearrange("p (g n) -> p g n", g=NG)
        exs = ext[:, :, PAST + TP:].rearrange("p g (b s) -> p g b s", b=DB)
        o = NG * EXT
        uT = big[:, o:o + NG * T].rearrange("p (g n) -> p g n", g=NG)
        o += NG * T
        vtok = big[:, o:o + 5 * PW].rearrange("p (i n) -> p i n", i=5)
        o += 5 * PW
        cat = big[:, o:o + DK * T].rearrange("p (k n) -> p k n", k=DK)
        assert o + DK * T <= FT * T
        loc = x_room
        lo = [0]

        def carve(n):
            lo[0] += n
            assert lo[0] <= 2 * DK * T, lo
            return loc[:, lo[0] - n:lo[0]]
        gms = carve(NG * P).rearrange("p (h s) -> p h s", h=NG)
        wsT = carve(NG * P).rearrange("p (h t) -> p h t", h=NG)
        wsB = carve(NG * TS).rearrange("p (h t) -> p h t", h=NG)
        gmb = carve(NG * P).rearrange("p (h t) -> p h t", h=NG)
        plw = carve(NG * P).rearrange("p (g d) -> p g d", g=NG)
        psc = carve(NG)
        pnew = carve(NG * TS).rearrange("p (g n) -> p g n", g=NG)
        lgg = carve(PW)
        lgb = carve(PW)
        past = carve(PW)
        bns = carve(5 * 6).rearrange("p (i n) -> p i n", i=5)
        mv = carve(5 * 4).rearrange("p (i n) -> p i n", i=5)
        prow_p = carve(PW)
        prow_s = carve(PW)
        sums = carve(2 * EXT).rearrange("p (i n) -> p i n", i=2)
        dif = carve(NG * T).rearrange("p (g n) -> p g n", g=NG)
        xl = big[:, 0:5 * DM].rearrange("p (i n) -> p i n", i=5)

        def cut(region, sizes):
            at, out = 0, {}
            for k, n in sizes:
                out[k] = region[:, at:at + n]
                at += n
            assert at <= region.shape[1], (at, region.shape)
            return out
        b_ = cut(big, [("qT", 8 * T), ("kT", 4 * T), ("vtk", 2 * TT * 256), ("gates", 5 * 48), ("vnew", 512),
                       ("kTc", 2048), ("qb", 256), ("gr", 3 * DB), ("gcur", 4), ("seg", 16)])
        qT = b_["qT"].rearrange("p (i n) -> p i n", i=8)
        kT = b_["kT"].rearrange("p (r g n) -> p r g n", r=2, g=2)
        vtk = b_["vtk"].rearrange("p (r i n) -> p r i n", r=2, i=TT)
        gates = b_["gates"].rearrange("p (i n) -> p i n", i=5)
        vnew = b_["vnew"].rearrange("p (r n) -> p r n", r=2)
        kTc = b_["kTc"].rearrange("p (u g n) -> p u g n", u=2, g=2)
        qb = b_["qb"].rearrange("p (g n) -> p g n", g=2)
        gr = b_["gr"].rearrange("p (b r) -> p b r", b=DB)
        gcur = b_["gcur"]
        y_ = cut(x_room[:, 0:4608], [("oG", 2048), ("sp", 1536), ("free", 512), ("vc", 512)])
        xTc = x_room[:, 0:4096].rearrange("p (u v g n) -> p u v g n", u=2, v=2, g=KV)
        gel = y_["oG"].rearrange("p (v g n) -> p v g n", v=2, g=KV)
        otok = y_["oG"].rearrange("p (i n) -> p i n", i=2)
        sp3 = y_["sp"].rearrange("p (u n) -> p u n", u=3)
        vc = y_["vc"].rearrange("p (i n) -> p i n", i=2)
        w_ = cut(w_room, [("g2", 4096), ("pt", 1024), ("kc", 510), ("gap", 2), ("oc", 12 * HD), ("w2k", 256), ("w2v", HD), ("smask", 1024)])
        smask = w_["smask"].rearrange("p (h n) -> p h n", h=2)
        gre = w_["g2"].rearrange("p (u v g x) -> p u v g x", u=2, v=2, g=KV)
        pts = w_["pt"].rearrange("p (u n) -> p u n", u=2)
        kc = w_["kc"].rearrange("p (g n) -> p g n", g=2)
        l_ = cut(x_room[:, 4608:], [("w1c", 4096)])
        w1c = l_["w1c"].rearrange("p (v r k f) -> p v r k f", v=2, r=2, k=8)
        oc = w_["oc"].rearrange("p (a d) -> p a d", a=12)
        w2k = w_["w2k"].rearrange("p (g n) -> p g n", g=2)
        w2v = w_["w2v"]
        a_ = cut(act_tmp[:, :, :].rearrange("p s n -> p (s n)"),
                 [("pp", 264), ("ia", 65), ("ib", 65), ("madd", 65), ("m8", 16), ("kcb", P), ("peT", 32), ("b1", 2),
                  ("hb", 2), ("lp", 64), ("cm", 16), ("cl", 16), ("wts", 12), ("coef", 12), ("mx", 12), ("nb", 12),
                  ("ls", 12), ("tmp", 12), ("od", P)])
        kcb = a_["kcb"].rearrange("p (g n) -> p g n", g=2)
        s_ = cut(stat[:, :, :].rearrange("p i n -> p (i n)"), [("vcb", 512), ("ocs", 12 * HD), ("pst", 4 * 16)])
        vcb = s_["vcb"].rearrange("p (g n) -> p g n", g=2)
        ocs = s_["ocs"].rearrange("p (a d) -> p a d", a=12)
        ps_mx, ps_nb, ps_l, ps_cf = [s_["pst"][:, i * 16:(i + 1) * 16] for i in range(4)]
        extra = sb("extra", [P, RB])
        extra2 = sb("extra2", [P, RB])
        kst = [e[:, 0:5 * 256].rearrange("p (i n) -> p i n", i=5) for e in (extra, extra2)]
        cmp_slots = [ring[:, 0, :], extra[:, :]]
        slc_slots = [ring[:, 1, :], ring[:, 2, :], ring[:, 3, :], extra2[:, :]]
        idx = sb("idx", [P, 4, 2 * DB], I32)
        idx_cur = sb("idx_cur", [P, 4, 4], I32)[:, :, :]
        idx_first = sem("idx_first")
        idx_set = sem("idx_set")
        y_out = [sem("y_out0"), sem("y_out1")]
        y_tok = sem("y_tok")
        yt_psum = sem("yt_psum")
        ytok = big[:, 0:2 * DM].rearrange("p (i n) -> p i n", i=2)
        ptb = sb("ptb", [P, 2 * DB], I32)
        gscr = nc.dram_tensor("gate_rows", [DB, 48, DT], F32, kind="Internal").ap()

        n_in = sem("n_in")
        pt_in = sem("pt_in")
        idx_ready = sem("idx_ready")
        q_ready = sem("q_ready")
        q_free = sem("q_free")
        kv_ready = sem("kv_ready")
        kv_sb = sem("kv_sb")
        kv_out = [sem("kv_out0"), sem("kv_out1")]
        g_scr = sem("g_scr")
        gr_in = sem("gr_in")
        zeroed = sem("zeroed")
        win_out = sem("win_out")
        cmp_full = [sem("cmp_full0"), sem("cmp_full1")]
        pc_full = [sem("pc_full0"), sem("pc_full1")]
        win_full = sem("win_full")
        cmp_free = sem("cmp_free")
        cmp_freeA = sem("cmp_freeA")
        gre_free = sem("gre_free")
        slc_full = [sem(f"slc_full{s}") for s in range(4)]
        slc_free = sem("slc_free")
        t_ready = sem("t_ready")
        t_act = sem("t_act")
        t_dve = sem("t_dve")
        hid_step = sem("hid_step")
        gel_ready = sem("gel_ready")
        cv_ready = sem("cv_ready")
        cv_sb = sem("cv_sb")
        vn_full = sem("vn_full")
        sc_ready = sem("sc_ready")
        soft = sem("soft")
        p_ready = sem("p_ready")
        p_norm = sem("p_norm")
        ptp_ready = sem("ptp_ready")
        pt_sb = sem("pt_sb")
        o_ready = sem("o_ready")
        o_done = sem("o_done")
        imp_ready = sem("imp_ready")
        imp_done = sem("imp_done")
        q_set = sem("q_set")
        w_ready = sem("w_ready")
        w_exp = sem("w_exp")
        od_ready = sem("od_ready")
        ot_ready = sem("ot_ready")
        ot_done = sem("ot_done")
        hb_ready = sem("hb_ready")
        hb_sb = sem("hb_sb")

        def units():
            out = []
            for i in range(TT):
                out.append(("cmp", i, 0, 0, 0, 0))
                out += [("full", i, r, gp, h, g2) for r in range(2) for gp in range(2) for h in range(HPG) for g2 in range(2)]
            return out
        UNITS = units()
        NU = len(UNITS)
        AHEAD = NU // 2
        SU = 12
        WINC, CMPU, WINN, SLCN = range(4)
        COL = [1, 0] + list(range(2, SU))
        SEGS = [(3, SU), (1, 3)]
        CHUNK = {WINC: 0}
        CHUNK.update({4 + k: k + 1 for k in range(8)})
        R0 = 16 + 2 * TT
        SR = 32 + 18
        assert NU % 6 == 0 and R0 % 2 == 0
        cmp_rows = cache_cmp.rearrange("n (c p) k g d -> (n c) (p k g d)", p=4)
        slc_rows = cache_slc.rearrange("n (c p) k g d -> (n c) (p k g d)", p=4)

        block = ctx.enter_context(nc.Block())

        @block.sync
        def _(sp):
            def load_block(n, pieces):
                if n - RING >= blk_pos["even"] + 10 and n - RING < blk_pos["odd"]:
                    sp.wait_ge(lo_ready, n - blk_pos["f1"] + 2 * FB - (RING - 1))
                elif 0 <= n - RING - blk_pos["odd"] < ODD_SPLIT:
                    sp.wait_ge(lo_ready, 6 * FB + n - RING - blk_pos["odd"] + 1)
                elif n - RING < blk_pos["even"]:
                    sp.wait_ge(lo_ready, n - (RING - 1))
                else:
                    sp.wait_ge(blk_done, n - (RING - 1))
                for dst, src in pieces:
                    sp.dma_start(dst, src).then_inc(ring_full[n % RING], 64 // len(pieces))

            def kblock(w, c0, n, slot):
                return ring[:, slot, 0:DK * n].rearrange("p (k n) -> p k n", k=DK), \
                    w.rearrange("(k p) n -> p k n", p=P)[:, :, c0:c0 + n]

            def ffn_loads(l, i, f):
                w1 = w_ffn_in[l, i].rearrange("(k p) n -> p k n", p=P)
                w2 = w_ffn_out[l, i]

                def slot_free(F, n):
                    if isinstance(n, int) and n < RING:
                        return
                    if isinstance(n, int) and f in (1, 3) and n < blk_pos[f"f{f}"] + RING:
                        sp.wait_ge(blk_done, n - (RING - 1))
                    else:
                        sp.wait_ge(lo_ready, F - (RING - 1))

                for h in range(2):
                    F0 = SP_BASE[f] + h * FB
                    n0 = blk_pos[f"f{f}"] + h * FB

                    def w1_in(j, u, n=P):
                        s = (n0 + u) % RING
                        slot_free(j + F0, j + n0)
                        v = ring[:, s, 0:2 * DK * n].rearrange("p (k c n) -> p k c n", k=DK, c=2)
                        for c in range(2):
                            d = c if n == P else 1 - c
                            sp.dma_start(v[:, :, d, :], w1[:, :, bass.ds(j * P + (h * FH * P + c * FF), n)])\
                                .then_inc(ring_full[s], 32)

                    def w2_in(m, u):
                        s = (n0 + FH + u) % RING
                        slot_free(m + (F0 + FH), m + (n0 + FH))
                        v = ring[:, s, 0:FW].rearrange("p (k n) -> p k n", n=P)
                        r0, full = h * FW, FH if h == 0 else FH - 1
                        half = FH // 2 if h == 0 else full
                        sp.dma_start(v[:, 0:half], w2[r0:r0 + half * P, bass.ds(m * P, P)]
                                     .rearrange("(k p) n -> p k n", p=P)).then_inc(ring_full[s], 32)
                        if h == 0:
                            sp.dma_start(v[:, half:], w2[half * P:FW, bass.ds(m * P, P)]
                                         .rearrange("(k p) n -> p k n", p=P)).then_inc(ring_full[s], 32)
                        else:
                            sp.dma_start(v[0:FL, full], w2[r0 + full * P:FF, bass.ds(m * P, P)]).then_inc(ring_full[s], 32)

                    for u in range(RING):
                        if f + h == 0 and u == 1:
                            sp.wait_ge(x_in, 16 * len(TILES))
                        w1_in(u, u)
                    for j in range(RING, FH):
                        w1_in(j, j, P if h == 0 or j < FH - 1 else FL)
                    with sp.Fori(0, DK // RING) as i:
                        for u in range(RING):
                            w2_in(i * RING + u, u)

            ffn_loads(0, 0, 0)
            n0 = blk_pos["even"]
            for i in range(6):
                load_block(n0 + i, [kblock(w_in_even, i * 256, 256, (n0 + i) % RING)])
            for i in range(4):
                load_block(n0 + 6 + i, [kblock(w_out_even, i * 256, 256, (n0 + 6 + i) % RING)])
            ffn_loads(0, 1, 1)
            ffn_loads(1, 0, 2)
            n0 = blk_pos["odd"]
            wv = w_in_odd.rearrange("(k p) n -> p k n", p=P)
            for gp in range(2):
                for hp in range(2):
                    n = n0 + gp * 2 + hp
                    v = ring[:, n % RING, :].rearrange("p (k h g d) -> p k h g d", k=DK, h=2, g=2)
                    load_block(n, [(v[:, :, h, g2, :], wv[:, :, ((2 * gp + g2) * HPG + 2 * hp + h) * HD:][:, :, 0:HD])
                                   for h in range(2) for g2 in range(2)])
            for c in range(6):
                load_block(n0 + 4 + c, [kblock(w_in_odd, NH * HD + c * 256, 256, (n0 + 4 + c) % RING)])
            load_block(n0 + 10, [kblock(w_in_odd, NH * HD + 6 * 256, 48, (n0 + 10) % RING)])
            sp.wait_ge(blk_done, n0 + 11)
            sp.wait_ge(kv_out[0], 6 * 16)
            sp.wait_ge(kv_out[1], 6 * 16)
            for q in range(4):
                sp.wait_ge(cmp_free, q + 1)
                sp.dma_start(cmp_slots[q % 2][0:TP // CS, :].rearrange("c (p n) -> c p n", p=4),
                             cmp_p[0].rearrange("(c q p) k g d -> q c p (k g d)", q=4, p=4)[q])\
                    .then_inc(pc_full[q % 2], 16)
            sp.dma_start(win_s[:, 0:WIN - DT], cache_win[:, DT:WIN]).then_inc(win_out, 16)
            for c in range(2):
                sp.wait_ge(kv_out[c], 6 * 16)
            with sp.Fori(0, DB) as b:
                sp.wait_ge(o_done, b * SU + NU)
                sp.dma_start(vnew[0:DT, 0, :], slc_s[bass.ds(b, 1), :, 1].rearrange("o t g d -> (o t) (g d)")).then_inc(vn_full, 16)
                sp.dma_start(vnew[0:DT, 1, :], win_s[bass.ds(b, 1), WIN - DT:WIN, 1].rearrange("o t g d -> (o t) (g d)"))\
                    .then_inc(vn_full, 16)
                sp.wait_ge(slc_free, b * 9 + 4)
                apart(sp)
                sp.dma_start(slc_slots[0], cache_win[bass.ds(b, 1)].rearrange("o (p j) k g d -> (o p) (j k g d)", j=4))\
                    .then_inc(win_full, 16)
            sp.wait_ge(slc_free, DB * 9 + 4)
            sp.wait_ge(cmp_freeA, DB * 8 + 2)
            sp.wait_ge(cmp_free, 4 + DB * 8 + 2)
            wo = w_out_odd.rearrange("(a g h d) n -> a g d h n", a=2, g=2, h=HPG)
            for i in range(4):
                n = n0 + 11 + i
                v = ring[:, n % RING, :].rearrange("p (a h n) -> p a h n", a=2, h=HPG)
                load_block(n, [(v[g2 * HD:(g2 + 1) * HD, gp], wo[gp, g2, :, :, i * 256:(i + 1) * 256])
                               for gp in range(2) for g2 in range(2)])
            ffn_loads(1, 1, 3)
            sp.wait_ge(out_done, 3 * 16)
            for c in range(2):
                sp.wait_ge(kv_out[c], 6 * 16)
            sp.wait_ge(win_out, 16)
            sp.wait_ge(y_out[0], 16 * 3)
            sp.wait_ge(y_out[1], 16 * 2)

        @block.gpsimd
        def _(pool):
            def centre(ln):
                pool.wait_ge(mean_ready, ln + 1)
                for m in range(DK):
                    pool.tensor_tensor(yT[:, m, :], yT[:, m, :], stat[:, 0, :], ALU.subtract).then_inc(centred, 1)

            def low(F, u, slot, w):
                pool.wait_ge(hi_ready, F + 1)
                pool.tensor_tensor(w_sp[:, u % 2, 1, 0:w], ring[:, slot, 0:w], w_sp[:, u % 2, 0, 0:w].bitcast(F32),
                                   ALU.subtract).then_inc(lo_ready, 1)

            def ffn(f, ln=None):
                for h in range(2):
                    F0 = SP_BASE[f] + h * FB
                    n0 = blk_pos[f"f{f}"] + h * FB
                    u0 = h * FB
                    low(F0, u0, n0 % RING, RB)
                    if h == 0 and ln is not None:
                        centre(ln)
                    with pool.Fori(0, 2) as i:
                        for u in range(1, 1 + RING):
                            low(i * RING + (F0 + u), u0 + u, (n0 + u) % RING, RB)
                    for j in range(1 + 2 * RING, FH):
                        low(F0 + j, u0 + j, (n0 + j) % RING, RB if h == 0 or j < FH - 1 else 2 * DK * FL)
                    with pool.Fori(0, DK // RING) as i:
                        for u in range(RING):
                            low(i * RING + (F0 + FH + u), u0 + FH + u, (n0 + FH + u) % RING, FW)

            ffn(0)
            pool.wait_ge(blk_done, 2 * FB - DK)
            pool.dma_start(gms, gm_ws.rearrange("h t s -> t h s")).then_inc(loc_in, 16)
            pool.dma_start(gmb, gm_b.rearrange("(o h) t -> o h t", o=1).broadcast_to([P, NG, P])).then_inc(loc_in, 16)
            pool.dma_start(plw, pool_w.rearrange("g c d -> c g d")).then_inc(loc_in, 16)
            pool.dma_start(psc, pool_scale.rearrange("(g p) -> p g", p=P)).then_inc(loc_in, 16)
            pool.dma_start(lgg, gm_ln_g.rearrange("(o n) -> o n", o=1).broadcast_to([P, PW])).then_inc(loc_in, 16)
            pool.dma_start(lgb, gm_ln_b.rearrange("(o n) -> o n", o=1).broadcast_to([P, PW])).then_inc(loc_in, 16)
            pool.dma_start(past[0:DB * PAST, :], state_pool.rearrange("b s n -> (b s) n")).then_inc(loc_in, 16)
            pool.dma_start(pool_s[:, 0:PAST - DT, :], state_pool[:, DT:PAST, :]).then_inc(out_done, 16)
            centre(0)
            pool.wait_ge(z_freeD, 8)
            pool.dma_start(pool_p.rearrange("o s n -> (o s) n"), prow_p[0:PAST, :]).then_inc(out_done, 16)
            pool.dma_start(pool_s[:, PAST - DT:PAST, :], prow_s[0:TS, :]).then_inc(out_done, 16)
            pool.wait_ge(z_freeD, 13)
            pool.dma_start(gmv_s.rearrange("b t n -> (b t) n"), vtok[0:TS, 4, :]).then_inc(gmv_out, 16)
            pool.wait_ge(gmv_out, 16)
            ffn(1, 1)
            ffn(2, 2)

            def low_odd(i):
                low(6 * FB + i, i, (blk_pos["odd"] + i) % RING, RB)
            low_odd(0)
            centre(3)
            low_odd(1)
            low_odd(2)
            pool.wait_ge(x_ready, 4 * DK)
            for g in range(16):
                if g == 8:
                    low_odd(3)
                pool.dma_start(ptb[g * 8:(g + 1) * 8, :], page_table.rearrange("(o b) (h g) -> g o (b h)", o=1, g=16)[g]
                               .broadcast_to([8, 2 * DB])).then_inc(pt_in, 16)
            low_odd(4)
            for g2 in range(2):
                for k in range(2):
                    pe_ = cmp_pe[k].rearrange("(k p) d -> p d k", p=2)[g2]
                    pool.dma_start(a_["peT"][g2 * HD:(g2 + 1) * HD, k * 16:(k + 1) * 16], pe_).then_inc(n_in, 16)
            pool.dma_start(a_["b1"], cmp_b1.rearrange("v f -> f v")).then_inc(n_in, 16)
            pool.memset(a_["pp"], 0.0).then_inc(zeroed, 1)
            pool.memset(a_["kcb"], 0.0).then_inc(zeroed, 1)
            pool.memset(s_["vcb"], 0.0).then_inc(zeroed, 1)
            pool.memset(b_["qb"], 0.0).then_inc(zeroed, 1)
            low_odd(5)
            kv_dst = [(cmp_p, cmp_s), (slc_p, slc_s), (win_p, win_s[:, WIN - DT:WIN])]
            for c in range(6):
                r, v = c // 2, c % 2
                pool.wait_ge(kv_sb, c + 1)
                pool.dma_start(kv_dst[r][0][0].rearrange("(i p) k g d -> p i k (g d)", p=P)[:, :, v],
                               vtk[:, r - 1] if v and r else kst[c % 2][:, 0:TT]).then_inc(kv_out[c % 2], 16)
                pool.dma_start(kv_dst[r][1].rearrange("b t k g d -> b t k (g d)")[:, :, v],
                               kst[c % 2][TS:P, TT, :]).then_inc(kv_out[c % 2], 16)
                if 6 + c < ODD_SPLIT:
                    low_odd(6 + c)
            pool.wait_ge(blk_done, blk_pos["odd"] + ODD_SPLIT)
            pool.dma_start(l_["w1c"].rearrange("p (k f) -> p k f", f=HID),
                           cmp_w1.rearrange("v (k p) f -> p (v k) f", p=P)).then_inc(n_in, 16)
            for g2 in range(2):
                pool.dma_start(w2k[:, g2, g2 * HD:(g2 + 1) * HD], cmp_w2[0]).then_inc(n_in, 16)
            pool.dma_start(w2v, cmp_w2[1]).then_inc(n_in, 16)
            pool.memset(w2k[:, 0, HD:P], 0.0).then_inc(zeroed, 1)
            pool.memset(w2k[:, 1, 0:HD], 0.0).then_inc(zeroed, 1)
            pool.wait_ge(q_free, 13)
            for i in range(DB):
                pool.dma_start(gscr[i].rearrange("c t -> t c"), gates[i * DT:(i + 1) * DT, TT, :]).then_inc(g_scr, 16)
            pool.wait_ge(g_scr, 16 * DB)
            for r in range(3):
                pool.dma_start(gr[:, :, r], gscr.rearrange("b (r u) t -> r (u t) b", r=3)[r]).then_inc(gr_in, 16)
            pool.wait_ge(idx_ready, 4)
            pool.wait_ge(blk_done, blk_pos["odd"] + 11)

            def gather(dst, rows, q, bh, full):
                pool.indirect_dma_start(out=dst, out_offset=None, in_=rows,
                                        in_offset=bass.IndirectOffsetOnAxis(ap=idx_cur[:, q, bh:bh + 1], axis=0)).then_inc(full, 16)

            def cmp_gather(b, o, i):
                pool.wait_ge(cmp_free, b * 8 + (o * 8 + 4 + i + 1))
                pool.wait_ge(cmp_freeA, b * 8 + (o * 8 + i + 1))
                apart(pool)
                gather(cmp_slots[i % 2], cmp_rows, i // 2, 2 * o + i % 2, cmp_full[i % 2])

            def sample(b, last):
                n = 2 if last else 4
                pool.tensor_copy(idx_cur[:, :, 0:n], idx[:, :, bass.ds(b * 2, n)]).then_inc(idx_set, 1)
                pool.wait_ge(idx_set, b + 1)
                for i in range(2, 8):
                    cmp_gather(b, 0, i)
                for c in range(1, 9):
                    if c == 5 and not last:
                        for i in range(2):
                            cmp_gather(b, 1, i)
                    pool.wait_ge(slc_free, b * 9 + (c if c < 4 else c + 1))
                    apart(pool)
                    gather(slc_slots[c % 4], slc_rows, (c - 1) % 4, (c - 1) // 4, slc_full[c % 4])
                if not last:
                    for s in range(2):
                        pool.wait_ge(cmp_full[s], b * 64 + 80)
                    for s in range(4):
                        pool.wait_ge(slc_full[s], b * 32 + 32)
            pool.tensor_copy(idx_cur[:, :, 0:2], idx[:, :, 0:2]).then_inc(idx_first, 1)
            pool.wait_ge(idx_first, 1)
            for i in range(2):
                cmp_gather(0, 0, i)
            for s in range(2):
                pool.wait_ge(cmp_full[s], 16)
            with pool.Fori(0, DB - 1) as b:
                sample(b, False)
            sample(DB - 1, True)
            ffn(3, 4)
            centre(5)

        @block.scalar
        def _(act):
            act.dma_start(cst[:, 0:P], cdram[:, 0:P]).then_inc(ident_in, 16)
            for i, (t0, n) in enumerate(TILES):
                src = x_prompt[0, t0:t0 + n, :] if i < TT else x_sample.rearrange("b t n -> (b t) n")
                act.dma_start(xl[0:n, i, :], src).then_inc(x_in, 16)
            act.dma_start(cst[:, P:], cdram[:, P:]).then_inc(consts_in, 16)
            act.dma_start(lng[:, :, :], ln_g.rearrange("l i (k p) -> p (l i) k", p=P)).then_inc(ln_in, 16)
            act.dma_start(lnb[:, :, :], ln_b.rearrange("l i (k p) -> p (l i) k", p=P)).then_inc(ln_in, 16)

            def high(f, U, full, done, slot, w=RB):
                act.wait_ge(ring_full[slot], full)
                if done is not None:
                    act.wait_ge(blk_done, done)
                act.activation(w_sp[:, U % 2, 0, 0:w], ring[:, slot, 0:w], ACT.Copy).then_inc(hi_ready, 1)

            def width(U):
                u = U % FB
                return FW if u >= FH else 2 * DK * FL if U == FB + FH - 1 else RB

            def high_at(f, U):
                n = blk_pos[f"f{f}"] + U
                high(f, U, full_at(n), n - 1 if U >= 2 else None, n % RING, width(U))

            def high_odd(i):
                n = blk_pos["odd"] + i
                high(None, i, full_at(n), n - 1 if i >= 2 else None, n % RING)

            def high_in(f, i, U):
                n = blk_pos[f"f{f}"] + U
                high(f, U, i * 64 + full_at(n), i * RING + (n - 1), n % RING, width(U))
            high_at(0, 0)
            for k in range(DK):
                act.wait_ge(xt_sb, k + 1)
                act.activation(x_hi[:, k, :], yT[:, k, :], ACT.Copy).then_inc(x_full, 1)
            high_at(0, 1)

            def ffn(f):
                for h in range(2):
                    n0 = blk_pos[f"f{f}"] + h * FB

                    def silu(j, s, n=P):
                        act.wait_ge(blk_done, j + (n0 + 1))
                        act.activation(act_tmp[0:n, s, :].rearrange("p (c n) -> p c n", c=2), halves(2 * s)[P - n:P],
                                       ACT.Silu).then_inc(silu_ready, 1)
                    silu(0, 0)
                    high_at(f, h * FB + 2)
                    with act.Fori(0, 2) as i:
                        for u in range(1, 1 + RING):
                            silu(i * RING + u, u % 2)
                            high_in(f, i, h * FB + u + 2)
                    for j in range(1 + 2 * RING, FH):
                        silu(j, j % 2, P if h == 0 or j < FH - 1 else FL)
                        high_at(f, h * FB + j + 2)
                    if h == 0:
                        for m in range(DK):
                            high_at(f, FH + m + 2)

            def norm(ln, before=None, after=None):
                b = ln * DK
                y0 = Y_BASE[ln] + 2 + (DK if ln not in MIX else 0)

                def high_next(U):
                    if after == "odd":
                        high_odd(U)
                    else:
                        high_at(after, U)
                for m in range(DK):
                    if before is not None and m + 2 < DK:
                        high_at(before, FB + FH + m + 2)
                    act.wait_ge(y_sum, y0 + m + 1)
                    if m >= 3:
                        act.wait_ge(sq_used, ln * (DK - 1) + max(1, m - 3))
                    act.activation(tmp3[m % 3], yT[:, m, :], ACT.Square).then_inc(sq_ready, 1)
                if after is not None:
                    high_next(0)
                act.wait_ge(stats_done, 2 * ln + 1)
                act.activation(hv(stat[:, 0, :]), halves(0), ACT.Copy).then_inc(mean_ready, 1)
                act.wait_ge(var_ready, ln + 1)
                act.activation(stat[:, 2, :], stat[:, 1, :], ACT.Sqrt).then_inc(std_ready, 1)
                if after is not None:
                    high_next(1)
                if ln == 1:
                    act.wait_ge(out_done, 3 * 16)
                for m in range(DK):
                    act.wait_ge(norm_ready, b + m + 1)
                    g, c = lng[:, ln, m:m + 1], lnb[:, ln, m:m + 1]
                    if after is not None:
                        act.activation(x_hi[:, m, :], yT[:, m, :], ACT.Identity, bias=c, scale=g)
                    act.activation(yT[:, m, :], yT[:, m, :], ACT.Identity, bias=c, scale=g)\
                        .then_inc(x_ready if after is None else x_full, 1)
            ffn(0)
            act.wait_ge(consts_in, 16)
            act.wait_ge(ln_in, 32)
            norm(0, before=0)
            act.wait_ge(loc_in, 7 * 16)
            for h in range(NG):
                act.wait_ge(z_ready, 4 + h + 1)
                act.activation(hv(uT[:, h, :]), halves(h), ACT.Copy).then_inc(z_freeA, 1)
            for i, (t0, n) in enumerate(TILES):
                act.wait_ge(v_var, i + 1)
                act.activation(mv[0:n, i, 3:4], mv[0:n, i, 2:3], ACT.Sqrt).then_inc(v_std, 1)
            for g in range(NG):
                act.wait_ge(z_ready, 22 + g)
                act.activation(hv(cat[:, g, :]), halves((g + 1) % 4), ACT.Copy, scale=psc[:, g:g + 1]).then_inc(z_freeA, 1)
            norm(1, after=1)
            ffn(1)
            norm(2, before=1, after=2)
            ffn(2)
            norm(3, before=2, after="odd")

            for z in range(8):
                act.wait_ge(q_ready, z + 1)
                act.activation(hv(qT[:, z, :]), halves(z % 4), ACT.Copy, scale=C("qscale")[:, z:z + 1]).then_inc(q_free, 1)
                if z % 2 == 1:
                    high_odd(z // 2 + 2)
            for r in range(2):
                for i in range(2):
                    high_odd(6 + 2 * r + i)
                for gp in range(2):
                    z = 8 + 2 * r + gp
                    act.wait_ge(q_ready, z + 1)
                    act.activation(hv(kT[:, r, gp, :]), halves(3), ACT.Copy).then_inc(q_free, 1)
            act.wait_ge(q_ready, 13)
            act.activation(gates[:, 0:TT, :], bank(0, TT * 48).rearrange("p (i n) -> p i n", i=TT), ACT.Sigmoid)
            act.activation(gates[0:TS, TT, :], bank(0)[0:TS, TT * 48:(TT + 1) * 48], ACT.Sigmoid).then_inc(q_free, 1)

            def t_round(n, dst, src):
                act.wait_ge(t_ready, n + 1)
                act.activation(dst, src, ACT.Copy).then_inc(t_act, 1)

            def xtc_round(base, kt, v, half, width, bk=0):
                t_round(base, xTc[:, kt, v, :, half * P:half * P + width],
                        bank(bk, KV * width).rearrange("p (g c) -> p g c", g=KV))

            def exps(n, s, w, scale, bias, accum):
                act.wait_ge(soft, n + 1)
                if accum is None:
                    act.activation(sp3[:, s, 0:w], sp3[:, s, 0:w], ACT.Exp).then_inc(p_ready, 1)
                else:
                    act.activation(sp3[:, s, 0:w], sp3[:, s, 0:w], ACT.Exp, scale=scale, bias=bias,
                                   accum_out=accum).then_inc(p_ready, 1)

            def pt_copy(n, u, rows, w):
                act.wait_ge(ptp_ready, n + 1)
                if not isinstance(rows, int):
                    act.activation(pts[0:rows[0], u, 0:P], bank(4 + u)[0:rows[0], 0:P], ACT.Copy)
                    act.activation(pts[0:rows[1], u, P:2 * P], bank(4 + u)[0:rows[1], P:2 * P], ACT.Copy).then_inc(pt_sb, 1)
                else:
                    act.activation(pts[0:rows, u, 0:w], bank(4 + u)[0:rows, 0:w], ACT.Copy).then_inc(pt_sb, 1)

            act.wait_ge(n_in, 9 * 16)
            act.wait_ge(hb_ready, 1)
            for k in range(2):
                ins = act.activation(a_["hb"][:, k:k + 1], bank(7)[:, k:k + 1], ACT.Identity, bias=a_["b1"][:, k:k + 1])
            ins.then_inc(hb_sb, 1)
            act.wait_ge(hb_sb, 1)
            for st in range(8):
                xtc_round(2 * st, st % 2, 0, 0, 32)
            act.wait_ge(hid_step, 8)
            for v in range(2):
                act.activation(gel[:, v, :, 0:NBP], bank(2 + v, KV * NBP).rearrange("p (g n) -> p g n", g=KV),
                               ACT.Gelu_apprx_tanh, bias=a_["hb"][:, v:v + 1]).then_inc(gel_ready, 1)
            def prompt_exp(n):
                kind, i, r, gp, h, g2 = UNITS[n]
                sl = slope((2 * gp + g2) * HPG + h)
                if kind == "cmp":
                    exps(n, n % 3, 512, None, None, None)
                else:
                    exps(n, n % 3, (i + 1) * P, sl, ps_nb[:, n % 16:n % 16 + 1], ps_l[:, n % 16:n % 16 + 1])

            act.sem_inc(cmp_freeA, 2)

            def regroup_values(b, o, q, half):
                act.wait_ge(cmp_full[half], b * 64 + (o * 64 + 16 * (q + 1)))
                act.wait_ge(gre_free, b * 8 + (o * 8 + 4 + 2 * q + half + 1))
                act.activation(gre[:, half, 1].rearrange("c g (p d) -> c g p d", p=4),
                               cmp_slots[half].rearrange("c (p v g d) -> c v g p d", p=4, v=2, g=KV)[:, 1],
                               ACT.Copy).then_inc(cmp_freeA, 1)

            prompt_exp(0)
            pt_copy(0, 0, P, 512)
            prompt_exp(1)
            for n, (kind, i, r, gp, h, g2) in enumerate(UNITS):
                if n + 1 < NU:
                    pt_copy(n + 1, (n + 1) % 2, P, 512 if UNITS[n + 1][0] == "cmp" else (UNITS[n + 1][1] + 1) * P)
                if n + 2 < NU:
                    prompt_exp(n + 2)
                if n in (AHEAD, AHEAD + 1):
                    regroup_values(0, 0, 0, n - AHEAD)
                if i > 0 and kind == "cmp" or n + 1 == NU:
                    i0 = i if n + 1 == NU else i - 1
                    t_round(16 + 2 * i0, qT[:, 0:4, i0 * P:(i0 + 1) * P], bank(0).rearrange("p (h t) -> p h t", h=HPG))
            sl = C("sslope")[:, 0:1]

            def weights(b):
                act.wait_ge(w_ready, b + 1)
                for j, (a0, a1) in enumerate(SEGS):
                    ins = act.activation(a_["wts"][:, a0:a1], a_["mx"][:, a0:a1], ACT.Exp, scale=sl,
                                         bias=b_["seg"][:, 2 + j:3 + j])
                ins.then_inc(w_exp, 1)

            def compress(b, o):
                for q in range(4):
                    if q > 0:
                        for half in range(2):
                            regroup_values(b, o, q, half)
                    for st in (2 * q, 2 * q + 1):
                        for v in range(2):
                            xtc_round(b * SR + (o * SR + R0 + 4 * st + 2 * v), st % 2, v, 0, P, bk=6 * v)
                    if q == 0 and o == 1:
                        weights(b)
                act.wait_ge(hid_step, b * 8 + (o * 8 + 16))
                for v in range(2):
                    for gp in range(2):
                        act.activation(gel[:, v, 2 * gp:2 * gp + 2, 0:NB],
                                       bank(2 + 2 * v + gp, 2 * NB).rearrange("p (g n) -> p g n", g=2),
                                       ACT.Gelu_apprx_tanh, bias=a_["hb"][:, v:v + 1]).then_inc(gel_ready, 1)

            def attend(b, last):
                ub = b * SU

                def unit_width(a):
                    return NB if a == CMPU else DT if a in (WINN, SLCN) else 512

                def k_round(a):
                    c = CHUNK[a]
                    t_round(b * SR + (R0 + 32 + 2 * c), kTc[:, c % 2, 0, :], bank(0))

                def exp_unit(a):
                    exps(ub + (NU + a), a % 3, unit_width(a), sl, a_["nb"][:, a:a + 1], a_["ls"][:, COL[a]:COL[a] + 1])

                def copy_unit(a):
                    w = unit_width(a)
                    if a == CMPU:
                        pt_copy(ub + (NU + a), a % 2, (P, NB - P), None)
                    else:
                        pt_copy(ub + (NU + a), a % 2, P if w == 512 else DT, 512 if w == 512 else P)
                exp_unit(0)
                exp_unit(1)
                copy_unit(0)
                for a in range(SU):
                    if a == 2:
                        k_round(a + 3)
                    if a + 2 < SU:
                        exp_unit(a + 2)
                    if a + 3 in CHUNK and a != 2:
                        k_round(a + 3)
                    if a + 1 < SU:
                        copy_unit(a + 1)
                    if a in (8, 9) and not last:
                        regroup_values(b, 1, 0, a - 8)

            def first_keys(b, o):
                t_round(b * SR + (o * SR + R0 + 32), kTc[:, 0, 0, :], bank(0))

            compress(0, 0)
            first_keys(0, 0)
            with act.Fori(0, DB - 1) as b:
                attend(b, False)
                compress(b, 1)
                first_keys(b, 1)
            attend(DB - 1, True)
            weights(DB - 1)
            norm(4, after=3)
            ffn(3)
            norm(5, before=3)
            for i, (t0, n) in enumerate(TILES):
                act.wait_ge(y_tok, i + 1)
                dst = y_p[0, t0:t0 + n, :] if i < TT else y_s.rearrange("b t n -> (b t) n")
                act.dma_start(dst, ytok[0:n, i % 2, :]).then_inc(y_out[i % 2], 16)

        @block.vector
        def _(dve):
            step = Chain(dve, dve_chain)
            dve.sem_inc(gu_free, 2)
            dve.sem_inc(y_sum, 2)
            dve.sem_inc(h_ready, 1)
            dve.sem_inc(ot_done, 1)
            for k in range(DK):
                dve.wait_ge(xt_psum, k + 1)
                dve.tensor_copy(yT[:, k, :], pair(k % 4)).then_inc(xt_sb, 1)
            dve.wait_ge(xt_sb, DK)
            for k in range(DK):
                dve.wait_ge(x_full, k + 1)
                dve.tensor_tensor(x_lo[:, k, :], yT[:, k, :], x_hi[:, k, :].bitcast(F32), ALU.subtract).then_inc(xt_first, 1)

            def add(scale, m, sem_, count):
                dve.wait_ge(sem_, count)
                y = hv(yT[:, m, :]) if isinstance(m, int) else hv(yT[:, bass.ds(m[0], 1), :])
                slot = m % 2 if isinstance(m, int) else m[1] % 2
                dve.scalar_tensor_tensor(y, y, scale, halves(2 + slot), ALU.mult, ALU.add).then_inc(y_sum, 1)

            def last_sums(ln, scale, sem_, count):
                y0 = Y_BASE[ln] + 2 + (DK if ln not in MIX else 0)

                def squares(m):
                    dve.wait_ge(sq_ready, ln * DK + m + 1)
                    first = act_tmp[:, 0, :] if m == 1 else stat[:, 1, :]
                    if m > 1:
                        dve.wait_ge(sq_used, ln * (DK - 1) + m - 1)
                    dve.tensor_tensor(stat[:, 1, :], first, tmp3[m % 3], ALU.add).then_inc(sq_used, 1)
                for m in range(DK):
                    add(scale, m, sem_, count + m + 1)
                    dve.wait_ge(y_sum, y0 + m + 1)
                    if m > 0:
                        first = yT[:, 0, :] if m == 1 else stat[:, 0, :]
                        step(dve.tensor_tensor(stat[:, 0, :], first, yT[:, m, :], ALU.add))
                    if m == DK - 1:
                        dve.sem_inc(sums_ready, 1)
                    if m > 1:
                        squares(m - 1)
                squares(DK - 1)
                dve.wait_ge(sq_used, (ln + 1) * (DK - 1))
                dve.sem_inc(sums_ready, 1)

            def ffn(f):
                for h in range(2):
                    c = f * FT + h * FH
                    n0 = blk_pos[f"f{f}"] + h * FB

                    def hidden(j, s, n=P):
                        dve.wait_ge(silu_ready, j + (c + 1))
                        gate = act_tmp[0:n, s, :].rearrange("p (c n) -> p c n", c=2)
                        up = halves(2 * s + (1 if n == P else 0))[0:n]
                        hh = hv(h_hi[0:n, bass.ds(j, 1), :])
                        dve.tensor_tensor(hh, gate, up, ALU.mult)
                        dve.wait_ge(h_ready, j + (c + 1))
                        dve.tensor_tensor(hv(tmp3[2][0:n]), gate, up, ALU.mult)\
                            .then_inc(gu_free, 1)
                        dve.wait_ge(gu_free, j + (c + 3))
                        dve.tensor_tensor(h_lo[0:n, bass.ds(j, 1), :], tmp3[2][0:n].rearrange("p (o n) -> p o n", o=1),
                                          h_hi[0:n, bass.ds(j, 1), :].bitcast(F32), ALU.subtract).then_inc(h_ready, 1)
                    with dve.Fori(0, FH // 2) as i:
                        for u in range(2):
                            hidden(i * 2 + u, u)
                    hidden(FH - 1, (FH - 1) % 2, P if h == 0 else FL)
                    if h == 0:
                        with dve.Fori(0, DK // 2) as i:
                            for u in range(2):
                                add(2 * ALPHA, (i * 2 + u, u), blk_done, i * 2 + (n0 + FH + u + 1))
                    else:
                        last_sums(LN_OF[f], 1.0, blk_done, n0 + FH)

            def norm(ln, eps):
                b = ln * DK

                def low(m):
                    dve.wait_ge(x_full, X_BASE[ln] + m + 1)
                    dve.tensor_tensor(x_lo[:, m, :], yT[:, m, :], x_hi[:, m, :].bitcast(F32), ALU.subtract)\
                        .then_inc(x_ready, 1)
                dve.wait_ge(mean_ready, ln + 1)
                step(dve.tensor_tensor(stat[:, 2, :], stat[:, 0, :], stat[:, 0, :], ALU.mult))
                dve.wait_ge(stats_done, 2 * ln + 2)
                step(dve.tensor_tensor(hv(stat[:, 1, :]), halves(1), hv(stat[:, 2, :]), ALU.subtract))
                dve.tensor_scalar(stat[:, 1, :], stat[:, 1, :], 0.0, eps, ALU.max, ALU.add).then_inc(var_ready, 1)
                dve.wait_ge(std_ready, ln + 1)
                step(dve.reciprocal(stat[:, 2, :], stat[:, 2, :]))
                for m in range(DK):
                    dve.wait_ge(centred, b + m + 1)
                    dve.tensor_tensor(yT[:, m, :], yT[:, m, :], stat[:, 2, :], ALU.mult).then_inc(norm_ready, 1)
                    if ln in X_BASE and m > 0:
                        low(m - 1)
                if ln in X_BASE:
                    low(DK - 1)

            ffn(0)
            norm(0, 4 * EPS)

            dve.wait_ge(consts_in, 16)
            dve.wait_ge(loc_in, 7 * 16)
            step(dve.memset(ext[:, :, 0:PAST], 0.0))
            for g in range(NG):
                dve.wait_ge(z_ready, g + 1)
                step(dve.tensor_copy(ext[:, g, PAST:PAST + TP], psum[:, g * 1024:g * 1024 + TP]))
                step(dve.tensor_copy(pnew[:, g, :], psum[:, g * 1024 + TP:g * 1024 + T]))
                dve.tensor_copy(exs[:, g, :, PAST:], psum[:, g * 1024 + TP:g * 1024 + T]
                                .rearrange("p (b t) -> p b t", b=DB)).then_inc(z_freeD, 1)
            dve.wait_ge(z_ready, 9)
            dve.tensor_tensor(wsT, bank(0).rearrange("p (h t) -> p h t", h=NG),
                              C("tri").rearrange("p (o t) -> p o t", o=1).broadcast_to([P, NG, P]),
                              ALU.mult).then_inc(z_freeD, 1)
            dve.wait_ge(z_ready, 10)
            for g in range(NG):
                ins = dve.tensor_copy(exs[:, g, :, 0:PAST], bank(2)[:, g * DB * PAST:(g + 1) * DB * PAST]
                                      .rearrange("p (b s) -> p b s", b=DB))
            ins.then_inc(z_freeD, 1)
            dve.wait_ge(z_ready, 11)
            dve.tensor_tensor(wsB[0:TS], bank(4, NG * TS)[0:TS].rearrange("p (h t) -> p h t", h=NG),
                              C("bdiag")[0:TS].rearrange("p (o t) -> p o t", o=1).broadcast_to([TS, NG, TS]),
                              ALU.mult).then_inc(z_freeD, 1)
            dve.wait_ge(z_ready, 12)
            dve.tensor_copy(prow_p[0:PAST, :], bank(6)[0:PAST])
            dve.tensor_copy(prow_s[0:TS, :], bank(7)[0:TS]).then_inc(z_freeD, 1)
            def pooling(g):
                src = ext[:, g, :]
                for r in range(g + 1):
                    w = 1 << r
                    dst = sums[:, r % 2, :]
                    lo_ = 2 * w - 1
                    step(dve.tensor_tensor(dst[:, lo_:], src[:, lo_:], src[:, lo_ - w:EXT - w], ALU.add))
                    src = dst
                d = dif[:, g, :]
                step(dve.scalar_tensor_tensor(d[:, 0:TP], src[:, PAST:PAST + TP], 0.5 ** (g + 1),
                                              ext[:, g, PAST:PAST + TP], ALU.mult, ALU.subtract))
                step(dve.tensor_tensor(d[:, 0:16], src[:, PAST:PAST + 16], C("rcnt")[:, g * 16:g * 16 + 16], ALU.mult))
                step(dve.tensor_tensor(d[:, 0:16], d[:, 0:16], ext[:, g, PAST:PAST + 16], ALU.subtract))
                dve.scalar_tensor_tensor(
                    d[:, TP:T].rearrange("p (b t) -> p b t", b=DB),
                    src[:, PAST + TP:].rearrange("p (b s) -> p b s", b=DB)[:, :, PAST:], 0.5 ** (g + 1),
                    exs[:, g, :, PAST:], ALU.mult, ALU.subtract).then_inc(e_dif, 1)
                dve.wait_ge(e_dif, g + 1)

            for i, (t0, n) in enumerate(TILES):
                src = bank(2 * (i % 4))[0:n]
                dve.wait_ge(z_ready, 13 + i)
                step(dve.bn_stats(bns[0:n, i, :], src))
                step(dve.bn_aggr(mv[0:n, i, 0:2], bns[0:n, i, :]))
                dve.tensor_scalar(mv[0:n, i, 2:3], mv[0:n, i, 1:2], EPS, None, ALU.add).then_inc(v_var, 1)
                dve.wait_ge(v_std, i + 1)
                step(dve.reciprocal(mv[0:n, i, 3:4], mv[0:n, i, 3:4]))
                step(dve.tensor_scalar(vtok[0:n, i, :], src, mv[0:n, i, 0:1], mv[0:n, i, 3:4],
                                       ALU.subtract, ALU.mult))
                step(dve.tensor_tensor(vtok[0:n, i, :], vtok[0:n, i, :], lgg[0:n], ALU.mult))
                dve.tensor_tensor(vtok[0:n, i, :], vtok[0:n, i, :], lgb[0:n], ALU.add).then_inc(z_freeD, 1)
                if i < NG:
                    dve.wait_ge(z_freeD, 9 + i)
                    pooling(i)
            dve.wait_ge(z_freeA, NG)
            for h in range(NG):
                s = (h + 1) % 4
                dve.wait_ge(z_ready, 18 + h)
                pp, ps = psum[:, s * 1024:s * 1024 + TP], psum[:, s * 1024 + TP:s * 1024 + T]
                cp, cs = cat[:, NG + h, 0:TP], cat[:, NG + h, TP:T]
                step(dve.tensor_tensor(cp.rearrange("p (c t) -> p c t", c=TT), pp.rearrange("p (c t) -> p c t", c=TT),
                                       gmb[:, h:h + 1, :].broadcast_to([P, TT, P]), ALU.add))
                step(dve.tensor_tensor(cs.rearrange("p (b t) -> p b t", b=DB), ps.rearrange("p (b t) -> p b t", b=DB),
                                       gmb[:, h:h + 1, 0:DT].broadcast_to([P, DB, DT]), ALU.add))
                dve.tensor_tensor(cat[:, NG + h, :], cat[:, NG + h, :], uT[:, h, :], ALU.mult).then_inc(z_freeD, 1)
            last_sums(1, ALPHA, y_ready, 0)
            dve.wait_ge(out_done, 3 * 16)
            norm(1, EPS)
            dve.wait_ge(gmv_out, 16)
            ffn(1)
            norm(2, 4 * EPS)
            ffn(2)
            norm(3, 4 * EPS)

            dve.wait_ge(pt_in, 16 * 16)
            for q in range(4):
                dve.tensor_scalar(idx[:, q, :], ptb[:, :], 32.0, C("rowpg")[:, q:q + 1], ALU.mult, ALU.add)\
                    .then_inc(idx_ready, 1)
            for c in range(6):
                r, v = c // 2, c % 2
                o0 = (c % 2) * 3
                dve.wait_ge(kv_ready, c + 1)
                if c >= 2:
                    dve.wait_ge(kv_out[c % 2], 16 * 2 * (c // 2))
                src = psum[:, o0 * 512:o0 * 512 + 1024].rearrange("p (i n) -> p i n", i=TT)
                dve.tensor_copy(vtk[:, r - 1] if v and r else kst[c % 2][:, 0:TT], src)
                dve.tensor_copy(kst[c % 2][TS:P, TT, :], bank(o0 + 2)[TS:P, 0:256]).then_inc(kv_sb, 1)

            def t_round(n, dst, src):
                dve.wait_ge(t_ready, n + 1)
                return dve.tensor_copy(dst, src).then_inc(t_dve, 1)

            def xtc_round(base, kt, v, half, width, bk=1):
                t_round(base, xTc[:, kt, v, :, half * P:half * P + width],
                        bank(bk, KV * width).rearrange("p (g c) -> p g c", g=KV))

            def regroup(sems, slot, full, free, rows):
                dve.wait_ge(sems[slot], full)
                dve.wait_ge(gre_free, free)
                src = cmp_slots[slot][0:rows].rearrange("c (p v g d) -> c v g p d", p=4, v=2, g=KV)
                dst = gre[0:rows, slot].rearrange("c v g (p d) -> c v g p d", p=4)
                dve.tensor_copy(dst[:, 0], src[:, 0])
                dve.tensor_copy(dst[:, 1], src[:, 1]).then_inc(cmp_free, 1)

            dve.wait_ge(kv_out[0], 6 * 16)
            dve.wait_ge(kv_out[1], 6 * 16)
            for q in range(4):
                regroup(pc_full, q % 2, 16 * (q // 2 + 1), q + 1, TP // CS)
                for kt in range(2):
                    xtc_round(4 * q + 2 * kt + 1, kt, 1, 0, 32)
            dve.wait_ge(zeroed, 6)
            dve.wait_ge(cv_ready, 1)
            for g2 in range(2):
                ins = dve.tensor_copy(kcb[g2 * HD:(g2 + 1) * HD, :, g2 * 32:g2 * 32 + NBP],
                                      bank(6, 2 * NBP)[g2 * HD:(g2 + 1) * HD].rearrange("p (g n) -> p g n", g=2))
            ins.then_inc(cv_sb, 1)
            dve.wait_ge(cv_ready, 2)
            src = bank(7, 256)[0:NBP].rearrange("p (a g d) -> p a g d", a=2, g=2)
            for h2 in range(2):
                for g2 in range(2):
                    o0 = (h2 * 2 + g2)
                    ins = dve.tensor_copy(vcb[o0 * 32:o0 * 32 + NBP, :, o0 * HD:(o0 + 1) * HD], src[:, :, g2, :])
            ins.then_inc(cv_sb, 1)

            def bc(x):
                return x.rearrange("p (u o) -> p u o", o=1).broadcast_to([P, NH, 32])

            def prompt_soft(n):
                kind, i, r, gp, h, g2 = UNITS[n]
                dve.wait_ge(sc_ready, n + 1)
                if n >= 3:
                    dve.wait_ge(ptp_ready, n - 2)
                S = sp3[:, n % 3, :]
                if kind == "cmp":
                    S3 = S.rearrange("p (u n) -> p u n", u=NH)

                    step(dve.tensor_tensor(S3, bank(2 + n % 2).rearrange("p (u n) -> p u n", u=NH),
                                           C("negdc")[:, i * 32:(i + 1) * 32].rearrange("p (o n) -> p o n", o=1)
                                           .broadcast_to([P, NH, 32]), ALU.add))
                    step(dve.tensor_reduce(a_["cm"], S3, AX.X, ALU.max))
                    step(dve.tensor_scalar(a_["cm"], a_["cm"], -1e20, None, ALU.max))
                    step(dve.tensor_tensor(S3, S3, bc(a_["cm"]), ALU.subtract))
                    dve.tensor_tensor(S3, S3, bc(C("uslope")), ALU.mult).then_inc(soft, 1)
                    return
                c = n % 16
                w = (i + 1) * P
                step(dve.tensor_tensor_reduce(out=S[:, 0:w], in0=bank(2 + n % 2, w), in1=C("negd")[:, TP - w:TP], scale=1.0,
                                              scalar=-3e38, op0=ALU.add, op1=ALU.max, accum_out=ps_mx[:, c:c + 1]))
                dve.tensor_scalar(ps_nb[:, c:c + 1], ps_mx[:, c:c + 1], -slope((2 * gp + g2) * HPG + h), None,
                                  ALU.mult).then_inc(soft, 1)

            def prompt_cmp_scale(n):
                kind, i, r, gp, h, g2 = UNITS[n]
                dve.wait_ge(p_ready, n + 1)
                step(dve.tensor_reduce(a_["cl"], sp3[:, n % 3, :].rearrange("p (u n) -> p u n", u=NH), AX.X, ALU.add))
                step(dve.tensor_scalar(a_["cl"], a_["cl"], 1e-30, None, ALU.max))
                step(dve.reciprocal(a_["cl"], a_["cl"]))
                step(dve.tensor_tensor(a_["cl"].rearrange("p (a h g) -> p a h g", a=2, h=HPG),
                                       a_["cl"].rearrange("p (a h g) -> p a h g", a=2, h=HPG),
                                       gates[:, i, 0:NH].rearrange("p (a g h) -> p a h g", a=2, g=2), ALU.mult))

            def prompt_out(n):
                kind, i, r, gp, h, g2 = UNITS[n]
                O = otok[:, i % 2, :]
                if kind == "cmp":
                    dve.wait_ge(o_ready, n + 1)
                    dve.tensor_tensor(O.rearrange("p (u d) -> p u d", u=NH),
                                      psum[:, 6 * 512:8 * 512].rearrange("p (u d) -> p u d", u=NH),
                                      a_["cl"].rearrange("p (u o) -> p u o", o=1).broadcast_to([P, NH, HD]), ALU.mult)\
                        .then_inc(o_done, 1)
                    return
                c = n % 16
                dve.wait_ge(p_ready, n + 1)
                step(dve.reciprocal(ps_cf[:, c:c + 1], ps_l[:, c:c + 1]))
                gc = (1 + r) * NH + (2 * gp + g2) * HPG + h
                step(dve.tensor_tensor(ps_cf[:, c:c + 1], ps_cf[:, c:c + 1], gates[:, i, gc:gc + 1], ALU.mult))
                dve.wait_ge(o_ready, n + 1)
                dve.wait_ge(o_done, n)
                u = (gp * HPG + h) * 2 + g2
                dve.scalar_tensor_tensor(O[:, u * HD:(u + 1) * HD], bank(6 + n % 2, HD), ps_cf[:, c:c + 1],
                                         O[:, u * HD:(u + 1) * HD], ALU.mult, ALU.add).then_inc(o_done, 1)


            def regroup_keys(b, o, q, half):
                dve.wait_ge(cmp_full[half], b * 64 + (o * 64 + 16 * (q + 1)))
                dve.wait_ge(gre_free, b * 8 + (o * 8 + 4 + 2 * q + half + 1))
                dve.tensor_copy(gre[:, half, 0].rearrange("c g (p d) -> c g p d", p=4),
                                cmp_slots[half].rearrange("c (p v g d) -> c v g p d", p=4, v=2, g=KV)[:, 0]).then_inc(cmp_free, 1)

            prompt_soft(0)
            prompt_cmp_scale(0)
            prompt_soft(1)
            for n, (kind, i, r, gp, h, g2) in enumerate(UNITS):
                if n + 2 < NU:
                    prompt_soft(n + 2)
                prompt_out(n)
                if n in (AHEAD, AHEAD + 1):
                    regroup_keys(0, 0, 0, n - AHEAD)
                if n + 2 < NU and UNITS[n + 2][0] == "cmp":
                    prompt_cmp_scale(n + 2)
                if i > 0 and kind == "cmp" or n + 1 == NU:
                    i0 = i if n + 1 == NU else i - 1
                    t_round(16 + 2 * i0 + 1, qT[:, 4:8, i0 * P:(i0 + 1) * P], bank(1).rearrange("p (h t) -> p h t", h=HPG))

            dve.wait_ge(gr_in, 16 * 3)
            nsl = C("sslope")[:, 1:2]

            def compress(b, o):
                for q in range(4):
                    if q > 0:
                        for half in range(2):
                            regroup_keys(b, o, q, half)
                    if q == 1 and o == 1:
                        output_rows(b)
                    for kt in range(2):
                        for v in range(2):
                            xtc_round(b * SR + (o * SR + R0 + 4 * (2 * q + kt) + 2 * v + 1), kt, v, 1, P, bk=1 + 6 * v)
                    if q == 0 and o == 1:
                        merge(b)

            def first_keys(b, o):
                t_round(b * SR + (o * SR + R0 + 33), kTc[:, 0, 1, :], bank(1))

            def attend(b, last):
                ub = b * SU
                for g2 in range(2):
                    for gp in range(2):
                        g = 2 * gp + g2
                        dve.tensor_copy(qb[g2 * HD:(g2 + 1) * HD, gp, g * 32:(g + 1) * 32].rearrange("p (h t) -> p h t", h=HPG),
                                        qT[g2 * HD:(g2 + 1) * HD, gp * HPG:(gp + 1) * HPG, bass.ds(b * DT + TP, DT)])\
                            .then_inc(q_set, 1)
                step(dve.tensor_copy(gcur[:, 0:3].rearrange("p (o r) -> p o r", o=1), gr[:, bass.ds(b, 1), :]))

                def soft_unit(a):
                    dve.wait_ge(sc_ready, ub + (NU + a + 1))
                    S = sp3[:, a % 3, :]
                    src = bank(2 + a % 2)
                    mx = a_["mx"][:, COL[a]:COL[a] + 1]
                    dve.wait_ge(ptp_ready, ub + (NU + a - 2))
                    w, m = {CMPU: (NB, C("snegc")), SLCN: (DT, C("snegn")), WINC: (512, C("snegw")),
                            WINN: (DT, C("snegn"))}.get(a) or (512, smask[:, (CHUNK[a] - 1) // 4, :])
                    apart(dve)
                    step(dve.tensor_tensor_reduce(out=S[:, 0:w], in0=src[:, 0:w], in1=m[:, 0:w], scale=1.0,
                                                  scalar=-3e38, op0=ALU.add, op1=ALU.max, accum_out=mx))
                    dve.tensor_tensor(a_["nb"][:, a:a + 1], mx, nsl, ALU.mult).then_inc(soft, 1)

                def out_unit(a):
                    dve.wait_ge(o_ready, ub + (NU + a + 1))
                    for g in range(KV):
                        ins = dve.tensor_copy(oc[g * 32:(g + 1) * 32, COL[a], :],
                                              bank(6 + a % 2)[g * 32:(g + 1) * 32, g * HD:(g + 1) * HD])
                    ins.then_inc(o_done, 1)

                pp, ia, ib, m8 = a_["pp"], a_["ia"], a_["ib"], a_["m8"]

                def importance():
                    dve.wait_ge(imp_ready, b + 1)
                    dve.tensor_copy(pp[:, 1:1 + NB], bank(7, NB)).then_inc(imp_done, 1)
                    dve.wait_ge(imp_done, b + 1)
                    step(dve.tensor_reduce(ia, pp[:, 1:1 + 4 * NSB].rearrange("p (j r) -> p j r", r=4), AX.X, ALU.add))
                    step(dve.tensor_reduce(ib, pp[:, 0:4 * NSB].rearrange("p (j r) -> p j r", r=4), AX.X, ALU.add))
                    step(dve.tensor_tensor(ia, ia, ib, ALU.add))
                    step(dve.memset(ia[:, 0:1], -NEG))
                    step(dve.memset(ia[:, NSB - 2:NSB], -NEG))

                def top_k():
                    apart(dve)
                    step(dve.max(m8[:, 0:8], ia))
                    apart(dve)
                    step(dve.match_replace(ib, m8[:, 0:8], ia, NEG))
                    apart(dve)
                    step(dve.max(m8[:, 8:16], ib))
                    apart(dve)
                    step(dve.match_replace(ia, m8[:, 8:16], ib, NEG))
                    step(dve.tensor_scalar(a_["madd"], ia, NEG, NEG, ALU.not_equal, ALU.mult))
                    for half in range(2):
                        m = a_["madd"][:, half * 32:half * 32 + 32].rearrange("p (o n u) -> p o n u", o=1, u=1)\
                            .broadcast_to([P, 4, 32, 4])
                        mh = a_["madd"][:, half * 32:half * 32 + 32]
                        step(dve.tensor_scalar(mh, mh, C("srow")[:, half:half + 1], None, ALU.add))
                        step(dve.tensor_tensor(smask[:, half, :].rearrange("p (i n u) -> p i n u", i=4, u=4),
                                               C("spos").rearrange("p (i n u) -> p i n u", i=4, u=4), m, ALU.add))

                dve.wait_ge(cv_ready, b * 2 + 3)
                dve.tensor_copy(kc, bank(6, 2 * NB).rearrange("p (g n) -> p g n", g=2)).then_inc(cv_sb, 1)
                dve.wait_ge(cv_ready, b * 2 + 4)
                dve.tensor_copy(vc[:, 0, :], bank(7)[:, 0:256])
                dve.tensor_copy(vc[0:NB - P, 1, :], bank(7)[0:NB - P, 256:512]).then_inc(cv_sb, 1)
                soft_unit(0)
                soft_unit(1)
                dve.wait_ge(p_ready, ub + (NU + CMPU + 1))
                step(dve.reciprocal(a_["tmp"][:, 0:1], a_["ls"][:, 0:1]))
                S = sp3[:, CMPU % 3, 0:NB]
                dve.tensor_scalar(S, S, a_["tmp"][:, 0:1], None, ALU.mult).then_inc(p_norm, 1)
                for a in range(SU):
                    if a + 2 < SU and a != 2:
                        soft_unit(a + 2)
                    out_unit(a)
                    if a + 3 in CHUNK:
                        c = CHUNK[a + 3]
                        t_round(b * SR + (R0 + 32 + 2 * c + 1), kTc[:, c % 2, 1, :], bank(1))
                    if a == 2:
                        soft_unit(a + 2)
                    if a == 0:
                        importance()
                    if a == 1:
                        top_k()
                    if a in (8, 9) and not last:
                        regroup_keys(b, 1, 0, a - 8)

            seg, coef, tmp = b_["seg"], a_["coef"], a_["tmp"]

            def merge(b):
                dve.wait_ge(o_done, b * SU + (NU + SU))
                step(dve.tensor_tensor(a_["mx"][:, 4:12], a_["mx"][:, 4:12], C("spiece"), ALU.add))
                for j, (a0, a1) in enumerate(SEGS):
                    step(dve.tensor_reduce(seg[:, j:j + 1], a_["mx"][:, a0:a1], AX.X, ALU.max))
                dve.tensor_tensor(seg[:, 2:4], seg[:, 0:2], nsl.broadcast_to([P, 2]), ALU.mult).then_inc(w_ready, 1)
                dve.wait_ge(w_exp, b + 1)
                step(dve.tensor_tensor(tmp[:, 1:12], a_["wts"][:, 1:12], a_["ls"][:, 1:12], ALU.mult))
                for j, (a0, a1) in enumerate(SEGS):
                    step(dve.tensor_reduce(seg[:, 4 + j:5 + j], tmp[:, a0:a1], AX.X, ALU.add))
                step(dve.reciprocal(seg[:, 6:8], seg[:, 4:6]))
                step(dve.tensor_tensor(seg[:, 6:8], seg[:, 6:8], gcur[:, 1:3], ALU.mult))
                step(dve.tensor_copy(coef[:, 0:1], gcur[:, 0:1]))
                for j, (a0, a1) in enumerate(SEGS):
                    step(dve.tensor_scalar(coef[:, a0:a1], a_["wts"][:, a0:a1], seg[:, 6 + j:7 + j], None, ALU.mult))
                step(dve.tensor_tensor(ocs, oc, coef.rearrange("p (a o) -> p a o", o=1).broadcast_to([P, SU, HD]), ALU.mult))
                step(dve.tensor_reduce(a_["od"][:, 0:HD], ocs.rearrange("p a d -> p d a"), AX.X, ALU.add))
                dve.tensor_copy(a_["od"][:, HD:P], a_["od"][:, 0:HD]).then_inc(od_ready, 1)

            def output_rows(b):
                dve.wait_ge(ot_ready, b + 1)
                apart(dve)
                for g2 in range(2):
                    src = bank(6)[g2 * HD:(g2 + 1) * HD, 0:P].rearrange("p (a g h t) -> p a g h t", a=2, g=2, h=HPG)[:, :, g2]
                    ins = dve.tensor_copy(qT[g2 * HD:(g2 + 1) * HD, :, bass.ds(b * DT + TP, DT)]
                                          .rearrange("p (a h) t -> p a h t", a=2), src)
                ins.then_inc(ot_done, 1)

            compress(0, 0)
            first_keys(0, 0)
            with dve.Fori(0, DB - 1) as b:
                step.off = b * STEPS
                n_before = step.n
                attend(b, False)
                compress(b, 1)
                first_keys(b, 1)
                assert step.n - n_before == STEPS, step.n - n_before
            step.n += (DB - 2) * STEPS
            step.off = 0
            attend(DB - 1, True)
            merge(DB - 1)
            output_rows(DB - 1)
            last_sums(4, ALPHA, y_ready, DK)
            norm(4, EPS)
            ffn(3)
            norm(5, 4 * EPS)
            for i, (t0, n) in enumerate(TILES):
                dve.wait_ge(yt_psum, i + 1)
                if i >= 2:
                    dve.wait_ge(y_out[i % 2], 16 * (i // 2))
                dve.tensor_copy(ytok[0:n, i % 2, :], psum[0:n, (i % 4) * 1024:(i % 4 + 1) * 1024]).then_inc(y_tok, 1)

        @block.tensor
        def _(pe):
            def wide(out, lhsT, rhs, start, stop):
                m = lhsT.shape[-1]
                pe.matmul(out[0:m, 0:TP], lhsT, rhs[:, 0:TP], start=start, stop=stop)
                return pe.matmul(out[0:m, TP:T], lhsT, rhs[:, TP:T], start=start, stop=stop)

            def split(out, lhsT, rhs, start, stop):
                for c in range(2):
                    last = pe.matmul(out[:, c], lhsT, rhs[:, c * TH:(c + 1) * TH], start=start, stop=stop)
                return last

            def split3(out, hi, lo, rhs_hi, rhs_lo, start, stop):
                split(out, hi, rhs_hi, start, False)
                split(out, hi, rhs_lo, False, False)
                return split(out, lo, rhs_hi, False, stop)

            def norm_sums(ln):
                pe.wait_ge(consts_in, 16)
                pe.wait_ge(sums_ready, 2 * ln + 1)
                split(halves(0), C("mean"), stat[:, 0, :], True, True).then_inc(stats_done, 1)
                pe.wait_ge(sums_ready, 2 * ln + 2)
                split(halves(1), C("mean"), stat[:, 1, :], True, True).then_inc(stats_done, 1)

            def ffn(f, ln):
                for h in range(2):
                    F0 = SP_BASE[f] + h * FB
                    u0 = h * FB
                    c0 = f * FT + h * FH
                    y0 = Y_BASE[ln] + 2 + h * DK

                    def gate_up(j, u, first=False):
                        pe.wait_ge(lo_ready, j + (F0 + 1))
                        if not isinstance(j, int) or j >= 2 or h + f > 0:
                            pe.wait_ge(gu_free, j + (c0 + 1))
                        if h == 1 and u > 0:
                            pe.wait_ge(y_sum, y0)
                        hi, lo = [w_sp[:, (u0 + u) % 2, d, :].rearrange("p (k c n) -> p k c n", k=DK, c=2)
                                  for d in range(2)]
                        s = u % 2
                        for k, c in [(k, c) for k in range(DK) for c in range(2)] if first else \
                                [(k, c) for c in range(2) for k in range(DK)]:
                            if first and c == 0:
                                pe.wait_ge(x_ready if ln > 0 else xt_first, DK * max(ln - 1, 0) + k + 1)
                            last = split3(halves(2 * s + c), hi[:, k, c, :], lo[:, k, c, :], x_hi[:, k, :], x_lo[:, k, :],
                                          k == 0, k == DK - 1)
                        last.then_inc(blk_done, 1)

                    def gate_up_half():
                        j = FH - 1
                        pe.wait_ge(lo_ready, F0 + j + 1)
                        pe.wait_ge(gu_free, c0 + j + 1)
                        hi, lo = [w_sp[:, (u0 + j) % 2, d, 0:2 * DK * FL].rearrange("p (k n) -> p k n", k=DK)
                                  for d in range(2)]
                        for k in range(DK):
                            last = split3(halves(2 * (j % 2)), hi[:, k, :], lo[:, k, :], x_hi[:, k, :], x_lo[:, k, :],
                                          k == 0, k == DK - 1)
                        last.then_inc(blk_done, 1)

                    def down(m, u):
                        pe.wait_ge(lo_ready, m + (F0 + FH + 1))
                        pe.wait_ge(gu_free, c0 + FH + 1)
                        pe.wait_ge(y_sum, m + (y0 - 1))
                        hi, lo = [w_sp[:, (u0 + FH + u) % 2, d, 0:FW].rearrange("p (k n) -> p k n", n=P) for d in range(2)]
                        for k in range(FH):
                            n = P if h == 0 or k < FH - 1 else FL
                            if k == FH - 1:
                                pe.wait_ge(h_ready, c0 + FH + 1)
                            last = split3(halves(2 + u % 2), hi[0:n, k, :], lo[0:n, k, :], h_hi[0:n, k, :], h_lo[0:n, k, :],
                                          k == 0, k == FH - 1)
                        last.then_inc(blk_done, 1)

                    gate_up(0, 0, first=h == 0)
                    with pe.Fori(0, 2) as i:
                        for u in range(1, 1 + RING):
                            gate_up(i * RING + u, u)
                    for j in range(1 + 2 * RING, FH):
                        if h == 1 and j == FH - 1:
                            gate_up_half()
                        else:
                            gate_up(j, j)
                    pe.wait_ge(h_ready, c0 + FH)
                    with pe.Fori(0, DK // 2) as i:
                        for u in range(2):
                            down(i * 2 + u, u)
                norm_sums(ln)

            def out_projection(ln, n0, src):
                for i in range(4):
                    n = n0 + i
                    v = ring[:, n % RING, :].rearrange("p (k n) -> p k n", k=DK)
                    pe.wait_ge(ring_full[n % RING], full_at(n))
                    for c in range(2):
                        m = 2 * i + c
                        pe.wait_ge(y_sum, Y_BASE[ln] + m + 1)
                        for k in range(DK):
                            last = split(halves(2 + c), v[:, k, c * P:(c + 1) * P], src[:, k, :], k == 0, k == DK - 1)
                        last.then_inc(y_ready, 1)
                    pe.wait_ge(y_ready, MIX.index(ln) * DK + m + 1)
                    pe.sem_inc(blk_done, 1)
                norm_sums(ln)

            pe.wait_ge(ident_in, 16)
            pe.wait_ge(x_in, 16 * len(TILES))
            for k in range(DK):
                if k >= 4:
                    pe.wait_ge(xt_sb, k - 3)
                for i, (t0, n) in enumerate(TILES):
                    last = pe.transpose(psum[:, (k % 4) * 1024 + t0:(k % 4) * 1024 + t0 + n],
                                        xl[0:n, i, k * P:(k + 1) * P], ident[0:n, 0:n])
                last.then_inc(xt_psum, 1)
            pe.wait_ge(xt_sb, DK)

            ffn(0, 0)

            n0 = blk_pos["even"]
            for i in range(4):
                s = (n0 + i) % RING
                v = ring[:, s, :].rearrange("p (k n) -> p k n", k=DK)
                pe.wait_ge(ring_full[s], full_at(n0 + i))
                for c in range(2):
                    z = 2 * i + c
                    if z >= 4:
                        pe.wait_ge(z_freeD, z - 3)
                    for k in range(DK):
                        if z == 0:
                            pe.wait_ge(x_ready, k + 1)
                        if z < 4:
                            last = wide(pair(z % 4), v[:, k, c * P:(c + 1) * P], yT[:, k, :], k == 0, k == DK - 1)
                        else:
                            last = split(halves(z % 4), v[:, k, c * P:(c + 1) * P], yT[:, k, :], k == 0, k == DK - 1)
                    last.then_inc(z_ready, 1)
                pe.wait_ge(z_ready, z + 1)
                pe.sem_inc(blk_done, 1)
            pe.wait_ge(loc_in, 7 * 16)
            pe.wait_ge(z_freeA, 1)
            for h in range(NG):
                last = pe.transpose(bank(0)[:, h * P:(h + 1) * P], gms[:, h, :], ident)
            last.then_inc(z_ready, 1)
            pe.wait_ge(z_freeA, 2)
            for g in range(NG):
                last = pe.transpose(bank(2)[:, g * DB * PAST:(g + 1) * DB * PAST], past[0:DB * PAST, g * P:(g + 1) * P],
                                    ident[0:DB * PAST, 0:DB * PAST])
            last.then_inc(z_ready, 1)
            pe.wait_ge(z_freeA, 3)
            pe.wait_ge(z_freeD, 5)
            for h in range(NG):
                last = pe.matmul(bank(4)[0:TS, h * TS:(h + 1) * TS], C("rep")[0:DT, :],
                                 wsT[0:DT, h:h + 1, 0:DT].broadcast_to([DT, DB, DT]), start=True, stop=True)
            last.then_inc(z_ready, 1)
            pe.wait_ge(z_freeA, 4)
            for g in range(NG):
                pe.transpose(bank(6)[0:PAST, g * P:(g + 1) * P], ext[:, g, TP:TP + PAST], ident)
                last = pe.transpose(bank(7)[0:TS, g * P:(g + 1) * P], pnew[:, g, :], ident)
            last.then_inc(z_ready, 1)
            for c in range(2):
                pe.wait_ge(ring_full[(n0 + 4 + c) % RING], full_at(n0 + 4 + c))
            for i, (t0, n) in enumerate(TILES):
                pe.wait_ge(z_freeD, 5 + i)
                for c in range(2):
                    v = ring[:, (n0 + 4 + c) % RING, :].rearrange("p (k n) -> p k n", k=DK)
                    for k in range(DK):
                        last = pe.matmul(bank(2 * (i % 4))[0:n, c * 256:(c + 1) * 256], yT[:, k, t0:t0 + n],
                                         v[:, k, :], start=k == 0, stop=k == DK - 1)
                last.then_inc(z_ready, 1)
            pe.wait_ge(z_ready, 17)
            pe.sem_inc(blk_done, 2)
            for h in range(NG):
                s = (h + 1) % 4
                pe.wait_ge(z_freeD, 13)
                for c in range(TT):
                    pe.matmul(psum[:, s * 1024 + c * P:s * 1024 + (c + 1) * P], vtok[:, c, h * P:(h + 1) * P],
                              wsT[:, h, :], start=True, stop=True)
                pe.matmul(psum[:, s * 1024 + TP:s * 1024 + T], vtok[0:TS, TT, h * P:(h + 1) * P],
                          wsB[0:TS, h, :], start=True, stop=True).then_inc(z_ready, 1)
            for g in range(NG):
                pe.wait_ge(z_freeD, 14 + g)
                pe.wait_ge(e_dif, g + 1)
                split(halves((g + 1) % 4), plw[:, g, :], dif[:, g, :], True, True).then_inc(z_ready, 1)
            pe.wait_ge(z_freeD, 17)
            pe.wait_ge(z_freeA, 8)
            out_projection(1, n0 + 6, cat)

            ffn(1, 2)
            ffn(2, 3)

            n0 = blk_pos["odd"]
            for i in range(4):
                hi, lo = [w_sp[:, i % 2, d, :].rearrange("p (k h n) -> p k h n", k=DK, h=2) for d in range(2)]
                pe.wait_ge(lo_ready, 6 * FB + i + 1)
                for h in range(2):
                    z = 2 * i + h
                    if z >= 4:
                        pe.wait_ge(q_free, z - 3)
                    for k in range(DK):
                        if z == 0:
                            pe.wait_ge(x_ready, 3 * DK + k + 1)
                        last = split3(halves(z % 4), hi[:, k, h, :], lo[:, k, h, :], x_hi[:, k, :], x_lo[:, k, :],
                                      k == 0, k == DK - 1)
                    last.then_inc(q_ready, 1)
                pe.wait_ge(q_ready, z + 1)
                pe.sem_inc(blk_done, 1)
            pe.wait_ge(q_free, 8)
            for c in range(6):
                hi, lo = [w_sp[:, c % 2, d, :].rearrange("p (k n) -> p k n", k=DK) for d in range(2)]
                pe.wait_ge(lo_ready, 6 * FB + 4 + c + 1)
                o0 = (c % 2) * 3
                if c >= 2:
                    pe.wait_ge(kv_sb, c - 1)
                for i in range(TT + 1):
                    t0 = min(i * P, T - P)
                    for k in range(DK):
                        for j, (xs, ws) in enumerate(((x_hi, hi), (x_hi, lo), (x_lo, hi))):
                            last = pe.matmul(psum[:, o0 * 512 + i * 256:o0 * 512 + (i + 1) * 256], xs[:, k, t0:t0 + P],
                                             ws[:, k, :], start=k == 0 and j == 0, stop=k == DK - 1 and j == 2)
                last.then_inc(kv_ready, 1)
                if c in (2, 4):
                    for gp in range(2):
                        z = 8 + (c - 2) + gp
                        pe.wait_ge(q_free, z)
                        for k in range(DK):
                            last = split3(halves(3), hi[:, k, gp * P:(gp + 1) * P], lo[:, k, gp * P:(gp + 1) * P],
                                          x_hi[:, k, :], x_lo[:, k, :], k == 0, k == DK - 1)
                        last.then_inc(q_ready, 1)
                    pe.wait_ge(q_ready, z + 1)
                pe.wait_ge(kv_ready, c + 1)
                pe.sem_inc(blk_done, 1)
            n = n0 + 10
            v = ring[:, n % RING, 0:DK * 48].rearrange("p (k n) -> p k n", k=DK)
            pe.wait_ge(ring_full[n % RING], full_at(n))
            pe.wait_ge(kv_sb, 5)
            for i, (t0, m) in enumerate(TILES):
                for k in range(DK):
                    last = pe.matmul(bank(0)[0:m, i * 48:(i + 1) * 48], yT[:, k, t0:t0 + m], v[:, k, :],
                                     start=k == 0, stop=k == DK - 1)
            last.then_inc(q_ready, 1)
            pe.wait_ge(q_ready, 13)
            pe.sem_inc(blk_done, 1)
            pe.sem_inc(cmp_free, 2)
            pe.sem_inc(slc_free, 4)
            pe.sem_inc(gre_free, 2)

            pe.wait_ge(n_in, 9 * 16)
            pe.wait_ge(q_free, 12)
            for k in range(2):
                for j in range(16):
                    last = pe.matmul(bank(7)[:, k:k + 1], w1c[:, k, j // 8, j % 8, :], a_["peT"][:, k * 16 + j:k * 16 + j + 1],
                                     start=j == 0, stop=j == 15)
            last.then_inc(hb_ready, 1)

            def t_round(n, even, tiles, free=0):
                pe.wait_ge(t_act if even else t_dve, n - free)
                for out, src in tiles:
                    last = pe.transpose(out, src, ident[0:src.shape[0], 0:src.shape[0]])
                return last.then_inc(t_ready, 1)

            def xtc_round(n, even, slot, v, kt, rows, bk=None, free=0):
                bk = bank((0 if even else 1) if bk is None else bk)
                t_round(n, even, [(bk[:, g * rows:(g + 1) * rows], gre[0:rows, slot, v, g, kt * P:(kt + 1) * P])
                                  for g in range(KV)], free)

            pe.wait_ge(q_free, 13)
            pe.wait_ge(kv_sb, 6)
            for st in range(9):
                q, kt = st // 2, st % 2
                if st < 8:
                    pe.wait_ge(cmp_free, q + 3)
                    for v in range(2):
                        xtc_round(st, v == 0, q % 2, v, kt, TP // CS)
                    if kt == 1:
                        pe.wait_ge(t_ready, 2 * st + 2)
                        pe.sem_inc(gre_free, 1)
                if st > 0:
                    pe.wait_ge(t_act, st)
                    pe.wait_ge(t_dve, st)
                    for v in range(2):
                        for r in range(2):
                            last = pe.matmul(bank(2 + v, KV * NBP), w1c[:, v, r, st - 1, :],
                                             xTc[:, (st - 1) % 2, v, :, r:r + NBP], start=st == 1 and r == 0,
                                             stop=st == 8 and r == 1)
                    last.then_inc(hid_step, 1)
            pe.wait_ge(gel_ready, 2)
            pe.wait_ge(hb_sb, 1)
            pe.wait_ge(zeroed, 6)
            for gp in range(2):
                for g2 in range(2):
                    last = pe.matmul(bank(6)[:, gp * NBP:(gp + 1) * NBP], w2k[:, g2, :], gel[:, 0, 2 * gp + g2, 0:NBP],
                                     start=g2 == 0, stop=g2 == 1)
            last.then_inc(cv_ready, 1)
            for g in range(KV):
                last = pe.matmul(bank(7)[0:NBP, g * HD:(g + 1) * HD], gel[:, 1, g, 0:NBP], w2v, start=True, stop=True)
            last.then_inc(cv_ready, 1)

            pe.wait_ge(cv_sb, 2)

            def prompt_scores(n):
                kind, i, r, gp, h, g2 = UNITS[n]
                if n >= 2:
                    pe.wait_ge(soft, n - 1)
                if kind == "cmp":
                    for a in range(2):
                        for hh in range(HPG):
                            last = pe.matmul(bank(2 + n % 2)[:, (a * HPG + hh) * 64:(a * HPG + hh + 1) * 64],
                                             qT[:, a * HPG + hh, i * P:(i + 1) * P], kcb[:, a, :], start=True, stop=True)
                else:
                    rows = slice(g2 * HD, (g2 + 1) * HD)
                    last = pe.matmul(bank(2 + n % 2, (i + 1) * P), qT[rows, gp * HPG + h, i * P:(i + 1) * P],
                                     kT[rows, r, gp, 0:(i + 1) * P], start=True, stop=True)
                last.then_inc(sc_ready, 1)

            def prompt_transposes(n):
                cmp = UNITS[n][0] == "cmp"
                pe.wait_ge(p_ready, n + 1)
                if n >= 2:
                    pe.wait_ge(pt_sb, n - 1)
                for j in range(4 if cmp else UNITS[n][1] + 1):
                    last = pe.transpose(bank(4 + n % 2)[:, j * P:(j + 1) * P], sp3[:, n % 3, j * P:(j + 1) * P], ident)
                last.then_inc(ptp_ready, 1)

            prompt_scores(0)
            prompt_scores(1)
            prompt_transposes(0)
            for n, (kind, i, r, gp, h, g2) in enumerate(UNITS):
                if n + 2 < NU:
                    prompt_scores(n + 2)
                if n + 1 < NU:
                    prompt_transposes(n + 1)
                pe.wait_ge(pt_sb, n + 1)
                if n >= 1:
                    pe.wait_ge(o_done, n if kind == "cmp" or UNITS[n - 1][0] == "cmp" else n - 1)
                nk = 4 if kind == "cmp" else i + 1
                for j in range(nk):
                    pt = pts[:, n % 2, j * P:(j + 1) * P]
                    if kind == "cmp":
                        last = pe.matmul(bank(6 + j // 2)[:, (j % 2) * 256:(j % 2 + 1) * 256], pt, vcb[:, j // 2, :],
                                         start=True, stop=True)
                    else:
                        g = 2 * gp + g2
                        last = pe.matmul(bank(6 + n % 2, HD), pt, vtk[:, r, j, g * HD:(g + 1) * HD],
                                         start=j == 0, stop=j == nk - 1)
                last.then_inc(o_ready, 1)
                if i > 0 and kind == "cmp" or n + 1 == NU:
                    i0 = i if n + 1 == NU else i - 1
                    pe.wait_ge(o_done, n + 1 if n + 1 == NU else n)
                    for a in range(2):
                        t_round(8 + i0, a == 0, [(bank(a)[:, hh * P:(hh + 1) * P],
                                                  otok[:, i0 % 2, (a * HPG + hh) * P:(a * HPG + hh + 1) * P])
                                                 for hh in range(HPG)])

            def compress(b, o):
                hb_ = R0 // 2 + o * (SR // 2)
                for q in range(4):
                    pe.wait_ge(cmp_free, b * 8 + (o * 8 + 4 + 2 * q + 2 + 2))
                    pe.wait_ge(cmp_freeA, b * 8 + (o * 8 + 2 * q + 2 + 2))
                    for kt in range(2):
                        for v in range(2):
                            if kt == 0 and v == 1 and q < 2:
                                if q == 0:
                                    pe.wait_ge(o_done, b * SU + (o * SU + NU))
                                else:
                                    pe.wait_ge(ot_done, b + (o + 1))
                            for half in range(2):
                                xtc_round(b * (SR // 2) + (hb_ + 2 * (2 * q + kt) + v), half == 0, half, v, kt, P,
                                          bk=half + 6 * v, free=0 if q + kt + v == 0 else 1)
                    pe.wait_ge(t_ready, b * SR + (o * SR + R0 + 8 * q + 8))
                    pe.sem_inc(gre_free, 2)
                    if q == 0:
                        pe.wait_ge(pt_sb, b * SU + (o * SU + NU))
                        pe.wait_ge(soft, b * SU + (o * SU + NU))
                    for st in (2 * q, 2 * q + 1):
                        pe.wait_ge(t_act, b * (SR // 2) + (hb_ + 2 * st + 2))
                        pe.wait_ge(t_dve, b * (SR // 2) + (hb_ + 2 * st + 2))
                        for v in range(2):
                            for gp in range(2):
                                for r in range(2):
                                    last = pe.matmul(bank(2 + 2 * v + gp, 2 * NB), w1c[:, v, r, st, :],
                                                     xTc[:, st % 2, v, 2 * gp:2 * gp + 2, r:r + NB],
                                                     start=st == 0 and r == 0, stop=st == 7 and r == 1)
                        last.then_inc(hid_step, 1)
                    if q == 0 and o == 1:
                        output_transpose(b)
                keys(b, o, WINC)
                pe.wait_ge(gel_ready, b * 4 + (o * 4 + 4))
                pe.wait_ge(o_done, b * SU + (o * SU + NU))
                pe.wait_ge(ot_done, b + (o + 1))
                for gp in range(2):
                    for g2 in range(2):
                        last = pe.matmul(bank(6)[:, gp * NB:(gp + 1) * NB], w2k[:, g2, :], gel[:, 0, 2 * gp + g2, 0:NB],
                                         start=g2 == 0, stop=g2 == 1)
                last.then_inc(cv_ready, 1)
                pe.wait_ge(gel_ready, b * 4 + (o * 4 + 6))
                for i, m in enumerate((P, NB - P)):
                    for g in range(KV):
                        last = pe.matmul(bank(7)[0:m, i * 256 + g * HD:i * 256 + (g + 1) * HD],
                                         gel[:, 1, g, i * P:i * P + m], w2v, start=True, stop=True)
                last.then_inc(cv_ready, 1)

            def output_transpose(b):
                pe.wait_ge(od_ready, b + 1)
                pe.wait_ge(o_done, b * SU + (NU + SU))
                pe.transpose(bank(6, P), a_["od"], ident).then_inc(ot_ready, 1)

            def keys(b, o, a):
                c = CHUNK[a]
                if a == WINC:
                    pe.wait_ge(win_full, b * 16 + (o * 16 + 16))
                else:
                    pe.wait_ge(slc_full[c % 4], b * 32 + 16 * ((c - 1) // 4 + 1))
                for gp in range(2):
                    t_round(b * (SR // 2) + (R0 // 2 + o * (SR // 2) + 16 + c), gp == 0,
                            [(bank(gp)[:, p * P:(p + 1) * P],
                              slc_slots[c % 4][:, p * ROW + gp * P:p * ROW + (gp + 1) * P]) for p in range(4)])

            def attend(b):
                ub = b * SU
                hb_ = b * (SR // 2)

                def scores(a):
                    if a > 1:
                        pe.wait_ge(soft, ub + (NU + a - 1))
                    for gp in range(2):
                        if a == CMPU:
                            w, rhs = NB, kc[:, gp, :]
                            pe.wait_ge(cv_sb, b * 2 + 3)
                        elif a in CHUNK:
                            c = CHUNK[a]
                            w, rhs = 512, kTc[:, c % 2, gp, :]
                            pe.wait_ge(t_act, hb_ + (R0 // 2 + 16 + c + 1))
                            if gp == 1:
                                pe.wait_ge(t_dve, hb_ + (R0 // 2 + 16 + c + 1))
                        else:
                            w, rhs = DT, kT[:, 0 if a == SLCN else 1, gp, bass.ds(b * DT + TP, DT)]
                        last = pe.matmul(bank(2 + a % 2)[:, 0:w], qb[:, gp, :], rhs, start=gp == 0, stop=gp == 1)
                    last.then_inc(sc_ready, 1)

                def parts(a):
                    if a == CMPU:
                        return [(P, 0, P), (NB - P, P, NB - P)]
                    if a in CHUNK:
                        return [(P, p * P, P) for p in range(4)]
                    return [(DT, 0, DT)]

                def transposes(a):
                    pe.wait_ge(p_norm if a == CMPU else p_ready, b + 1 if a == CMPU else ub + (NU + a + 1))
                    pe.wait_ge(pt_sb, ub + (NU + a - 1))
                    for j, (m, c0, w) in enumerate(parts(a)):
                        last = pe.transpose(bank(4 + a % 2)[0:m, j * P:(j + 1) * P], sp3[:, a % 3, c0:c0 + w], ident)
                    last.then_inc(ptp_ready, 1)

                def output(a):
                    pe.wait_ge(pt_sb, ub + (NU + a + 1))
                    pe.wait_ge(o_done, ub + (NU + a - 1))
                    if a == 1:
                        pe.wait_ge(imp_done, b + 1)
                    if a == WINN:
                        pe.wait_ge(vn_full, b * 32 + 32)
                    for j, (m, c0, w) in enumerate(parts(a)):
                        if a == CMPU:
                            rhs = vc[0:m, j, :]
                        elif a in CHUNK:
                            rhs = slc_slots[CHUNK[a] % 4][:, j * ROW + 256:j * ROW + 512]
                        else:
                            rhs = vnew[0:DT, 0 if a == SLCN else 1, :]
                        last = pe.matmul(bank(6 + a % 2, 256), pts[0:m, a % 2, j * P:(j + 1) * P], rhs,
                                         start=j == 0, stop=j == len(parts(a)) - 1)
                    last.then_inc(o_ready, 1)
                    if a in CHUNK:
                        pe.wait_ge(o_ready, ub + (NU + a + 1))
                        pe.sem_inc(slc_free, 1)

                pe.wait_ge(q_set, b * 4 + 4)
                scores(0)
                scores(1)
                transposes(0)
                pe.wait_ge(cv_sb, b * 2 + 4)
                for a in range(SU):
                    if a + 2 < SU:
                        scores(a + 2)
                    output(a)
                    if a + 3 in CHUNK:
                        keys(b, 0, a + 3)
                    if a + 1 < SU:
                        transposes(a + 1)
                    if a == 0:
                        pe.matmul(bank(7, NB), C("hsum"), sp3[:, CMPU % 3, 0:NB], start=True, stop=True)\
                            .then_inc(imp_ready, 1)

            compress(0, 0)
            with pe.Fori(0, DB - 1) as b:
                attend(b)
                compress(b, 1)
            attend(DB - 1)
            output_transpose(DB - 1)

            pe.wait_ge(ot_done, DB + 1)
            pe.wait_ge(o_done, NU + DB * SU)
            out_projection(4, n0 + 11, qT)
            ffn(3, 5)
            pe.wait_ge(x_ready, 6 * DK)
            for i, (t0, n) in enumerate(TILES):
                if i >= 4:
                    pe.wait_ge(y_tok, i - 3)
                for k in range(DK):
                    last = pe.transpose(psum[0:n, (i % 4) * 1024 + k * P:(i % 4) * 1024 + (k + 1) * P],
                                        yT[:, k, t0:t0 + n], ident)
                last.then_inc(yt_psum, 1)


_INS = ["x_prompt", "x_sample", "state_l0_pool", "cache_l1_cmp_kv", "cache_l1_slc_kv", "cache_l1_win_kv", "page_table",
        "w_ffn_in", "w_ffn_out", "ln_g", "ln_b", "w_in_even", "pool_w", "pool_scale", "gm_ln_g", "gm_ln_b", "gm_ws",
        "gm_b", "w_out_even", "w_in_odd", "cmp_pe", "cmp_w1", "cmp_b1", "cmp_w2", "w_out_odd"]
_OUTS = [(1, TP, DM), (DB, DT, DM), (1, PAST, PW), (DB, PAST, PW), (DB, DT, PW),
         (1, TP, 2, KV, HD), (1, TP, 2, KV, HD), (1, WIN, 2, KV, HD),
         (DB, DT, 2, KV, HD), (DB, DT, 2, KV, HD), (DB, WIN, 2, KV, HD)]


def kernel(**inputs):
    import concourse.bacc as _bacc
    from concourse.bass_utils import run_bass_kernel_spmd as _run

    nc = _bacc.Bacc("TRN2", target_bir_lowering=False, num_devices=1)
    arrays, args = {}, []
    for name in _INS:
        a = np.ascontiguousarray(inputs[name])
        arrays[f"in_{name}"] = a
        args.append(nc.dram_tensor(f"in_{name}", a.shape, mybir.dt.from_np(a.dtype), kind="ExternalInput").ap())
    where, table = constants()
    arrays["shape_tables"] = table
    tables = nc.dram_tensor("shape_tables", table.shape, F32, kind="ExternalInput").ap()
    outs = [nc.dram_tensor(f"out_{i}", shape, F32, kind="ExternalOutput").ap() for i, shape in enumerate(_OUTS)]
    bass_hybrid_trunk_step(nc, args, where, tables, outs)
    r = _run(nc, [arrays], core_ids=[0])
    return tuple(r.results[0][f"out_{i}"] for i in range(len(_OUTS)))
```
